# Optimizing a Trainium2 kernel written in Bass

```python
import jax, jax.numpy as jnp
from jax import lax
import numpy as np

D_MODEL = 1024
BATCH = 1
SEQ = 256
DEPTH = 1

N_MIXERS = 3
N_LAYERS_A = len(range(0, DEPTH, N_MIXERS))
N_LAYERS_B = len(range(1, DEPTH, N_MIXERS))
N_LAYERS_C = len(range(2, DEPTH, N_MIXERS))
RMS_EPS = 1e-6
N_MOD = 6
FFN_HIDDEN = -(-8 * D_MODEL // (3 * 256)) * 256

NSA_HEAD_DIM = 64
NSA_HEADS = D_MODEL // NSA_HEAD_DIM
NSA_KV_GROUPS = 4
NSA_HEADS_PER_GROUP = NSA_HEADS // NSA_KV_GROUPS
CMP_LEN = 32
CMP_STRIDE = 16
CMP_HIDDEN = 2 * NSA_HEAD_DIM
SEL_LEN = 64
SEL_TOPK = 16
WINDOW = 512
NSA_Q_BLOCK = SEL_LEN
NSA_SCALE = NSA_HEAD_DIM ** -0.5
SEL_BIG = 1e9
NSA_IN = NSA_HEADS * NSA_HEAD_DIM + 6 * NSA_KV_GROUPS * NSA_HEAD_DIM + 3 * NSA_HEADS

RWKV_HEAD_DIM = 64
RWKV_HEADS = D_MODEL // RWKV_HEAD_DIM
DECAY_LORA = 64
AAA_LORA = 64
GATE_LORA = 128
RWKV_GN_EPS = 64e-5

POOL_WINDOWS = (2, 4, 8, 16)
POOL_GROUPS = len(POOL_WINDOWS)
POOL_GROUP_DIM = D_MODEL // POOL_GROUPS

kernel_name = "hybrid_nsa_rwkv7_pool_adaln_trunk"

def rms_norm(x, w):
    xf = x.astype(jnp.float32)
    y = xf * lax.rsqrt(jnp.mean(xf * xf, axis=-1, keepdims=True) + RMS_EPS)
    return y.astype(x.dtype) * w

def modulate(h, shift, scale):
    return h * (1 + scale[:, None, :]) + shift[:, None, :]

def masked_softmax(s, mask):
    s = jnp.where(mask, s.astype(jnp.float32), -jnp.inf)
    m = jnp.max(s, axis=-1, keepdims=True)
    m = jnp.where(jnp.isfinite(m), m, 0.0)
    e = jnp.where(mask, jnp.exp(s - m), 0.0)
    return e / jnp.maximum(jnp.sum(e, axis=-1, keepdims=True), 1e-30)

def swiglu(h, w_gate, w_up, w_down):
    return (jax.nn.silu(h @ w_gate) * (h @ w_up)) @ w_down

def nsa_mixer(h, w_in, cmp_pos, cmp_w1, cmp_w2, qk_norm, w_out):
    B, S, _ = h.shape
    H, G, HG, DK = NSA_HEADS, NSA_KV_GROUPS, NSA_HEADS_PER_GROUP, NSA_HEAD_DIM
    n_cmp = (S - CMP_LEN) // CMP_STRIDE + 1
    n_sel = S // SEL_LEN
    topk = min(SEL_TOPK, n_sel)
    qd, kd = H * DK, G * DK
    proj = h @ w_in
    q, k_c, v_c, k_s, v_s, k_w, v_w, gates = jnp.split(proj, [qd + i * kd for i in range(7)], axis=-1)

    def head_rms(z, w):
        zf = z.astype(jnp.float32)
        return (zf * lax.rsqrt(jnp.mean(zf * zf, axis=-1, keepdims=True) + RMS_EPS)).astype(z.dtype) * w

    q = head_rms(q.reshape(B, S, H, DK), qk_norm[0]).reshape(B, S, G, HG, DK).transpose(0, 2, 3, 1, 4)

    blk_idx = jnp.arange(n_cmp)[:, None] * CMP_STRIDE + jnp.arange(CMP_LEN)[None, :]

    def compress(kv, pos, w1, w2):
        blocks = kv.reshape(B, S, G, DK)[:, blk_idx] + pos[:, None, :]
        blocks = blocks.transpose(0, 3, 1, 2, 4).reshape(B, G, n_cmp, CMP_LEN * DK)
        return jax.nn.gelu(blocks @ w1) @ w2

    kc = head_rms(compress(k_c, cmp_pos[0], cmp_w1[0], cmp_w2[0]), qk_norm[1])
    vc = compress(v_c, cmp_pos[1], cmp_w1[1], cmp_w2[1])
    cmp_end = jnp.arange(n_cmp) * CMP_STRIDE + CMP_LEN - 1

    ks = head_rms(k_s.reshape(B, S, G, DK), qk_norm[2]).transpose(0, 2, 1, 3).reshape(B, G, n_sel, SEL_LEN, DK)
    vs = v_s.reshape(B, S, G, DK).transpose(0, 2, 1, 3).reshape(B, G, n_sel, SEL_LEN, DK)
    cmp_start = jnp.arange(n_cmp)[:, None] * CMP_STRIDE
    sel_start = jnp.arange(n_sel) * SEL_LEN
    overlap = ((cmp_start < sel_start[None, :] + SEL_LEN) & (cmp_start + CMP_LEN > sel_start[None, :])).astype(jnp.float32)

    pad = ((0, 0), (0, 0), (WINDOW, 0), (0, 0))
    kw = jnp.pad(head_rms(k_w.reshape(B, S, G, DK), qk_norm[3]).transpose(0, 2, 1, 3), pad)
    vw = jnp.pad(v_w.reshape(B, S, G, DK).transpose(0, 2, 1, 3), pad)

    gates = jax.nn.sigmoid(gates.astype(jnp.float32)).reshape(B, S, 3, G, HG).transpose(2, 0, 3, 4, 1)
    slopes = jnp.exp2(-8.0 * (jnp.arange(H, dtype=jnp.float32) + 1) / H).reshape(G, HG)
    b_ix = jnp.arange(B)[:, None, None, None]
    g_ix = jnp.arange(G)[None, :, None, None]
    j_sel = jnp.arange(n_sel)

    def block(qb):
        q0 = qb * NSA_Q_BLOCK
        t = q0 + jnp.arange(NSA_Q_BLOCK)
        qq = lax.dynamic_slice_in_dim(q, q0, NSA_Q_BLOCK, axis=3)
        dist_c = t[:, None] - cmp_end[None, :]
        s_c = jnp.einsum('bghqd,bgnd->bghqn', qq, kc) * NSA_SCALE - slopes[:, :, None, None] * dist_c
        p_c = masked_softmax(s_c, dist_c >= 0)
        o_c = jnp.einsum('bghqn,bgnd->bghqd', p_c, vc)
        imp = jnp.einsum('bghqn,nj->bgqj', p_c, overlap)
        valid = sel_start[None, :] <= t[:, None]
        forced = (j_sel == 0) | (j_sel == qb) | (j_sel == qb - 1)
        score = jnp.where(valid, jnp.where(forced, SEL_BIG, imp), -SEL_BIG)
        vals, idx = lax.top_k(score, topk)
        sel_ok = vals > -SEL_BIG / 2
        kg = ks[b_ix, g_ix, idx]
        vg = vs[b_ix, g_ix, idx]
        pos = idx[..., None] * SEL_LEN + jnp.arange(SEL_LEN)
        dist_s = t[None, None, :, None, None] - pos
        mask_s = sel_ok[..., None] & (dist_s >= 0)
        s_s = jnp.einsum('bghqd,bgqnld->bghqnl', qq, kg) * NSA_SCALE - slopes[None, :, :, None, None, None] * dist_s[:, :, None]
        p_s = masked_softmax(s_s.reshape(B, G, HG, NSA_Q_BLOCK, topk * SEL_LEN),
                             mask_s[:, :, None].reshape(B, G, 1, NSA_Q_BLOCK, topk * SEL_LEN))
        o_s = jnp.einsum('bghqnl,bgqnld->bghqd', p_s.reshape(B, G, HG, NSA_Q_BLOCK, topk, SEL_LEN), vg)
        kwin = lax.dynamic_slice_in_dim(kw, q0, WINDOW + NSA_Q_BLOCK, axis=2)
        vwin = lax.dynamic_slice_in_dim(vw, q0, WINDOW + NSA_Q_BLOCK, axis=2)
        p_k = q0 - WINDOW + jnp.arange(WINDOW + NSA_Q_BLOCK)
        dist_w = t[:, None] - p_k[None, :]
        mask_w = (dist_w >= 0) & (dist_w < WINDOW) & (p_k >= 0)[None, :]
        s_w = jnp.einsum('bghqd,bgkd->bghqk', qq, kwin) * NSA_SCALE - slopes[:, :, None, None] * dist_w
        o_w = jnp.einsum('bghqk,bgkd->bghqd', masked_softmax(s_w, mask_w), vwin)
        gb = lax.dynamic_slice_in_dim(gates, q0, NSA_Q_BLOCK, axis=4)[..., None]
        o = gb[0] * o_c + gb[1] * o_s + gb[2] * o_w
        return o.transpose(0, 3, 1, 2, 4).reshape(B, NSA_Q_BLOCK, H * DK)

    o = lax.map(block, jnp.arange(S // NSA_Q_BLOCK))
    o = o.transpose(1, 0, 2, 3).reshape(B, S, H * DK)
    return o @ w_out

def rwkv7_mixer(h, mu, w_rkv, w0, wd_a, wd_b, a0, wa_a, wa_b, wg_a, wg_b, k_k, k_a, r_k, ln_w, ln_b, w_out):
    B, S, D = h.shape
    H, N = RWKV_HEADS, RWKV_HEAD_DIM
    f32 = jnp.float32
    xx = jnp.pad(h, ((0, 0), (1, 0), (0, 0)))[:, :-1] - h
    xr, xw, xk, xv, xa, xg = [h + xx * mu[i] for i in range(6)]
    r = xr @ w_rkv[0]
    k = xk @ w_rkv[1]
    v = xv @ w_rkv[2]
    w_log = -jax.nn.softplus(-(w0 + jnp.tanh(xw @ wd_a) @ wd_b)) - 0.5
    decay = jnp.exp(-jnp.exp(w_log.astype(f32)))
    a = jax.nn.sigmoid((a0 + (xa @ wa_a) @ wa_b).astype(f32))
    g = jax.nn.sigmoid(xg @ wg_a) @ wg_b

    def heads(z):
        return z.reshape(B, S, H, N).astype(f32)

    r_h, v_h, w_h, a_h, k_h = heads(r), heads(v), heads(decay), heads(a), heads(k)
    kk = k_h * k_k.reshape(H, N).astype(f32)
    kk = kk * lax.rsqrt(jnp.maximum(jnp.sum(kk * kk, axis=-1, keepdims=True), 1e-24))
    k_h = k_h * (1 + (a_h - 1) * k_a.reshape(H, N).astype(f32))

    def step(state, inp):
        r_t, w_t, k_t, v_t, kk_t, a_t = inp
        sa = jnp.einsum('bhij,bhj->bhi', state, -kk_t)
        state = (state * w_t[:, :, None, :] + sa[..., None] * (kk_t * a_t)[:, :, None, :]
                 + v_t[..., None] * k_t[:, :, None, :])
        return state, jnp.einsum('bhij,bhj->bhi', state, r_t)

    xs = tuple(z.transpose(1, 0, 2, 3) for z in (r_h, w_h, k_h, v_h, kk, a_h))
    _, y = lax.scan(step, jnp.zeros((B, H, N, N), f32), xs)
    y = y.transpose(1, 0, 2, 3)
    mean = jnp.mean(y, axis=-1, keepdims=True)
    var = jnp.mean(jnp.square(y - mean), axis=-1, keepdims=True)
    y = ((y - mean) * lax.rsqrt(var + RWKV_GN_EPS)).reshape(B, S, D) * ln_w + ln_b
    y = y + (jnp.sum(r_h * k_h * r_k.astype(f32), axis=-1, keepdims=True) * v_h).reshape(B, S, D)
    return (y * g) @ w_out

def pool_mixer(h, w_grp, b, scale):
    B, S, D = h.shape
    hf = h.astype(jnp.float32)
    cs = jnp.pad(jnp.cumsum(hf, axis=1), ((0, 0), (1, 0), (0, 0)))
    t1 = jnp.arange(1, S + 1)
    groups = []
    for gi, win in enumerate(POOL_WINDOWS):
        csg = cs[:, :, gi * POOL_GROUP_DIM:(gi + 1) * POOL_GROUP_DIM]
        lo = jnp.maximum(t1 - win, 0)
        groups.append((csg[:, 1:] - csg[:, lo]) / (t1 - lo).astype(jnp.float32)[None, :, None])
    pooled = jnp.concatenate(groups, axis=-1) - hf
    y = jnp.einsum('bsgi,gio->bsgo', pooled.reshape(B, S, POOL_GROUPS, POOL_GROUP_DIM), w_grp).reshape(B, S, D) + b
    return y * scale

def setup_inputs(seed: int = 0) -> dict:
    key = jax.random.key(seed)
    ks = iter(jax.random.split(key, 40))
    D, F = D_MODEL, FFN_HIDDEN

    def nrm(shape, scale):
        return jax.random.normal(next(ks), shape, jnp.float32) * scale

    return {
        "x": nrm((BATCH, SEQ, D), 1.0),
        "c": nrm((BATCH, D), 1.0),
        "ada_w": nrm((DEPTH, D, N_MOD * D), 0.5 * D ** -0.5),
        "ada_b": nrm((DEPTH, N_MOD * D), 0.02),
        "norm_mix_w": 1.0 + nrm((DEPTH, D), 0.02),
        "norm_ffn_w": 1.0 + nrm((DEPTH, D), 0.02),
        "ffn_w_gate": nrm((DEPTH, D, F), D ** -0.5),
        "ffn_w_up": nrm((DEPTH, D, F), D ** -0.5),
        "ffn_w_down": nrm((DEPTH, F, D), F ** -0.5),
        "nsa_w_in": nrm((N_LAYERS_A, D, NSA_IN), D ** -0.5),
        "nsa_cmp_pos": nrm((N_LAYERS_A, 2, CMP_LEN, NSA_HEAD_DIM), 0.1),
        "nsa_cmp_w1": nrm((N_LAYERS_A, 2, CMP_LEN * NSA_HEAD_DIM, CMP_HIDDEN), (CMP_LEN * NSA_HEAD_DIM) ** -0.5),
        "nsa_cmp_w2": nrm((N_LAYERS_A, 2, CMP_HIDDEN, NSA_HEAD_DIM), CMP_HIDDEN ** -0.5),
        "nsa_qk_norm": 1.0 + nrm((N_LAYERS_A, 4, NSA_HEAD_DIM), 0.02),
        "nsa_w_out": nrm((N_LAYERS_A, NSA_HEADS * NSA_HEAD_DIM, D), D ** -0.5),
        "rwkv_mu": jax.random.uniform(next(ks), (N_LAYERS_B, 6, D), jnp.float32),
        "rwkv_w_rkv": nrm((N_LAYERS_B, 3, D, D), D ** -0.5),
        "rwkv_w0": nrm((N_LAYERS_B, D), 0.5),
        "rwkv_wd_a": nrm((N_LAYERS_B, D, DECAY_LORA), D ** -0.5),
        "rwkv_wd_b": nrm((N_LAYERS_B, DECAY_LORA, D), 0.5 * DECAY_LORA ** -0.5),
        "rwkv_a0": nrm((N_LAYERS_B, D), 0.5),
        "rwkv_wa_a": nrm((N_LAYERS_B, D, AAA_LORA), D ** -0.5),
        "rwkv_wa_b": nrm((N_LAYERS_B, AAA_LORA, D), 0.5 * AAA_LORA ** -0.5),
        "rwkv_wg_a": nrm((N_LAYERS_B, D, GATE_LORA), D ** -0.5),
        "rwkv_wg_b": nrm((N_LAYERS_B, GATE_LORA, D), GATE_LORA ** -0.5),
        "rwkv_k_k": 0.85 + nrm((N_LAYERS_B, D), 0.02),
        "rwkv_k_a": 1.0 + nrm((N_LAYERS_B, D), 0.02),
        "rwkv_r_k": nrm((N_LAYERS_B, RWKV_HEADS, RWKV_HEAD_DIM), 0.1),
        "rwkv_ln_w": 1.0 + nrm((N_LAYERS_B, D), 0.02),
        "rwkv_ln_b": nrm((N_LAYERS_B, D), 0.02),
        "rwkv_w_out": nrm((N_LAYERS_B, D, D), D ** -0.5),
        "pool_w": nrm((N_LAYERS_C, POOL_GROUPS, POOL_GROUP_DIM, POOL_GROUP_DIM), POOL_GROUP_DIM ** -0.5),
        "pool_b": nrm((N_LAYERS_C, D), 0.02),
        "pool_scale": 0.5 + nrm((N_LAYERS_C, D), 0.1),
    }

def reference(x, c, ada_w, ada_b, norm_mix_w, norm_ffn_w, ffn_w_gate, ffn_w_up, ffn_w_down,
              nsa_w_in, nsa_cmp_pos, nsa_cmp_w1, nsa_cmp_w2, nsa_qk_norm, nsa_w_out,
              rwkv_mu, rwkv_w_rkv, rwkv_w0, rwkv_wd_a, rwkv_wd_b, rwkv_a0, rwkv_wa_a, rwkv_wa_b,
              rwkv_wg_a, rwkv_wg_b, rwkv_k_k, rwkv_k_a, rwkv_r_k, rwkv_ln_w, rwkv_ln_b, rwkv_w_out,
              pool_w, pool_b, pool_scale):
    c_act = jax.nn.silu(c)
    for i in range(DEPTH):
        mod = c_act @ ada_w[i] + ada_b[i]
        sh_m, sc_m, g_m, sh_f, sc_f, g_f = jnp.split(mod, N_MOD, axis=-1)
        h = modulate(rms_norm(x, norm_mix_w[i]), sh_m, sc_m)
        kind, j = i % N_MIXERS, i // N_MIXERS
        if kind == 0:
            y = nsa_mixer(h, nsa_w_in[j], nsa_cmp_pos[j], nsa_cmp_w1[j], nsa_cmp_w2[j], nsa_qk_norm[j], nsa_w_out[j])
        elif kind == 1:
            y = rwkv7_mixer(h, rwkv_mu[j], rwkv_w_rkv[j], rwkv_w0[j], rwkv_wd_a[j], rwkv_wd_b[j], rwkv_a0[j],
                            rwkv_wa_a[j], rwkv_wa_b[j], rwkv_wg_a[j], rwkv_wg_b[j], rwkv_k_k[j], rwkv_k_a[j],
                            rwkv_r_k[j], rwkv_ln_w[j], rwkv_ln_b[j], rwkv_w_out[j])
        else:
            y = pool_mixer(h, pool_w[j], pool_b[j], pool_scale[j])
        x = x + (g_m[:, None, :] * y).astype(x.dtype)
        h = modulate(rms_norm(x, norm_ffn_w[i]), sh_f, sc_f)
        x = x + (g_f[:, None, :] * swiglu(h, ffn_w_gate[i], ffn_w_up[i], ffn_w_down[i])).astype(x.dtype)
    return x


_drawn_inputs = setup_inputs


def setup_inputs(seed=0):
    import zlib

    import numpy as np

    out = dict(_drawn_inputs(seed))
    spreads = {}
    factors = {'ada_b': 2.983,
     'norm_mix_w': 8.0,
     'norm_ffn_w': 8.0,
     'nsa_cmp_pos': 5.112,
     'nsa_qk_norm': 8.0}
    for name, (base, spread) in spreads.items():
        noise = np.random.default_rng([zlib.crc32(name.encode()), seed]).standard_normal(out[name].shape)
        drawn = base * np.exp(spread * noise) if base else spread * noise
        out[name] = __import__('jax').numpy.asarray(drawn.astype(out[name].dtype))
    for name, factor in factors.items():
        out[name] = (out[name] * factor).astype(out[name].dtype)
    return out
```

```python
from contextlib import ExitStack

import concourse.bass as bass
from concourse import mybir

F32 = mybir.dt.float32
F32R = mybir.dt.float32r
ALU = mybir.AluOpType
ACT = mybir.ActivationFunctionType
AX_X = mybir.AxisListType.X

P = 128
MASKED = 1e30
HUGE = 3e38
EPS = 1e-6
GELU_C = 0.7978845608028654
GELU_A = 0.044715


def spread(ap, axis, n):
    ap = ap.unsqueeze(axis)
    shape = list(ap.shape)
    shape[axis] = n
    return ap.to_broadcast(shape)


def trunk_kernel(nc, x, c, ada_w, ada_b, norm_mix_w, norm_ffn_w, w_gate, w_up, w_down,
                 w_in, cmp_pos, cmp_w1, cmp_w2, qk_norm, w_out, out):
    _, SEQ, D = x.shape
    F = w_gate.shape[2]
    DK = qk_norm.shape[2]
    H = w_out.shape[1] // DK
    G = (w_in.shape[2] - H * DK - 3 * H) // (6 * DK)
    HG = H // G
    L = cmp_pos.shape[2]
    STRIDE = L // 2
    NC = (SEQ - L) // STRIDE + 1
    TT = SEQ // P
    KD = D // P
    NP = G // 2
    QD, KV = H * DK, G * DK
    NB = D // 512
    NJ = F // 256
    SCALE = float(DK) ** -0.5
    assert TT == 2 and KD == 8 and NP == 2 and DK == 64 and HG == 4 and L == 32 and F == NJ * 256

    HALF = 1024
    NRAW, NRING = 3, 6
    START = {"c": 0, "s": 4, "w": 8, "gates": 12, "q0": 14, "q1": 18, "out": 22}
    FFN0 = START["out"] + KD
    COLUMN = {"q0": 0, "q1": NP * HG * DK, "c": QD, "s": QD + 2 * KV, "w": QD + 4 * KV, "gates": QD + 6 * KV}
    NAT = {("s", 0): 0, ("s", 1): 1, ("w", 0): 2, ("w", 1): 3, ("q0", 0): 4, ("q0", 1): 5, ("q1", 0): 6, ("q1", 1): 7}
    ROOT = {use: n for n, use in enumerate(
        ["x", ("s", 0), ("s", 1), ("w", 0), ("w", 1), "kc", ("q0", 0), ("q0", 1), ("q1", 0), ("q1", 1),
         ("x2", 0), ("x2", 1)])}
    FIRST_BLOCK = ["G0", "U0", "G1", "U1", "D0"]
    BLOCK = ["G0", "U0", "D1", "G1", "U1", "D0"]

    def half_at(j, what):
        if isinstance(j, int) and j == 0:
            return FFN0 + FIRST_BLOCK.index(what)
        return FFN0 + 5 + 6 * (j - 1) + (0 if isinstance(j, int) and j == NJ else BLOCK.index(what))

    def slot_of(j, what):
        if isinstance(j, int):
            return half_at(j, what) % NRING
        return (FFN0 + 5 + BLOCK.index(what)) % NRING

    STEPS = [(pr, tt, i) for pr in range(NP) for tt in range(TT) for i in range(HG)]
    NS = len(STEPS)
    LAG = 2
    Q1_STEP = 6
    GROUP1 = range(5, 9)
    GROUP1_OUT = 10
    GROUP2 = range(11, 15)
    order = [("c", tt, kv) for tt in range(TT) for kv in range(2)]
    order += [("hid",), ("k", 0), ("k", 1), ("cw2",), ("kc",), ("q", 0, 0), ("q", 0, 1), ("cs", 0, 0), ("cs", 0, 1)]
    for m in range(NS + LAG):
        if m == Q1_STEP:
            order += [("q", 1, 0), ("q", 1, 1)]
        if m == NS // 2:
            order += [("cs", 1, 0), ("cs", 1, 1)]
        if m == GROUP1_OUT:
            order += [("gm", 0), ("gm", 1), ("shf",)]
        if m >= LAG:
            pr, tt, i = STEPS[m - LAG]
            order += [("p", m - LAG, b) for b in range(tt + 1)]
            if i == HG - 1:
                order += [("pc", pr, tt, a) for a in range(2)]
    order += [("scf",), ("gf", 0), ("gf", 1)]
    T_AT = {use: n for n, use in enumerate(order)}

    with ExitStack() as ctx:
        def sem(name):
            return ctx.enter_context(nc.semaphore(name))

        base = (nc.sbuf_base + 31) // 32 * 32
        here = [base]

        def sized(shape):
            n = 4
            for s in shape[1:]:
                n *= s
            return (n + 31) // 32 * 32

        def at(name, shape, offset, dt=F32):
            return nc.alloc_sbuf_tensor_at(name, shape, dt, offset=offset)

        def sb(name, shape, dt=F32):
            offset = here[0]
            here[0] += sized(shape)
            return at(name, shape, offset, dt)

        def region(nbytes):
            offset = here[0]
            here[0] += nbytes
            return offset

        x_sb = sb("x_sb", [P, TT, D])
        raw = sb("raw", [P, NRAW, 2 * HALF])
        w_hi = sb("w_hi", [P, NRING, HALF], F32R)
        w_lo = sb("w_lo", [P, NRING, HALF], F32R)
        r_h = region(16384)
        h_hi = at("h_hi", [P, KD, SEQ], r_h, F32R)
        h_lo = at("h_lo", [P, KD, SEQ], r_h + 8192, F32R)
        NLATE = 3
        ada_l = [at(f"ada_late{i}", [P, 4, 256], r_h + 4096 * i) for i in range(NLATE)]
        pcT = at("pcT", [NC, 2, HG * P], r_h + 4096 * NLATE)
        ident = sb("ident", [P, P])
        ones = sb("ones", [P, P])
        W_MIX, W_FFN, SC_MIX, SH_MIX, SC_FFN, SH_FFN, C_IN, C_ACT = range(8)
        cols = sb("cols", [P, 8, KD])
        c_rep = sb("c_rep", [P, KD, 32])
        rows = sb("rows", [P, 512])
        ada_bias = sb("ada_bias", [P, 2, 512])
        sums = sb("sums", [P, 12, 8])
        roots = sb("roots", [P, 12, 8])
        minus_half = sb("minus_half", [P, 8])
        cw2 = sb("cw2", [P, 2, DK])
        qk_col = sb("qk_col", [P, 4])
        pos_col = sb("pos_col", [P, 2, STRIDE])
        norm_nat = sb("norm_nat", [8, 2, P])
        gates = sb("gates", [P, TT, 3 * H])
        den = sb("den", [P, 4, 4])
        recip = sb("recip", [P, 4, 4])
        weight = sb("weight", [P, 4, 4])
        negmax = sb("negmax", [P, 4, 4])
        qk_nat = sb("qk_nat", [4, 2, DK])
        pos_nat = sb("pos_nat", [2 * STRIDE, 2, DK])
        gel = sb("gel", [P, 2, 60])
        gel_t = sb("gel_t", [P, 2, 60])
        kcT = sb("kcT", [P, G * NC])
        kc_nat = sb("kc_nat", [G * NC, 2, DK])
        vc = sb("vc", [NC, G, DK])
        cmask = sb("cmask", [P, TT * HG, NC])
        cbias = sb("cbias", [P, NP, 2, TT * HG, NC])
        cprob = sb("cprob", [P, NP, 2 * TT * HG, NC])
        cstat = sb("cstat", [P, 4, 2 * TT * HG])
        cdist = sb("cdist", [P, TT, NC])
        kT = sb("kT", [P, NP, 2, SEQ])
        v_nat = sb("v_nat", [P, TT, 2, KV])

        r_q = region(4096)
        q_nat = at("q_nat", [P, TT, 512], r_q)
        gm_b = at("gm_b", [P, D], r_q)
        r_qT = region(8192)
        qT = at("qT", [P, NP, TT, HG, P], r_qT)
        r_bias = region(16384)
        bias = at("bias", [P, H, 2 * P], r_bias)
        gf_b = at("gf_b", [P, D], r_bias)
        r_o = region(16384)
        o_hi = at("o_hi", [P, TT, KD, P], r_o, F32R)
        o_lo = at("o_lo", [P, TT, KD, P], r_o + 8192, F32R)
        sq = at("sq", [P, 512], r_o)
        kcv = at("kcv", [P, TT, 2 * G, 2, DK], r_o + 8192)
        k_nat = at("k_nat", [P, TT, 2, KV], r_o + 2048)
        out_sb = at("out_sb", [P, TT, D], r_o + 8192)
        ada_e = [at("ada_e0", [P, 4, 512], r_bias), at("ada_e1", [P, 4, 512], r_bias + 8192),
                 at("ada_e2", [P, 4, 512], r_o)]
        r_p = region(16384)
        prob = at("prob", [P, 4, 4, 2 * P], r_p)
        xn = at("xn", [P, TT, D], r_p)
        h_f = at("h_f", [P, KD, SEQ], r_p + 8192)
        r_pt = region(24576)
        cw1 = at("cw1", [P, 2, STRIDE, P], r_pt)
        blocks = at("blocks", [P, 2, STRIDE, G * NC], r_pt + 16384)
        pt = [at("pt0", [P, 2, 2, 1, HG * P], r_pt + 16384), at("pt1", [P, 2, 2, 2, HG * P], r_pt)]
        th = at("th", [P, 2, 256], r_pt)
        sg = at("sg", [P, 2, 256], r_pt + 2048)
        act_f = at("act_f", [P, 2, 256], r_pt + 4096)
        act_hi = at("act_hi", [P, 2, 256], r_pt + 6144, F32R)
        act_lo = at("act_lo", [P, 2, 256], r_pt + 8192, F32R)
        mixed = at("mixed", [P, 2, 512], r_pt + 10240)
        assert here[0] <= nc.sbuf_usable_end, here[0]

        bank = [ctx.enter_context(nc.psum_tensor(f"bank{i}", [P, 512], F32)) for i in range(8)]

        x_in = [sem(f"x_in{t}") for t in range(TT)]
        c_in, norm_in, qk_in, pos_in, cw2_in, cw1_in = (sem(n) for n in ("c_in", "norm_in", "qk_in", "pos_in", "cw2_in", "cw1_in"))
        bias_in = [sem(f"bias_in{g}") for g in range(3)]
        ada_in = [sem(f"ada_in{i}") for i in range(3)]
        late_in = [sem(f"late_in{i}") for i in range(NLATE)]
        raw_in = [sem(f"raw_in{i}") for i in range(NRAW)]
        hi_done, lo_done, used = sem("hi_done"), sem("lo_done"), sem("used")
        consts = sem("consts")
        bias_ready = sem("bias_ready")
        dve = sem("dve")
        pool = sem("pool")
        c_tanh, c_ready, sq_x = sem("c_tanh"), sem("c_ready"), sem("sq_x")
        params_t, col_turn = sem("params_t"), sem("col_turn")
        var_ready, root_ready = sem("var_ready"), sem("root_ready")
        xn_ready, xnT = sem("xn_ready"), sem("xnT")
        ada_used, rows_ready, mix_cols = sem("ada_used"), sem("rows_ready"), sem("mix_cols")
        hf_ready, hhi_ready, h_ready = sem("hf_ready"), sem("hhi_ready"), sem("h_ready")
        copied, squared, scaled = sem("copied"), sem("squared"), sem("scaled")
        gates_ready = sem("gates_ready")
        t_filled, t_drained = sem("t_filled"), sem("t_drained")
        gel_sq, gel_in, gel_tanh, gel_ready, kc_sum, kc_ready = (sem(n) for n in ("gel_sq", "gel_in", "gel_tanh", "gel_ready", "kc_sum", "kc_ready"))
        s_ready, max_ready, exp_ready, weight_ready, p_ready = (sem(n) for n in ("s_ready", "max_ready", "exp_ready", "weight_ready", "p_ready"))
        cs_ready, ce_ready, cp_ready = sem("cs_ready"), sem("ce_ready"), sem("cp_ready")
        pv_done, ohi_ready, o_ready = sem("pv_done"), sem("ohi_ready"), sem("o_ready")
        late_used = sem("late_used")
        y_done = sem("y_done")
        xn2_ready, xn2T, h2f_ready, h2hi_ready, h2_ready = (sem(n) for n in ("xn2_ready", "xn2T", "h2f_ready", "h2hi_ready", "h2_ready"))
        th_ready, act_ready, ahi_ready, a_ready = (sem(n) for n in ("th_ready", "act_ready", "ahi_ready", "a_ready"))
        y2_done, out_ready, out_done = sem("y2_done"), sem("out_ready"), sem("out_done")

        def unit_of(n):
            return n // 2

        def raw_half(n, width=HALF):
            return raw[:, unit_of(n) % NRAW, (n % 2) * width:(n % 2 + 1) * width]

        def raw_ffn(what):
            slot = (START["out"] + KD) // 2 % NRAW + "GUD".index(what[0])
            f = int(what[1])
            if what[0] == "D":
                return raw[:, slot % NRAW, f * HALF:(f + 1) * HALF]
            return raw[:, slot % NRAW, :].rearrange("p (k n) -> p k n", n=256)[:, :, f * P:(f + 1) * P]

        def split_parts(tensor, slot, what):
            v = tensor[:, slot, :]
            return v if what[0] == "D" else v.rearrange("p (k n) -> p k n", n=P)

        def ffn_unit(j, what):
            return (FFN0 // 2) + 3 * j + "GUD".index(what[0])

        def owner(j, what):
            return j - 1 if what == "D1" else j

        def width_of(n):
            return KD // 2 * 3 * H if START["gates"] <= n < START["q0"] else HALF

        block = ctx.enter_context(nc.Block())

        @block.sync
        def _(sp):
            for t in range(TT):
                sp.dma_start(x_sb[:, t, :], x[0, t * P:(t + 1) * P, :]).then_inc(x_in[t], 16)
            ada_v = ada_w[0].rearrange("(p k) n -> p k n", k=KD)

            def load(u, src, cols_of=2 * HALF, shape=None):
                dst = raw[:, u % NRAW, 0:cols_of]
                if shape:
                    dst = dst.rearrange("p (k n) -> p k n", n=shape)
                sp.dma_start(dst, src).then_inc(raw_in[u % NRAW], 16)

            def free(u):
                if u >= NRAW:
                    sp.wait_ge(lo_done, 2 * (u - NRAW) + 2)

            for k in range(KD):
                if k >= 3:
                    sp.wait_ge(ada_used, k - 2)
                sp.dma_start(ada_e[k % 3][:], ada_v[:, k, 0:2048].rearrange("p (j n) -> p j n", j=4)).then_inc(ada_in[k % 3], 16)

            w_in_v = w_in[0].rearrange("(k p) n -> p k n", p=P)

            def load_in(name, part):
                u = START[name] // 2 + part
                free(u)
                if name == "gates":
                    load(u, w_in_v[:, :, COLUMN[name]:COLUMN[name] + 3 * H], KD * 3 * H, 3 * H)
                else:
                    load(u, w_in_v[:, 4 * part:4 * part + 4, COLUMN[name]:COLUMN[name] + 512], shape=512)

            def load_out(part):
                u = START["out"] // 2 + part
                free(u)
                pr, i = part // 2, 2 * (part % 2)
                v = w_out[0].rearrange("(r a i d) n -> r a d i n", r=NP, a=2, i=HG)
                for a in range(2):
                    sp.dma_start(raw[64 * a:64 * a + 64, u % NRAW, :].rearrange("p (i n) -> p i n", i=2),
                                 v[pr, a, :, i:i + 2, :]).then_inc(raw_in[u % NRAW], 8 * 2)

            for part in range(2):
                load_in("c", part)
            load_in("s", 0)
            w1_v = cmp_w1[0].rearrange("v (a l d) f -> v a d l f", a=2, l=STRIDE)
            for kv in range(2):
                for a in range(2):
                    sp.dma_start(cw1[64 * a:64 * a + 64, kv, :, :], w1_v[kv, a]).then_inc(cw1_in, 16)
            load_in("s", 1)
            for name in ("w",):
                for part in range(2):
                    load_in(name, part)
            load_in("gates", 0)
            for name in ("q0", "q1"):
                for part in range(2):
                    load_in(name, part)

            def load_late(q):
                g, h, k = q // 16, q // 8 % 2, q % 8
                if q < NLATE:
                    sp.wait_ge(used, START["out"])
                else:
                    sp.wait_ge(late_used, q - NLATE + 1)
                src = ada_v[:, k, 2048 * (g + 1):2048 * (g + 2)].rearrange("p (j n) -> p j n", j=4)[:, :, 256 * h:256 * h + 256]
                sp.dma_start(ada_l[q % NLATE][:], src).then_inc(late_in[q % NLATE], 16)

            for part in range(3):
                load_out(part)
            for q in range(6):
                load_late(q)
            load_out(3)

            def load_ffn(j, what):
                if isinstance(j, int) and j == 0:
                    free(FFN0 // 2 + "GUD".index(what))
                else:
                    last = {"G": (j - 1, "G1"), "U": (j - 1, "U1"), "D": (j, "D1")}[what]
                    if isinstance(j, int) and j == 1 and what != "D":
                        sp.wait_ge(lo_done, half_at(0, last[1]) + 1)
                    else:
                        jj, w = last
                        sp.wait_ge(lo_done, FFN0 + 5 + 6 * (jj - 1) + BLOCK.index(w) + 1)
                slot = (FFN0 // 2 + "GUD".index(what)) % NRAW
                if what == "D":
                    src = w_down[0].rearrange("(j f p) n -> j p f n", f=2, p=P)[j]
                    dst = raw[:, slot, :].rearrange("p (f n) -> p f n", f=2)
                else:
                    w = w_gate if what == "G" else w_up
                    src = w[0].rearrange("(k p) (j n) -> j p k n", p=P, n=256)[j]
                    dst = raw[:, slot, :].rearrange("p (k n) -> p k n", n=256)
                sp.dma_start(dst, src).then_inc(raw_in[slot], 16)

            for q in range(6, 16):
                load_late(q)
            for q in range(16, 32):
                load_late(q)
                if q == 20:
                    load_ffn(0, "G")
                if q == 24:
                    load_ffn(0, "U")
            load_ffn(0, "D")
            for j in range(1, NJ):
                for what in "GUD":
                    load_ffn(j, what)

            for tt in range(TT):
                for nb in range(NB):
                    sp.wait_ge(out_ready, tt * NB + nb + 1)
                    sp.dma_start(out[0, tt * P:(tt + 1) * P, nb * 512:nb * 512 + 512],
                                 out_sb[:, tt, nb * 512:nb * 512 + 512]).then_inc(out_done, 16)
            sp.wait_ge(out_done, 16 * TT * NB)

        @block.gpsimd
        def _(gp):
            g = nc.gpsimd
            n_pool = [0]

            def link(ins):
                n_pool[0] += 1
                ins.then_inc(pool, 1)
                gp.wait_ge(pool, n_pool[0])

            g.memset(minus_half[:], -0.5)
            g.memset(ones[:], 1.0)
            link(g.memset(ident[:], 0.0))
            g.affine_select(out=ident[:], in_=ident[:], compare_op=ALU.not_equal, fill=1.0, base=0,
                            pattern=[[-1, P]], channel_multiplier=1).then_inc(consts, 1)

            def root(use, n, parts=P):
                k = ROOT[use]
                gp.wait_ge(var_ready, k + 1)
                g.tensor_tensor(roots[0:parts, k, 0:n], sums[0:parts, k, 0:n], minus_half[0:parts, 0:n], ALU.pow).then_inc(root_ready, 1)

            root("x", TT)
            slope = [2.0 ** (-8.0 * (h + 1) / H) for h in range(H)]
            link(g.iota(cdist[:], pattern=[[P, TT], [-STRIDE, NC]], base=1 - L, channel_multiplier=1,
                        allow_small_or_imprecise_dtypes=True))
            for h in range(H):
                pr, a, i = h // (2 * HG), h // HG % 2, h % HG
                for tt in range(TT):
                    last = g.tensor_scalar(cbias[:, pr, a, tt * HG + i, :], cdist[:, tt, :], slope[h], 0.0, ALU.mult, ALU.add)
            link(last)
            link(g.memset(cmask[:], 1.0))
            g.affine_select(out=cmask[:].rearrange("p (t i) n -> p t i n", t=TT), in_=cmask[:].rearrange("p (t i) n -> p t i n", t=TT),
                            compare_op=ALU.is_ge, fill=0.0, base=1 - L, pattern=[[P, TT], [0, HG], [-STRIDE, NC]], channel_multiplier=1)
            for pr in range(NP):
                v = cbias[:, pr].rearrange("p a (t i) n -> p a t i n", t=TT)
                for a in range(2):
                    last = g.affine_select(out=v[:, a], in_=v[:, a], compare_op=ALU.is_ge, fill=MASKED, base=1 - L,
                                           pattern=[[P, TT], [0, HG], [-STRIDE, NC]], channel_multiplier=1)
            link(last)
            gp.wait_ge(ada_used, KD)
            link(g.iota(bias[:, H - 1, :], pattern=[[-1, 2 * P]], base=P, channel_multiplier=1,
                        allow_small_or_imprecise_dtypes=True))
            for h in range(H):
                last = g.tensor_scalar(bias[:, h, :], bias[:, H - 1, :], slope[h], 0.0, ALU.mult, ALU.add)
            link(last)
            for h in range(0, H, HG):
                last = g.affine_select(out=bias[:, h:h + HG, :], in_=bias[:, h:h + HG, :], compare_op=ALU.is_ge, fill=MASKED, base=P,
                                       pattern=[[0, HG], [-1, 2 * P]], channel_multiplier=1)
            last.then_inc(bias_ready, 1)

            root(("s", 0), G)
            root(("s", 1), G)
            root(("w", 0), G)
            root(("w", 1), G)
            root("kc", 1, G * NC)
            root(("q0", 0), 2 * HG)
            root(("q0", 1), 2 * HG)

            def normalise(m):
                n = P * (STEPS[m][1] + 1)
                gp.wait_ge(weight_ready, m + 1)
                for ab in range(4):
                    last = g.tensor_scalar(prob[:, m % 4, ab, 0:n], prob[:, m % 4, ab, 0:n], weight[:, m % 4, ab:ab + 1], 1.0,
                                           ALU.mult, ALU.mult)
                last.then_inc(p_ready, 1)

            for m in range(NS):
                if m == 4:
                    root(("q1", 0), 2 * HG)
                    root(("q1", 1), 2 * HG)
                normalise(m)
            root(("x2", 0), 1)
            root(("x2", 1), 1)

        @block.scalar
        def _(act):
            s = nc.scalar
            act.dma_start(cols[:, C_IN, :], c[0].rearrange("(p k) -> p k", k=KD)).then_inc(c_in, 16)
            act.dma_start(norm_nat[:, 0, :], norm_mix_w[0].rearrange("(k p) -> k p", p=P)).then_inc(norm_in, 16)
            act.dma_start(norm_nat[:, 1, :], norm_ffn_w[0].rearrange("(k p) -> k p", p=P)).then_inc(norm_in, 16)
            for a in range(2):
                act.dma_start(qk_nat[:, a, :], qk_norm[0]).then_inc(qk_in, 16)
            for kv in range(2):
                act.dma_start(pos_nat[STRIDE * kv:STRIDE * (kv + 1), :, :],
                              cmp_pos[0, kv].rearrange("(a l) d -> l a d", a=2)).then_inc(pos_in, 16)
            act.dma_start(cw2[:], cmp_w2[0].rearrange("v f d -> f v d")).then_inc(cw2_in, 16)

            def load_bias(gr):
                for j in range(4):
                    b = 4 * gr + j
                    act.dma_start(ada_bias[32 * j:32 * j + 32, gr % 2, :],
                                  ada_b[0:1, 512 * b:512 * b + 512].to_broadcast([32, 512])).then_inc(bias_in[gr], 16)

            load_bias(0)
            load_bias(1)
            act.wait_ge(c_in, 16)
            s.activation(cols[:, C_ACT, :], cols[:, C_IN, :], ACT.Tanh, scale=0.5).then_inc(c_tanh, 1)

            def hi(n):
                w = width_of(n)
                act.wait_ge(raw_in[unit_of(n) % NRAW], raw_target(n))
                if n >= NRING:
                    act.wait_ge(used, n - NRING + 1)
                s.activation(w_hi[:, n % NRING, 0:w], raw_half(n, w), ACT.Copy).then_inc(hi_done, 1)

            def raw_target(n):
                u = unit_of(n)
                return 16 * sum(2 if START["out"] // 2 <= v < FFN0 // 2 else 1 for v in range(u % NRAW, u + 1, NRAW))

            def hi_ffn(j, what):
                o = owner(j, what)
                slot = (FFN0 // 2 + "GUD".index(what[0])) % NRAW
                act.wait_ge(raw_in[slot], ffn_target(slot, o))
                n = half_at(j, what)
                act.wait_ge(used, n - NRING + 1)
                r = slot_of(j, what)
                s.activation(split_parts(w_hi, r, what), raw_ffn(what), ACT.Copy).then_inc(hi_done, 1)

            def ffn_target(slot, o):
                before = 16 * sum(2 if START["out"] // 2 <= v < FFN0 // 2 else 1 for v in range(slot, FFN0 // 2, NRAW))
                return before + 16 * (o + 1)

            for n in range(3):
                hi(n)
            for i in range(4):
                act.wait_ge(hf_ready, i + 1)
                s.activation(h_hi[:, 2 * i:2 * i + 2, :], h_f[:, 2 * i:2 * i + 2, :], ACT.Copy).then_inc(hhi_ready, 1)
            for n in range(3, 6):
                hi(n)

            def square(name, tt, bk, width):
                act.wait_ge(used, DONE[name])
                if NAT[name, tt] >= 1:
                    act.wait_ge(var_ready, ROOT[PREV[name, tt]] + 1)
                s.activation(sq[:, 0:width], bank[bk][:, 0:width], ACT.Square).then_inc(squared, 1)

            DONE = {name: START[name] + (2 if name == "gates" else 4) for name in START}
            PREV = dict(zip(list(NAT)[1:], list(NAT)))
            for n in range(6, 8):
                hi(n)
            act.wait_ge(used, DONE["c"])
            for tt in range(TT):
                s.activation(kcv[:, tt], spread(bank[6 + tt][:, :].rearrange("p (g d) -> p g d", d=DK), 2, 2), ACT.Copy).then_inc(copied, 1)
            for name, bk, br, upto in (("s", 0, 0, range(8, 12)), ("w", 2, 1, range(12, 16))):
                for n in upto:
                    hi(n)
                for tt in range(TT):
                    square(name, tt, bk + tt, KV)
                    s.activation(v_nat[:, tt, br, :], bank[bk + tt][:, KV:2 * KV], ACT.Copy).then_inc(copied, 1)
                if name == "w":
                    act.wait_ge(t_filled, T_AT["hid",] + 1)
                    hid = bank[4 + T_AT["hid",] % 2][:, 0:128].rearrange("p (v n) -> p v n", v=2)[:, :, 0:G * NC]
                    s.activation(gel_t[:], hid, ACT.Square).then_inc(gel_sq, 1)
                    act.wait_ge(gel_in, 1)
                    s.activation(gel_t[:], gel_t[:], ACT.Tanh, scale=GELU_C).then_inc(gel_tanh, 1)
            act.wait_ge(used, DONE["gates"])
            for tt in range(TT):
                s.activation(gates[:, tt, :], bank[6 + tt][:, 0:3 * H], ACT.Tanh, scale=0.5).then_inc(copied, 1)
            for n in range(16, 19):
                hi(n)
            act.wait_ge(t_filled, T_AT["cw2",] + 1)
            kcb = bank[4 + T_AT["cw2",] % 2]
            s.activation(kc_nat[:, 0, :], kcb[0:G * NC, 0:DK], ACT.Square, accum_out=sums[0:G * NC, ROOT["kc"], 1:2]).then_inc(kc_sum, 1)
            for n in range(19, 22):
                hi(n)
            for tt in range(TT):
                square("q0", tt, tt, 512)

            def c_exp(pr):
                act.wait_ge(cs_ready, pr + 1)
                s.activation(cprob[:, pr], cprob[:, pr], ACT.Exp, scale=-1.0).then_inc(ce_ready, 1)

            def exps(m):
                n = P * (STEPS[m][1] + 1)
                for ab in range(4):
                    act.wait_ge(max_ready, 4 * m + ab + 1)
                    v = prob[:, m % 4, ab, 0:n]
                    s.activation(v, v, ACT.Exp, bias=negmax[:, m % 4, ab:ab + 1], scale=-1.0,
                                 accum_out=den[:, m % 4, ab:ab + 1]).then_inc(exp_ready, 1)

            def o_part(v):
                pr, tt = v // TT, v % TT
                act.wait_ge(pv_done, v + 1)
                s.activation(o_hi[:, tt, HG * pr:HG * pr + HG, :], bank[6][:, :].rearrange("p (i n) -> p i n", i=HG),
                             ACT.Copy).then_inc(ohi_ready, 1)

            c_exp(0)
            ahead = {0: 22, 1: 23, 2: 24, 3: 25, 5: 26, 6: 27}
            for m in range(NS + LAG):
                if m == 4:
                    for tt in range(TT):
                        square("q1", tt, 6 + tt, 512)
                if m == NS // 2:
                    c_exp(1)
                if m < NS:
                    exps(m)
                if m in ahead:
                    hi(ahead[m])
                if m == 9:
                    act.wait_ge(rows_ready, 1)
                    load_bias(2)
                if m > LAG and (m - LAG) % HG == 0:
                    o_part((m - LAG) // HG - 1)
            for n in (28, 29):
                hi(n)
            o_part(NP * TT - 1)
            for what in FIRST_BLOCK:
                hi_ffn(0, what)
            for i in range(4):
                tt, half = i // 2, i % 2
                act.wait_ge(h2f_ready, i + 1)
                s.activation(h_hi[:, 4 * half:4 * half + 4, tt * P:(tt + 1) * P],
                             h_f[:, 4 * half:4 * half + 4, tt * P:(tt + 1) * P], ACT.Copy).then_inc(h2hi_ready, 1)

            def act_gate(j, f):
                act.wait_ge(used, half_at(j, f"U{f}") + 1)
                s.activation(th[:, f, :], bank[4 + f][:, 0:256], ACT.Tanh, scale=0.5).then_inc(th_ready, 1)
                act.wait_ge(act_ready, 2 * j + f + 1)
                s.activation(act_hi[:, f, :], act_f[:, f, :], ACT.Copy).then_inc(ahi_ready, 1)

            act_gate(0, 0)
            for what in ("G0", "U0"):
                hi_ffn(1, what)
            act_gate(0, 1)
            hi_ffn(1, "D1")

            def act_block(j):
                for what in ("G1", "U1", "D0"):
                    hi_ffn(j, what)
                act_gate(j, 0)
                for what in ("G0", "U0"):
                    hi_ffn(j + 1, what)
                act_gate(j, 1)
                hi_ffn(j + 1, "D1")

            for j in range(1, NJ - 1):
                act_block(j)
            j = NJ - 1
            for what in ("G1", "U1", "D0"):
                hi_ffn(j, what)
            act_gate(j, 0)
            act_gate(j, 1)
            hi_ffn(NJ, "D1")

        @block.vector
        def _(ve):
            v = nc.vector
            n_dve = [0]

            def link(ins):
                n_dve[0] += 1
                ins.then_inc(dve, 1)
                ve.wait_ge(dve, n_dve[0])

            def mean_eps(use, n, size, parts=P):
                v.tensor_scalar(sums[0:parts, ROOT[use], 0:n], sums[0:parts, ROOT[use], 0:n], 1.0 / size, EPS,
                                ALU.mult, ALU.add).then_inc(var_ready, 1)

            for t in range(TT):
                ve.wait_ge(x_in[t], 16)
                link(v.tensor_tensor_reduce(xn[:, t, :], x_sb[:, t, :], x_sb[:, t, :], 1.0, 0.0, ALU.mult, ALU.add,
                                            sums[:, ROOT["x"], t:t + 1]))
            mean_eps("x", TT, D)
            ve.wait_ge(c_tanh, 1)
            link(v.tensor_scalar(cols[:, C_ACT, :], cols[:, C_ACT, :], 0.5, 0.5, ALU.mult, ALU.add))
            link(v.tensor_tensor(cols[:, C_ACT, :], cols[:, C_ACT, :], cols[:, C_IN, :], ALU.mult))
            v.tensor_copy(c_rep[:], spread(cols[:, C_ACT, :], 2, 32)).then_inc(c_ready, 1)
            ve.wait_ge(root_ready, ROOT["x"] + 1)
            for t in range(TT):
                v.tensor_scalar(xn[:, t, :], x_sb[:, t, :], roots[:, ROOT["x"], t:t + 1], None, ALU.mult).then_inc(xn_ready, 1)
            ve.wait_ge(params_t, 1)
            pb = bank[5]
            v.tensor_copy(cols[:, W_MIX:W_FFN + 1, :], pb[:, 0:16].rearrange("p (a k) -> p a k", a=2))
            v.tensor_scalar(qk_col[:, 0:1], pb[:, 16:17], -SCALE, None, ALU.mult)
            v.tensor_copy(qk_col[:, 1:4], pb[:, 17:20])
            link(v.tensor_copy(pos_col[:], pb[:, 32:64].rearrange("p (a k) -> p a k", a=2)))

            def lo(n):
                w = width_of(n)
                ve.wait_ge(hi_done, n + 1)
                v.tensor_tensor(w_lo[:, n % NRING, 0:w], raw_half(n, w), w_hi[:, n % NRING, 0:w].bitcast(F32), ALU.subtract).then_inc(lo_done, 1)

            def lo_ffn(j, what):
                ve.wait_ge(hi_done, half_at(j, what) + 1)
                r = slot_of(j, what)
                v.tensor_tensor(split_parts(w_lo, r, what), raw_ffn(what), split_parts(w_hi, r, what).bitcast(F32),
                                ALU.subtract).then_inc(lo_done, 1)

            def rows_of(gr, bk):
                ve.wait_ge(ada_used, KD) if gr == 0 else ve.wait_ge(late_used, 16 * gr)
                ve.wait_ge(bias_in[gr], 64)
                v.tensor_tensor(rows[:], bank[bk][:, :], ada_bias[:, gr % 2, :], ALU.add).then_inc(rows_ready, 1)

            rows_of(0, 4)
            for n in range(3):
                lo(n)
            ve.wait_ge(mix_cols, 1)
            v.tensor_copy(cols[:, SH_MIX, :], pb[:, 64:72])
            link(v.scalar_tensor_tensor(out=cols[:, SC_MIX, :], in0=pb[:, 72:80], scalar=1.0, in1=cols[:, W_MIX, :], op0=ALU.add, op1=ALU.mult))
            for i in range(4):
                ve.wait_ge(xnT, i + 1)
                for k in (2 * i, 2 * i + 1):
                    last = v.tensor_scalar(h_f[:, k, :], bank[i][:, (k % 2) * 256:(k % 2) * 256 + 256],
                                           cols[:, SC_MIX, k:k + 1], cols[:, SH_MIX, k:k + 1], ALU.mult, ALU.add)
                last.then_inc(hf_ready, 1)
            for i in range(4):
                ve.wait_ge(hhi_ready, i + 1)
                v.tensor_tensor(h_lo[:, 2 * i:2 * i + 2, :], h_f[:, 2 * i:2 * i + 2, :], h_hi[:, 2 * i:2 * i + 2, :].bitcast(F32),
                                ALU.subtract).then_inc(h_ready, 1)
            for n in range(3, 8):
                lo(n)

            def t_bank(*use):
                ve.wait_ge(t_filled, T_AT[use] + 1)
                return bank[4 + T_AT[use] % 2]

            def drained(*use, ins):
                ins.then_inc(t_drained, 1)

            def spread_blocks(tt, kv):
                b = t_bank("c", tt, kv)
                for a in range(2):
                    first = (0, 1)[a] if tt == 0 else 0
                    n = (8, 7)[a] if tt == 0 else (7, 8)[a]
                    at_n = 8 * tt + first - a
                    src = b[64 * a:64 * a + 64, :].rearrange("p (g n l) -> p g l n", g=G, l=STRIDE)
                    dst = blocks[64 * a:64 * a + 64, kv].rearrange("p l (g n) -> p g l n", g=G)
                    for g in range(G):
                        last = v.tensor_tensor(dst[:, g, :, at_n:at_n + n], src[:, g, :, first:first + n],
                                               spread(pos_col[64 * a:64 * a + 64, kv, :], 2, n), ALU.add)
                drained("c", tt, kv, ins=last)

            def head_sums(name, tt, heads):
                k = NAT[name, tt]
                ve.wait_ge(squared, k + 1)
                link(v.tensor_reduce(sums[:, ROOT[name, tt], 0:heads], sq[:, 0:heads * DK].rearrange("p (h d) -> p h d", d=DK), AX_X, ALU.add))
                v.tensor_scalar(sums[:, ROOT[name, tt], 0:heads], sums[:, ROOT[name, tt], 0:heads], 1.0 / DK, EPS,
                                ALU.mult, ALU.add).then_inc(var_ready, 1)

            def head_scale(name, tt, dst, bk, heads):
                ve.wait_ge(root_ready, ROOT[name, tt] + 1)
                if name[0] != "q":
                    ve.wait_ge(copied, NAT[name, tt] + 3)
                r = roots[:, ROOT[name, tt], 0:heads]
                if name[0] == "q":
                    v.tensor_tensor(dst.rearrange("p (i a d) -> p a i d", a=2, d=DK), bank[bk][:, :].rearrange("p (a i d) -> p a i d", a=2, d=DK),
                                    spread(r.rearrange("p (a i) -> p a i", a=2), 3, DK), ALU.mult).then_inc(scaled, 1)
                else:
                    v.tensor_tensor(dst.rearrange("p (h d) -> p h d", d=DK), bank[bk][:, 0:heads * DK].rearrange("p (h d) -> p h d", d=DK),
                                    spread(r, 2, DK), ALU.mult).then_inc(scaled, 1)

            for tt in range(TT):
                for kv in range(2):
                    spread_blocks(tt, kv)
            for name, bk, br, upto in (("s", 0, 0, range(8, 12)), ("w", 2, 1, range(12, 16))):
                for n in upto:
                    lo(n)
                for tt in range(TT):
                    head_sums(name, tt, G)
                for tt in range(TT):
                    head_scale(name, tt, k_nat[:, tt, br, :], bk + tt, G)
            b = t_bank("hid")
            hid = b[:, 0:128].rearrange("p (v n) -> p v n", v=2)[:, :, 0:G * NC]
            ve.wait_ge(gel_sq, 1)
            link(v.tensor_scalar(gel_t[:], gel_t[:], GELU_A, 1.0, ALU.mult, ALU.add))
            v.tensor_tensor(gel_t[:], gel_t[:], hid, ALU.mult).then_inc(gel_in, 1)
            ve.wait_ge(gel_tanh, 1)
            link(v.tensor_scalar(gel_t[:], gel_t[:], 0.5, 0.5, ALU.mult, ALU.add))
            v.tensor_tensor(gel[:], gel_t[:], hid, ALU.mult).then_inc(t_drained, 1)
            for tt in range(TT):
                b = t_bank("k", tt)
                for br in range(2):
                    last = v.tensor_scalar(kT[:, :, br, tt * P:(tt + 1) * P], b[:, br * 256:br * 256 + 256].rearrange("p (r n) -> p r n", r=NP),
                                           qk_col[:, 2 + br:3 + br], None, ALU.mult)
                last.then_inc(t_drained, 1)
            ve.wait_ge(copied, 8)
            link(v.tensor_scalar(gates[:], gates[:], 0.5, 0.5, ALU.mult, ALU.add))
            for n in range(16, 19):
                lo(n)
            b = t_bank("cw2")
            ve.wait_ge(kc_sum, 1)
            v.tensor_copy(vc[:], b[0:NC, DK:DK + G * DK].rearrange("p (g d) -> p g d", g=G))
            v.tensor_scalar(sums[0:G * NC, ROOT["kc"], 0:1], sums[0:G * NC, ROOT["kc"], 1:2], 1.0 / DK, EPS,
                            ALU.mult, ALU.add).then_inc(var_ready, 1)
            for n in range(19, 22):
                lo(n)
            ve.wait_ge(root_ready, ROOT["kc"] + 1)
            for a in range(2):
                last = v.tensor_scalar(kc_nat[:, a, :], b[0:G * NC, 0:DK], roots[0:G * NC, ROOT["kc"], 0:1], None, ALU.mult)
            last.then_inc(t_drained, 1)
            b = t_bank("kc")
            v.tensor_scalar(kcT[:], b[:, 0:G * NC], qk_col[:, 1:2], None, ALU.mult).then_inc(t_drained, 1)

            def queries(pr):
                for tt in range(TT):
                    b = t_bank("q", pr, tt)
                    v.tensor_scalar(qT[:, pr, tt], b[:, :].rearrange("p (i n) -> p i n", i=HG), qk_col[:, 0:1], None, ALU.mult).then_inc(t_drained, 1)

            for tt in range(TT):
                head_sums("q0", tt, 2 * HG)
            for tt in range(TT):
                head_scale("q0", tt, q_nat[:, tt, :], tt, 2 * HG)
            queries(0)
            ve.wait_ge(bias_ready, 1)

            def c_scores(pr):
                cp = cprob[:, pr]
                for a in range(2):
                    b = t_bank("cs", pr, a)
                    last = v.tensor_tensor(cp[:, a * TT * HG:(a + 1) * TT * HG, :], b[:, 0:TT * HG * NC].rearrange("p (t n) -> p t n", n=NC),
                                           cbias[:, pr, a], ALU.add)
                    last.then_inc(t_drained, 1)
                ve.wait_ge(t_drained, T_AT["cs", pr, 1] + 1)
                link(v.tensor_reduce(cstat[:, 0, :], cp, AX_X, ALU.min))
                v.tensor_tensor(cp, cp, spread(cstat[:, 0, :], 2, NC), ALU.subtract).then_inc(cs_ready, 1)

            def c_weights(pr):
                cp = cprob[:, pr]
                ve.wait_ge(ce_ready, pr + 1)
                for a in range(2):
                    last = v.tensor_tensor(cp[:, a * TT * HG:(a + 1) * TT * HG, :], cp[:, a * TT * HG:(a + 1) * TT * HG, :], cmask[:], ALU.mult)
                link(last)
                link(v.tensor_reduce(cstat[:, 1, :], cp, AX_X, ALU.add))
                link(v.tensor_scalar(cstat[:, 1, :], cstat[:, 1, :], 1e-30, None, ALU.max))
                link(v.reciprocal(cstat[:, 2, :], cstat[:, 1, :]))
                for a in range(2):
                    h0 = (2 * pr + a) * HG
                    last = v.tensor_tensor(cstat[:, 3, a * TT * HG:(a + 1) * TT * HG].rearrange("p (t i) -> p t i", t=TT),
                                           cstat[:, 2, a * TT * HG:(a + 1) * TT * HG].rearrange("p (t i) -> p t i", t=TT),
                                           gates[:, :, h0:h0 + HG], ALU.mult)
                link(last)
                v.tensor_tensor(cp, cp, spread(cstat[:, 3, :], 2, NC), ALU.mult).then_inc(cp_ready, 1)

            def maxima(m):
                pr, tt, i = STEPS[m]
                n = P * (tt + 1)
                ve.wait_ge(s_ready, m + 1)
                if m >= 4:
                    ve.wait_ge(t_filled, T_AT["p", m - 4, STEPS[m - 4][1]] + 1)
                for a in range(2):
                    h = (2 * pr + a) * HG + i
                    for br in range(2):
                        v.tensor_tensor_reduce(prob[:, m % 4, 2 * a + br, 0:n], bank[2 * (m % 2) + a][:, br * n:(br + 1) * n],
                                               bias[:, h, 2 * P - n:2 * P], 1.0, HUGE, ALU.add, ALU.min,
                                               negmax[:, m % 4, 2 * a + br:2 * a + br + 1]).then_inc(max_ready, 1)

            def weights(m):
                pr, tt, i = STEPS[m]
                ve.wait_ge(exp_ready, 4 * m + 4)
                link(v.reciprocal(recip[:, m % 4, :], den[:, m % 4, :]))
                gt = gates[:, tt, H:3 * H].rearrange("p (b r a i) -> p r i a b", b=2, r=NP, a=2)[:, pr, i]
                v.tensor_tensor(weight[:, m % 4, :].rearrange("p (a b) -> p a b", a=2), recip[:, m % 4, :].rearrange("p (a b) -> p a b", a=2),
                                gt, ALU.mult).then_inc(weight_ready, 1)

            def take_p(m):
                pr, tt, i = STEPS[m]
                if pr > 0 and i == 0:
                    ve.wait_ge(pv_done, tt + 1)
                if tt == 0:
                    b = t_bank("p", m, 0)
                    v.tensor_copy(pt[0][:, :, :, 0, i * P:(i + 1) * P], b[:, :].rearrange("p (a b n) -> p a b n", a=2, b=2)).then_inc(t_drained, 1)
                else:
                    for a in range(2):
                        b = t_bank("p", m, a)
                        v.tensor_copy(pt[1][:, a, :, :, i * P:(i + 1) * P], b[:, :].rearrange("p (b k n) -> p b k n", b=2, k=2)).then_inc(t_drained, 1)

            def take_pc(pr, tt):
                if pr * TT + tt > 0:
                    ve.wait_ge(pv_done, pr * TT + tt)
                for a in range(2):
                    b = t_bank("pc", pr, tt, a)
                    v.tensor_copy(pcT[:, a, :], b[0:NC, :]).then_inc(t_drained, 1)

            def o_rest(n):
                pr, tt = n // TT, n % TT
                ve.wait_ge(ohi_ready, n + 1)
                v.tensor_tensor(o_lo[:, tt, HG * pr:HG * pr + HG, :], bank[6][:, :].rearrange("p (i n) -> p i n", i=HG),
                                o_hi[:, tt, HG * pr:HG * pr + HG, :].bitcast(F32), ALU.subtract).then_inc(o_ready, 1)

            c_scores(0)
            ahead = {0: 22, 1: 23, 2: 24, 3: 25, 5: 26, 6: 27}
            for m in range(NS + LAG):
                if m == 5:
                    for tt in range(TT):
                        head_scale("q1", tt, q_nat[:, tt, :], 6 + tt, 2 * HG)
                if m == Q1_STEP:
                    queries(1)
                if m == NS // 2:
                    c_scores(1)
                if m < NS:
                    maxima(m)
                if m in (0, NS // 2):
                    c_weights(0 if m == 0 else 1)
                if 1 <= m <= NS:
                    weights(m - 1)
                if m == 4:
                    for tt in range(TT):
                        head_sums("q1", tt, 2 * HG)
                if m == GROUP1_OUT:
                    for nb in range(NB):
                        b = t_bank("gm", nb)
                        v.tensor_copy(gm_b[:, nb * 512:nb * 512 + 512], b[:, :]).then_inc(t_drained, 1)
                    b = t_bank("shf")
                    v.tensor_copy(cols[:, SH_FFN, :], b[:, 0:KD]).then_inc(t_drained, 1)
                if m in ahead:
                    lo(ahead[m])
                if m >= LAG:
                    pr, tt, i = STEPS[m - LAG]
                    take_p(m - LAG)
                    if i == HG - 1:
                        take_pc(pr, tt)
                if m > LAG and (m - LAG) % HG == 0:
                    o_rest((m - LAG) // HG - 1)
                if m == GROUP1[-1] + 1:
                    rows_of(1, 7)
            for n in (28, 29):
                lo(n)
            o_rest(NP * TT - 1)
            rows_of(2, 7)
            b = t_bank("scf")
            link(v.scalar_tensor_tensor(out=cols[:, SC_FFN, :], in0=b[:, 0:KD], scalar=1.0, in1=cols[:, W_FFN, :], op0=ALU.add, op1=ALU.mult))
            v.tensor_copy(cols[:, C_IN, :], b[:, 0:KD]).then_inc(t_drained, 1)
            for nb in range(NB):
                b = t_bank("gf", nb)
                v.tensor_copy(gf_b[:, nb * 512:nb * 512 + 512], b[:, :]).then_inc(t_drained, 1)
            for what in FIRST_BLOCK:
                lo_ffn(0, what)

            for tt in range(TT):
                ve.wait_ge(y_done, 1) if tt == 0 else ve.wait_ge(used, FFN0)
                for nb in range(NB):
                    link(v.tensor_tensor(mixed[:, nb, :], bank[tt * NB + nb][:, :], gm_b[:, nb * 512:nb * 512 + 512], ALU.mult))
                    last = v.tensor_tensor(x_sb[:, tt, nb * 512:nb * 512 + 512], x_sb[:, tt, nb * 512:nb * 512 + 512], mixed[:, nb, :], ALU.add)
                link(last)
                link(v.tensor_tensor_reduce(xn[:, tt, :], x_sb[:, tt, :], x_sb[:, tt, :], 1.0, 0.0, ALU.mult, ALU.add,
                                            sums[:, ROOT["x2", tt], 0:1]))
                mean_eps(("x2", tt), 1, D)
                ve.wait_ge(root_ready, ROOT["x2", tt] + 1)
                v.tensor_scalar(xn[:, tt, :], x_sb[:, tt, :], roots[:, ROOT["x2", tt], 0:1], None, ALU.mult).then_inc(xn2_ready, 1)
            for i in range(4):
                tt, half = i // 2, i % 2
                ve.wait_ge(xn2T, i + 1)
                for k in range(4 * half, 4 * half + 4):
                    last = v.tensor_scalar(h_f[:, k, tt * P:(tt + 1) * P], bank[4 + i][:, (k % 4) * P:(k % 4 + 1) * P],
                                           cols[:, SC_FFN, k:k + 1], cols[:, SH_FFN, k:k + 1], ALU.mult, ALU.add)
                last.then_inc(h2f_ready, 1)
            for i in range(4):
                tt, half = i // 2, i % 2
                ve.wait_ge(h2hi_ready, i + 1)
                ks, ts = slice(4 * half, 4 * half + 4), slice(tt * P, (tt + 1) * P)
                v.tensor_tensor(h_lo[:, ks, ts], h_f[:, ks, ts], h_hi[:, ks, ts].bitcast(F32), ALU.subtract).then_inc(h2_ready, 1)

            def dve_gate(j, f):
                ve.wait_ge(th_ready, 2 * j + f + 1)
                v.scalar_tensor_tensor(out=sg[:, f, :], in0=th[:, f, :], scalar=1.0, in1=bank[4 + f][:, 0:256],
                                       op0=ALU.add, op1=ALU.mult).then_inc(dve, 1)
                ve.wait_ge(dve, n_dve[0] + 2 * j + f + 1)
                v.scalar_tensor_tensor(out=act_f[:, f, :], in0=sg[:, f, :], scalar=0.5, in1=bank[4 + f][:, 256:512],
                                       op0=ALU.mult, op1=ALU.mult).then_inc(act_ready, 1)
                ve.wait_ge(ahi_ready, 2 * j + f + 1)
                v.tensor_tensor(act_lo[:, f, :], act_f[:, f, :], act_hi[:, f, :].bitcast(F32), ALU.subtract).then_inc(a_ready, 1)

            dve_gate(0, 0)
            for what in ("G0", "U0"):
                lo_ffn(1, what)
            dve_gate(0, 1)
            lo_ffn(1, "D1")

            def dve_block(j):
                for what in ("G1", "U1", "D0"):
                    lo_ffn(j, what)
                dve_gate(j, 0)
                for what in ("G0", "U0"):
                    lo_ffn(j + 1, what)
                dve_gate(j, 1)
                lo_ffn(j + 1, "D1")

            for j in range(1, NJ - 1):
                dve_block(j)
            j = NJ - 1
            for what in ("G1", "U1", "D0"):
                lo_ffn(j, what)
            dve_gate(j, 0)
            dve_gate(j, 1)
            lo_ffn(NJ, "D1")
            n_dve[0] += 2 * NJ
            for tt in range(TT):
                ve.wait_ge(y2_done, 1) if tt == 0 else ve.wait_ge(used, half_at(NJ, "D1") + 1)
                for nb in range(NB):
                    link(v.tensor_tensor(mixed[:, nb, :], bank[tt * NB + nb][:, :], gf_b[:, nb * 512:nb * 512 + 512], ALU.mult))
                    v.tensor_tensor(out_sb[:, tt, nb * 512:nb * 512 + 512], x_sb[:, tt, nb * 512:nb * 512 + 512], mixed[:, nb, :],
                                    ALU.add).then_inc(out_ready, 1)

        @block.tensor
        def _(pe):
            t = nc.tensor

            def mm3(dst, l_hi, l_lo, r_hi, r_lo, start, stop):
                t.matmul(dst, l_hi, r_hi, start=start, stop=False, skip_group_check=True)
                t.matmul(dst, l_hi, r_lo, start=False, stop=False, skip_group_check=True)
                return t.matmul(dst, l_lo, r_hi, start=False, stop=stop, skip_group_check=True)

            pe.wait_ge(consts, 1)
            pe.wait_ge(norm_in, 32)
            pe.wait_ge(qk_in, 32)
            pe.wait_ge(pos_in, 32)
            for a in range(2):
                t.transpose(bank[5][:, 8 * a:8 * a + 8], norm_nat[:, a, :], ident[0:8, 0:8])
            t.transpose(bank[5][:, 16:20], qk_nat[:].rearrange("p a d -> p (a d)"), ident[0:4, 0:4])
            t.transpose(bank[5][:, 32:64], pos_nat[:].rearrange("p a d -> p (a d)"), ident[0:2 * STRIDE, 0:2 * STRIDE]).then_inc(params_t, 1)
            pe.wait_ge(c_ready, 1)
            for k in range(KD):
                if k == 4:
                    pe.wait_ge(xn_ready, TT)
                    for kk in range(KD):
                        for tt in range(TT):
                            last = t.transpose(bank[kk // 2][:, (kk % 2) * 256 + tt * P:(kk % 2) * 256 + (tt + 1) * P],
                                               xn[:, tt, kk * P:(kk + 1) * P], ident[:, :])
                        if kk % 2:
                            last.then_inc(xnT, 1)
                pe.wait_ge(ada_in[k % 3], 16 * (k // 3 + 1))
                for j in range(4):
                    last = t.matmul(bank[4][32 * j:32 * j + 32, :], c_rep[:, k, :], ada_e[k % 3][:, j, :], start=(k == 0), stop=(k == KD - 1))
                last.then_inc(ada_used, 1)

            n_cols = [0]

            def columns(dst, j0, n):
                for kk in range(n):
                    j = j0 + kk // 4
                    last = t.matmul(dst[:, kk:kk + 1], rows[32 * j:32 * j + 1, (kk % 4) * P:(kk % 4 + 1) * P], ones[32 * j:32 * j + 1, 0:1],
                                    start=True, stop=True)
                    if kk % 4 == 3 and kk < n - 1:
                        n_cols[0] += 1
                        last.then_inc(col_turn, 1)
                        pe.wait_ge(col_turn, n_cols[0])
                return last

            pe.wait_ge(rows_ready, 1)
            columns(bank[5][:, 64:80], 0, 16).then_inc(mix_cols, 1)

            def project(name, bk, halves=None):
                for hh in (range(4) if halves is None else halves):
                    n = START[name] + hh
                    pe.wait_ge(lo_done, n + 1)
                    if name == "c":
                        pe.wait_ge(h_ready, hh + 1)
                    for kk in range(2):
                        k = 2 * hh + kk
                        w = slice(kk * 512, kk * 512 + 512)
                        for tt in range(TT):
                            last = mm3(bank[bk + tt][:, :], h_hi[:, k, tt * P:(tt + 1) * P], h_lo[:, k, tt * P:(tt + 1) * P],
                                       w_hi[:, n % NRING, w], w_lo[:, n % NRING, w], k == 0, k == KD - 1)
                    last.then_inc(used, 1)

            def t_bank(*use):
                n = T_AT[use]
                if n >= 2:
                    pe.wait_ge(t_drained, n - 1)
                return bank[4 + n % 2]

            project("c", 6)
            project("s", 0)
            for tt in range(TT):
                for kv in range(2):
                    b = t_bank("c", tt, kv)
                    pe.wait_ge(copied, tt + 1)
                    for g in range(G):
                        last = t.transpose(b[:, g * P:(g + 1) * P], kcv[:, tt, kv * G + g].rearrange("p a d -> p (a d)"), ident[:, :])
                    last.then_inc(t_filled, 1)
            project("w", 2)
            b = t_bank("hid")
            pe.wait_ge(cw1_in, 64)
            pe.wait_ge(t_drained, T_AT["c", 1, 1] + 1)
            for kv in range(2):
                for l in range(STRIDE):
                    last = t.matmul(b[:, kv * 64:kv * 64 + G * NC], cw1[:, kv, l, :], blocks[:, kv, l, :], start=(l == 0), stop=(l == STRIDE - 1))
            last.then_inc(t_filled, 1)
            for hh in range(2):
                n = START["gates"] + hh
                pe.wait_ge(lo_done, n + 1)
                pe.wait_ge(copied, 2)
                for kk in range(4):
                    k = 4 * hh + kk
                    w = slice(kk * 3 * H, (kk + 1) * 3 * H)
                    for tt in range(TT):
                        last = mm3(bank[6 + tt][:, 0:3 * H], h_hi[:, k, tt * P:(tt + 1) * P], h_lo[:, k, tt * P:(tt + 1) * P],
                                   w_hi[:, n % NRING, w], w_lo[:, n % NRING, w], k == 0, k == KD - 1)
                last.then_inc(used, 1)
            for tt in range(TT):
                b = t_bank("k", tt)
                pe.wait_ge(scaled, 3 + tt)
                for br in range(2):
                    for pr in range(NP):
                        last = t.transpose(b[:, (br * NP + pr) * P:(br * NP + pr + 1) * P], k_nat[:, tt, br, pr * P:(pr + 1) * P], ident[:, :])
                last.then_inc(t_filled, 1)
            pe.wait_ge(copied, 4)
            project("q0", 0)
            b = t_bank("cw2")
            pe.wait_ge(t_drained, T_AT["hid",] + 1)
            pe.wait_ge(cw2_in, 16)
            t.matmul(b[0:G * NC, 0:DK], gel[:, 0, :], cw2[:, 0, :], start=True, stop=True)
            for g in range(G):
                last = t.matmul(b[0:NC, DK + g * DK:DK + (g + 1) * DK], gel[:, 1, g * NC:(g + 1) * NC], cw2[:, 1, :], start=True, stop=True)
            last.then_inc(t_filled, 1)
            b = t_bank("kc")
            pe.wait_ge(t_drained, T_AT["cw2",] + 1)
            t.transpose(b[:, 0:G * NC], kc_nat[:].rearrange("p a d -> p (a d)"), ident[0:G * NC, 0:G * NC]).then_inc(t_filled, 1)

            def queries(pr):
                for tt in range(TT):
                    b = t_bank("q", pr, tt)
                    pe.wait_ge(scaled, 5 + 2 * pr + tt)
                    for i in range(HG):
                        last = t.transpose(b[:, i * P:(i + 1) * P], q_nat[:, tt, i * P:(i + 1) * P], ident[:, :])
                    last.then_inc(t_filled, 1)

            def c_scores(pr):
                for a in range(2):
                    b = t_bank("cs", pr, a)
                    pe.wait_ge(t_drained, T_AT["q", pr, 1] + 1)
                    for tt in range(TT):
                        for i in range(HG):
                            gc = (2 * pr + a) * NC
                            o = (tt * HG + i) * NC
                            last = t.matmul(b[:, o:o + NC], qT[64 * a:64 * a + 64, pr, tt, i, :], kcT[64 * a:64 * a + 64, gc:gc + NC],
                                            start=True, stop=True)
                    last.then_inc(t_filled, 1)

            def scores(m):
                pr, tt, i = STEPS[m]
                n = P * (tt + 1)
                if m >= 2:
                    pe.wait_ge(max_ready, 4 * (m - 1))
                for a in range(2):
                    last = t.matmul(bank[2 * (m % 2) + a][:, 0:2 * n].rearrange("p (b n) -> p b n", b=2), qT[64 * a:64 * a + 64, pr, tt, i, :],
                                    kT[64 * a:64 * a + 64, pr, :, 0:n], start=True, stop=True)
                last.then_inc(s_ready, 1)

            def turn(m):
                pr, tt, i = STEPS[m]
                pe.wait_ge(p_ready, m + 1)
                for bk in range(tt + 1):
                    b = t_bank("p", m, bk)
                    for q in range(4):
                        ab, kt = (q, 0) if tt == 0 else (2 * bk + q // 2, q % 2)
                        last = t.transpose(b[:, q * P:(q + 1) * P], prob[:, m % 4, ab, kt * P:(kt + 1) * P], ident[:, :])
                    last.then_inc(t_filled, 1)

            def turn_c(pr, tt):
                pe.wait_ge(cp_ready, pr + 1)
                for a in range(2):
                    b = t_bank("pc", pr, tt, a)
                    for i in range(HG):
                        last = t.transpose(b[0:NC, i * P:(i + 1) * P], cprob[:, pr, (a * TT + tt) * HG + i, :], ident[:, :])
                    last.then_inc(t_filled, 1)

            def values(pr, tt):
                n = pr * TT + tt
                if n == 0:
                    pe.wait_ge(scaled, 7)
                else:
                    pe.wait_ge(o_ready, n)
                pe.wait_ge(t_drained, T_AT["pc", pr, tt, 1] + 1)
                for br in range(2):
                    for kt in range(tt + 1):
                        for a in range(2):
                            gc = (2 * pr + a) * DK
                            t.matmul(bank[6][64 * a:64 * a + 64, :], v_nat[:, kt, br, gc:gc + DK], pt[tt][:, a, br, kt, :],
                                     start=(br == 0 and kt == 0), stop=False)
                for a in range(2):
                    last = t.matmul(bank[6][64 * a:64 * a + 64, :], vc[:, 2 * pr + a, :], pcT[:, a, :], start=False, stop=True)
                last.then_inc(pv_done, 1)

            def late(q):
                h, k = q // 8 % 2, q % 8
                pe.wait_ge(late_in[q % NLATE], 16 * (q // NLATE + 1))
                for j in range(4):
                    last = t.matmul(bank[7][32 * j:32 * j + 32, 256 * h:256 * h + 256], c_rep[:, k, :], ada_l[q % NLATE][:, j, :],
                                    start=(k == 0), stop=(k == KD - 1))
                last.then_inc(late_used, 1)

            def attention_out(ck):
                n = START["out"] + ck
                pe.wait_ge(lo_done, n + 1)
                pe.wait_ge(o_ready, TT * (ck // HG + 1))
                if ck == 0:
                    pe.wait_ge(max_ready, 4 * NS)
                for tt in range(TT):
                    for nb in range(NB):
                        w = slice(nb * 512, nb * 512 + 512)
                        last = mm3(bank[tt * NB + nb][:, :], o_hi[:, tt, ck, :], o_lo[:, tt, ck, :], w_hi[:, n % NRING, w], w_lo[:, n % NRING, w],
                                   ck == 0, ck == KD - 1)
                    if ck == KD - 1 and tt == 0:
                        last.then_inc(y_done, 1)
                last.then_inc(used, 1)

            queries(0)
            c_scores(0)
            for m in range(NS + LAG):
                if m == Q1_STEP:
                    queries(1)
                if m == NS // 2:
                    c_scores(1)
                if m == 0:
                    pe.wait_ge(scaled, 6)
                if m < NS:
                    scores(m)
                if m < 4:
                    if m == 0:
                        pe.wait_ge(copied, 8)
                    project("q1", 6, [m])
                if m in GROUP1:
                    if m == GROUP1[0]:
                        pe.wait_ge(scaled, 8)
                    for q in range(4 * (m - GROUP1[0]), 4 * (m - GROUP1[0]) + 4):
                        late(q)
                if m in GROUP2:
                    if m == GROUP2[0]:
                        pe.wait_ge(rows_ready, 2)
                    for q in range(16 + 4 * (m - GROUP2[0]), 20 + 4 * (m - GROUP2[0])):
                        late(q)
                if m == GROUP1_OUT:
                    pe.wait_ge(rows_ready, 2)
                    for nb in range(NB):
                        b = t_bank("gm", nb)
                        t.matmul(b[:, :], ones[32 * nb:32 * nb + 1, :], rows[32 * nb:32 * nb + 1, :], start=True, stop=True).then_inc(t_filled, 1)
                    b = t_bank("shf")
                    columns(b, 2, KD).then_inc(t_filled, 1)
                if m >= LAG:
                    pr, tt, i = STEPS[m - LAG]
                    turn(m - LAG)
                    if i == HG - 1:
                        turn_c(pr, tt)
                        values(pr, tt)
            for ck in range(HG):
                attention_out(ck)
            pe.wait_ge(rows_ready, 3)
            b = t_bank("scf")
            columns(b, 0, KD).then_inc(t_filled, 1)
            for nb in range(NB):
                b = t_bank("gf", nb)
                j = 2 + nb
                t.matmul(b[:, :], ones[32 * j:32 * j + 1, :], rows[32 * j:32 * j + 1, :], start=True, stop=True).then_inc(t_filled, 1)
            for ck in range(HG, KD):
                attention_out(ck)

            for i in range(4):
                tt, half = i // 2, i % 2
                pe.wait_ge(xn2_ready, tt + 1)
                if i == 0:
                    pe.wait_ge(t_drained, len(T_AT))
                for k in range(4):
                    last = t.transpose(bank[4 + i][:, k * P:(k + 1) * P], xn[:, tt, (4 * half + k) * P:(4 * half + k + 1) * P], ident[:, :])
                last.then_inc(xn2T, 1)

            def gate_up(j, what):
                f = int(what[1])
                r = slot_of(j, what)
                pe.wait_ge(lo_done, half_at(j, what) + 1)
                col = 0 if what[0] == "G" else 256
                w = [tensor[:, r, :].rearrange("p (k n) -> p k n", n=P) for tensor in (w_hi, w_lo)]
                for k in range(KD):
                    last = mm3(bank[4 + f][:, col:col + SEQ], w[0][:, k, :], w[1][:, k, :], h_hi[:, k, :], h_lo[:, k, :], k == 0, k == KD - 1)
                last.then_inc(used, 1)

            def down(j, what, first=False, final=False):
                f = int(what[1])
                r = slot_of(j, what)
                pe.wait_ge(lo_done, half_at(j, what) + 1)
                pe.wait_ge(a_ready, 2 * owner(j, what) + f + 1)
                for tt in range(TT):
                    for nb in range(NB):
                        w = slice(nb * 512, nb * 512 + 512)
                        last = mm3(bank[tt * NB + nb][:, :], act_hi[:, f, tt * P:(tt + 1) * P], act_lo[:, f, tt * P:(tt + 1) * P],
                                   w_hi[:, r, w], w_lo[:, r, w], first, final)
                    if final and tt == 0:
                        last.then_inc(y2_done, 1)
                last.then_inc(used, 1)

            def up_block(j, first=False):
                for what in (FIRST_BLOCK if first else BLOCK):
                    if what[0] == "D":
                        down(j, what, first=first)
                    else:
                        if what[0] == "G":
                            if not first:
                                pe.wait_ge(act_ready, 2 * j + int(what[1]) - 1)
                        gate_up(j, what)

            pe.wait_ge(h2_ready, 4)
            up_block(0, first=True)
            for j in range(1, NJ):
                up_block(j)
            down(NJ, "D1", final=True)


_INS = ["x", "c", "ada_w", "ada_b", "norm_mix_w", "norm_ffn_w", "ffn_w_gate", "ffn_w_up", "ffn_w_down",
        "nsa_w_in", "nsa_cmp_pos", "nsa_cmp_w1", "nsa_cmp_w2", "nsa_qk_norm", "nsa_w_out"]


def kernel(**inputs):
    import numpy as _np
    import concourse.bacc as _bacc
    from concourse import mybir as _mybir
    from concourse.bass_utils import run_bass_kernel_spmd as _run

    nc = _bacc.Bacc("TRN2", target_bir_lowering=False, num_devices=1)
    arrays, args = {}, []
    for name in _INS:
        a = _np.ascontiguousarray(inputs[name])
        arrays[f"in_{name}"] = a
        args.append(nc.dram_tensor(f"in_{name}", a.shape, _mybir.dt.from_np(a.dtype), kind="ExternalInput").ap())
    args.append(nc.dram_tensor("out_0", inputs["x"].shape, _mybir.dt.float32, kind="ExternalOutput").ap())
    trunk_kernel(nc, *args)
    r = _run(nc, [arrays], core_ids=[0])
    return r.results[0]["out_0"]
```

```python
from contextlib import ExitStack

import concourse.bass as bass
from concourse import mybir

F32 = mybir.dt.float32
F32R = mybir.dt.float32r
ALU = mybir.AluOpType
ACT = mybir.ActivationFunctionType
AX_X = mybir.AxisListType.X

P = 128
MASKED = 1e30
HUGE = 3e38
EPS = 1e-6
GELU_C = 0.7978845608028654
GELU_A = 0.044715


def spread(ap, axis, n):
    ap = ap.unsqueeze(axis)
    shape = list(ap.shape)
    shape[axis] = n
    return ap.to_broadcast(shape)


def trunk_kernel(nc, x, c, ada_w, ada_b, norm_mix_w, norm_ffn_w, w_gate, w_up, w_down,
                 w_in, cmp_pos, cmp_w1, cmp_w2, qk_norm, w_out, out):
    _, SEQ, D = x.shape
    F = w_gate.shape[2]
    DK = qk_norm.shape[2]
    H = w_out.shape[1] // DK
    G = (w_in.shape[2] - H * DK - 3 * H) // (6 * DK)
    HG = H // G
    L = cmp_pos.shape[2]
    STRIDE = L // 2
    NC = (SEQ - L) // STRIDE + 1
    TT = SEQ // P
    KD = D // P
    NP = G // 2
    QD, KV = H * DK, G * DK
    NB = D // 512
    NJ = F // 256
    SCALE = float(DK) ** -0.5
    assert TT == 2 and KD == 8 and NP == 2 and DK == 64 and HG == 4 and L == 32 and F == NJ * 256

    HALF = 1024
    NRAW, NRING = 3, 6
    START = {"c": 0, "s": 4, "w": 8, "gates": 12, "q0": 14, "q1": 18, "out": 22}
    FFN0 = START["out"] + KD
    COLUMN = {"q0": 0, "q1": NP * HG * DK, "c": QD, "s": QD + 2 * KV, "w": QD + 4 * KV, "gates": QD + 6 * KV}
    NAT = {("s", 0): 0, ("s", 1): 1, ("w", 0): 2, ("w", 1): 3, ("q0", 0): 4, ("q0", 1): 5, ("q1", 0): 6, ("q1", 1): 7}
    ROOT = {use: n for n, use in enumerate(
        ["x", ("s", 0), ("s", 1), ("w", 0), ("w", 1), "kc", ("q0", 0), ("q0", 1), ("q1", 0), ("q1", 1),
         ("x2", 0), ("x2", 1)])}
    FIRST_BLOCK = ["G0", "U0", "G1", "U1", "D0"]
    BLOCK = ["G0", "U0", "D1", "G1", "U1", "D0"]

    def half_at(j, what):
        if isinstance(j, int) and j == 0:
            return FFN0 + FIRST_BLOCK.index(what)
        return FFN0 + 5 + 6 * (j - 1) + (0 if isinstance(j, int) and j == NJ else BLOCK.index(what))

    def slot_of(j, what):
        if isinstance(j, int):
            return half_at(j, what) % NRING
        return (FFN0 + 5 + BLOCK.index(what)) % NRING

    STEPS = [(pr, tt, i) for pr in range(NP) for tt in range(TT) for i in range(HG)]
    NS = len(STEPS)
    LAG = 3
    Q1_STEP = 6
    Q1_AT = {0: 2, 1: 3}
    C_STEP = (1, NS // 2 + 1)
    LATE_BEHIND = {}
    for n, q in zip(range(START["s"], START["gates"]), ((0,), (1, 2), (3,), (4, 5), (6,), (7, 8), (9,), (10,))):
        LATE_BEHIND[n] = q
    for n, q in zip(range(START["q0"], START["q1"]), ((11, 12), (13,), (14,), (15,))):
        LATE_BEHIND[n] = q
    LATE_STEP = {m: range(16 + 2 * (m - 6), 18 + 2 * (m - 6)) for m in range(6, 14)}
    order = [("c", tt, kv) for tt in range(TT) for kv in range(2)]
    order += [("hid",), ("gates",), ("k", 0), ("k", 1), ("cw2",), ("kc",), ("q", 0, 0), ("q", 0, 1)]
    for m in range(NS + LAG):
        if m == Q1_STEP:
            order += [("q", 1, 0), ("q", 1, 1)]
        if m in C_STEP:
            order += [("cs", C_STEP.index(m))]
        if m >= LAG:
            pr, tt, i = STEPS[m - LAG]
            order += [("p", m - LAG, b) for b in range(tt + 1)]
            if i == HG - 1:
                order += [("pc", pr, tt, a) for a in range(2)]
    order += [("gm", 0), ("gm", 1), ("shf",), ("scf",), ("gf", 0), ("gf", 1)]
    T_AT = {use: n for n, use in enumerate(order)}

    with ExitStack() as ctx:
        def sem(name):
            return ctx.enter_context(nc.semaphore(name))

        base = (nc.sbuf_base + 31) // 32 * 32
        here = [base]

        def sized(shape):
            n = 4
            for s in shape[1:]:
                n *= s
            return (n + 31) // 32 * 32

        def at(name, shape, offset, dt=F32):
            return nc.alloc_sbuf_tensor_at(name, shape, dt, offset=offset)

        def sb(name, shape, dt=F32):
            offset = here[0]
            here[0] += sized(shape)
            return at(name, shape, offset, dt)

        def region(nbytes):
            offset = here[0]
            here[0] += nbytes
            return offset

        x_sb = sb("x_sb", [P, TT, D])
        raw = sb("raw", [P, NRAW, 2 * HALF])
        w_hi = sb("w_hi", [P, NRING, HALF], F32R)
        w_lo = sb("w_lo", [P, NRING, HALF], F32R)
        r_h = region(16384)
        h_hi = at("h_hi", [P, KD, SEQ], r_h, F32R)
        h_lo = at("h_lo", [P, KD, SEQ], r_h + 8192, F32R)
        pcT = at("pcT", [NC, 2, HG * P], r_h + 12288)
        ident = sb("ident", [P, P])
        ones = sb("ones", [P, P])
        W_MIX, W_FFN, SC_MIX, SH_MIX, SC_FFN, SH_FFN, C_IN, C_ACT = range(8)
        cols = sb("cols", [P, 8, KD])
        c_rep = sb("c_rep", [P, KD, 32])
        rows = sb("rows", [P, 2, 512])
        ada_bias = sb("ada_bias", [P, 512])
        sums = sb("sums", [P, 12, 8])
        roots = sb("roots", [P, 12, 8])
        minus_half = sb("minus_half", [P, 8])
        cw2 = sb("cw2", [P, 2, DK])
        qk_col = sb("qk_col", [P, 4])
        pos_col = sb("pos_col", [P, 2, STRIDE])
        norm_nat = sb("norm_nat", [8, 2, P])
        gates = sb("gates", [P, TT, 3 * H])
        den = sb("den", [P, 4, 4])
        recip = sb("recip", [P, 4, 4])
        weight = sb("weight", [P, 4, 4])
        negmax = sb("negmax", [P, 4, 4])
        qk_nat = sb("qk_nat", [4, 2, DK])
        pos_nat = sb("pos_nat", [2 * STRIDE, 2, DK])
        gel = sb("gel", [P, 2, 60])
        gel_t = sb("gel_t", [P, 2, 60])
        kcT = sb("kcT", [P, NP, 2, NC])
        kc_nat = sb("kc_nat", [G * NC, 2, DK])
        vc = sb("vc", [NC, G, DK])
        cmask = sb("cmask", [P, TT * HG, NC])
        cbias = sb("cbias", [P, NP, 2, TT * HG, NC])
        cprob = sb("cprob", [P, NP, 2 * TT * HG, NC])
        cstat = sb("cstat", [P, 4, 2 * TT * HG])
        cdist = sb("cdist", [P, TT, NC])
        kT = sb("kT", [P, NP, 2, SEQ])
        v_nat = sb("v_nat", [P, TT, 2, KV])

        r_q = region(4096)
        q_nat = at("q_nat", [P, TT, 512], r_q)
        gates_t = at("gates_t", [3 * H, SEQ], r_q)
        gm_b = at("gm_b", [P, D], r_q)
        r_qT = region(8192)
        qT = at("qT", [P, NP, TT, HG, P], r_qT)
        r_bias = region(16384)
        bias = at("bias", [P, H, 2 * P], r_bias)
        gf_b = at("gf_b", [P, D], r_bias)
        r_o = region(16384)
        o_hi = at("o_hi", [P, TT, KD, P], r_o, F32R)
        o_lo = at("o_lo", [P, TT, KD, P], r_o + 8192, F32R)
        sq = at("sq", [P, 2, 512], r_o)
        kcv = at("kcv", [P, TT, 2 * G, 2, DK], r_o + 8192)
        k_nat = at("k_nat", [P, TT, 2, KV], r_o + 4096)
        out_sb = at("out_sb", [P, TT, D], r_o + 8192)
        r_p = region(16384)
        prob = at("prob", [P, 4, 4, 2 * P], r_p)
        xn = at("xn", [P, TT, D], r_p)
        h_f = at("h_f", [P, KD, SEQ], r_p + 8192)
        NLATE = (4, 3)
        ada_l = [[at(f"ada_late{g}_{i}", [P, 4, 256], (r_p, r_h)[g] + 4096 * i) for i in range(NLATE[g])] for g in range(2)]
        r_pt = region(24576)
        cw1 = at("cw1", [P, 2, STRIDE, P], r_pt)
        blocks = at("blocks", [P, 2, STRIDE, G * NC], r_pt + 16384)
        pt = [at("pt0", [P, 2, 2, 1, HG * P], r_pt + 16384), at("pt1", [P, 2, 2, 2, HG * P], r_pt)]
        ada_e = [at(f"ada_e{k}", [P, 4, 512], offset) for k, offset in enumerate(
            [r_bias, r_bias + 8192, r_o, r_o + 8192, r_qT, r_pt, r_pt + 8192, r_pt + 16384])]
        th = at("th", [P, 2, 256], r_pt)
        sg = at("sg", [P, 2, 256], r_pt + 2048)
        act_f = at("act_f", [P, 2, 256], r_pt + 4096)
        act_hi = at("act_hi", [P, 2, 256], r_pt + 6144, F32R)
        act_lo = at("act_lo", [P, 2, 256], r_pt + 8192, F32R)
        mixed = at("mixed", [P, 2, 512], r_pt + 10240)
        assert here[0] <= nc.sbuf_usable_end, here[0]

        bank = [ctx.enter_context(nc.psum_tensor(f"bank{i}", [P, 512], F32)) for i in range(8)]

        x_in = [sem(f"x_in{t}") for t in range(TT)]
        c_in, norm_in, qk_in, pos_in, cw2_in, cw1_in = (sem(n) for n in ("c_in", "norm_in", "qk_in", "pos_in", "cw2_in", "cw1_in"))
        bias_in = [sem(f"bias_in{g}") for g in range(3)]
        ada_in = [sem(f"ada_in{k}") for k in range(KD)]
        late_in = [[sem(f"late_in{g}_{i}") for i in range(NLATE[g])] for g in range(2)]
        raw_in = [sem(f"raw_in{i}") for i in range(NRAW)]
        hi_done, lo_done, used = sem("hi_done"), sem("lo_done"), sem("used")
        consts = sem("consts")
        bias_ready = sem("bias_ready")
        dve = sem("dve")
        own = sem("own")
        pool = sem("pool")
        c_tanh, c_ready, sq_x = sem("c_tanh"), sem("c_ready"), sem("sq_x")
        params_t, cols_ready = sem("params_t"), sem("cols_ready")
        x2_ready, x2_squared, xn2_act = sem("x2_ready"), sem("x2_squared"), sem("xn2_act")
        var_ready, root_ready = sem("var_ready"), sem("root_ready")
        xn_ready, xnT, gates_done = sem("xn_ready"), sem("xnT"), sem("gates_done")
        ada_used, rows_ready, mix_cols = sem("ada_used"), sem("rows_ready"), sem("mix_cols")
        hf_ready, hhi_ready, h_ready = sem("hf_ready"), sem("hhi_ready"), sem("h_ready")
        copied, squared, scaled = sem("copied"), sem("squared"), sem("scaled")
        gates_ready = sem("gates_ready")
        t_filled, t_drained = sem("t_filled"), sem("t_drained")
        gel_sq, gel_in, gel_tanh, gel_ready, kc_sum, kc_ready = (sem(n) for n in ("gel_sq", "gel_in", "gel_tanh", "gel_ready", "kc_sum", "kc_ready"))
        s_ready, max_ready, exp_ready, weight_ready, p_ready = (sem(n) for n in ("s_ready", "max_ready", "exp_ready", "weight_ready", "p_ready"))
        cs_ready, ce_ready, cp_ready = sem("cs_ready"), sem("ce_ready"), sem("cp_ready")
        pv_done, ohi_ready, o_ready = sem("pv_done"), sem("ohi_ready"), sem("o_ready")
        late_used = sem("late_used")
        y_done = sem("y_done")
        xn2_ready, xn2T, h2f_ready, h2hi_ready, h2_ready = (sem(n) for n in ("xn2_ready", "xn2T", "h2f_ready", "h2hi_ready", "h2_ready"))
        th_ready, act_ready, ahi_ready, a_ready = (sem(n) for n in ("th_ready", "act_ready", "ahi_ready", "a_ready"))
        y2_done, out_ready, out_done = sem("y2_done"), sem("out_ready"), sem("out_done")

        def unit_of(n):
            return n // 2

        def raw_half(n, width=HALF):
            return raw[:, unit_of(n) % NRAW, (n % 2) * width:(n % 2 + 1) * width]

        def raw_ffn(what):
            slot = (START["out"] + KD) // 2 % NRAW + "GUD".index(what[0])
            f = int(what[1])
            if what[0] == "D":
                return raw[:, slot % NRAW, f * HALF:(f + 1) * HALF]
            return raw[:, slot % NRAW, :].rearrange("p (k n) -> p k n", n=256)[:, :, f * P:(f + 1) * P]

        def split_parts(tensor, slot, what):
            v = tensor[:, slot, :]
            return v if what[0] == "D" else v.rearrange("p (k n) -> p k n", n=P)

        def ffn_unit(j, what):
            return (FFN0 // 2) + 3 * j + "GUD".index(what[0])

        def owner(j, what):
            return j - 1 if what == "D1" else j

        def width_of(n):
            return KD // 2 * 3 * H if START["gates"] <= n < START["q0"] else HALF

        block = ctx.enter_context(nc.Block())

        @block.sync
        def _(sp):
            sp.dma_start(cols[:, C_IN, :], c[0].rearrange("(p k) -> p k", k=KD)).then_inc(c_in, 16)
            for t in range(TT):
                sp.dma_start(x_sb[:, t, :], x[0, t * P:(t + 1) * P, :]).then_inc(x_in[t], 16)
            ada_v = ada_w[0].rearrange("(p k) n -> p k n", k=KD)

            def load(u, src, cols_of=2 * HALF, shape=None):
                dst = raw[:, u % NRAW, 0:cols_of]
                if shape:
                    dst = dst.rearrange("p (k n) -> p k n", n=shape)
                sp.dma_start(dst, src).then_inc(raw_in[u % NRAW], 16)

            def free(u):
                if u >= NRAW:
                    sp.wait_ge(lo_done, 2 * (u - NRAW) + 2)

            def small_loads(k):
                if k == 0:
                    for a, w in enumerate((norm_mix_w, norm_ffn_w)):
                        sp.dma_start(norm_nat[:, a, :], w[0].rearrange("(k p) -> k p", p=P)).then_inc(norm_in, 16)
                    for a in range(2):
                        sp.dma_start(qk_nat[:, a, :], qk_norm[0]).then_inc(qk_in, 16)
                    for kv in range(2):
                        sp.dma_start(pos_nat[STRIDE * kv:STRIDE * (kv + 1), :, :],
                                     cmp_pos[0, kv].rearrange("(a l) d -> l a d", a=2)).then_inc(pos_in, 16)
                if k == 1:
                    for j in range(4):
                        sp.dma_start(ada_bias[32 * j:32 * j + 32, :],
                                     ada_b[0:1, 512 * j:512 * j + 512].to_broadcast([32, 512])).then_inc(bias_in[0], 16)
                    sp.dma_start(cw2[:], cmp_w2[0].rearrange("v f d -> f v d")).then_inc(cw2_in, 16)

            for k in range(KD):
                small_loads(k)
                sp.dma_start(ada_e[k][:], ada_v[:, k, 0:2048].rearrange("p (j n) -> p j n", j=4)).then_inc(ada_in[k], 16)

            w_in_v = w_in[0].rearrange("(k p) n -> p k n", p=P)

            def load_in(name, part):
                u = START[name] // 2 + part
                free(u)
                if name == "gates":
                    load(u, w_in_v[:, :, COLUMN[name]:COLUMN[name] + 3 * H], KD * 3 * H, 3 * H)
                else:
                    load(u, w_in_v[:, 4 * part:4 * part + 4, COLUMN[name]:COLUMN[name] + 512], shape=512)

            def load_out(part):
                u = START["out"] // 2 + part
                free(u)
                pr, i = part // 2, 2 * (part % 2)
                v = w_out[0].rearrange("(r a i d) n -> r a d i n", r=NP, a=2, i=HG)
                for a in range(2):
                    sp.dma_start(raw[64 * a:64 * a + 64, u % NRAW, :].rearrange("p (i n) -> p i n", i=2),
                                 v[pr, a, :, i:i + 2, :]).then_inc(raw_in[u % NRAW], 8 * 2)

            def load_late(q):
                g, h, k = q // 16, q // 8 % 2, q % 8
                n, slot = q % 16, q % 16 % NLATE[g]
                if n >= NLATE[g]:
                    sp.wait_ge(late_used, q - NLATE[g] + 1)
                elif g == 0:
                    sp.wait_ge(h_ready, 4)
                else:
                    sp.wait_ge(used, START["out"])
                src = ada_v[:, k, 2048 * (g + 1):2048 * (g + 2)].rearrange("p (j n) -> p j n", j=4)[:, :, 256 * h:256 * h + 256]
                sp.dma_start(ada_l[g][slot][:], src).then_inc(late_in[g][slot], 16)

            for part in range(2):
                load_in("c", part)
            load_in("s", 0)
            w1_v = cmp_w1[0].rearrange("v (a l d) f -> v a d l f", a=2, l=STRIDE)
            sp.wait_ge(ada_used, KD)
            for kv in range(2):
                for a in range(2):
                    sp.dma_start(cw1[64 * a:64 * a + 64, kv, :, :], w1_v[kv, a]).then_inc(cw1_in, 16)
            for q in range(2):
                load_late(q)
            load_in("s", 1)
            for q in range(2, 5):
                load_late(q)
            load_in("w", 0)
            for q in range(5, 8):
                load_late(q)
            load_in("w", 1)
            for q in range(8, 10):
                load_late(q)
            load_in("gates", 0)
            load_late(10)
            load_in("q0", 0)
            for q in range(11, 14):
                load_late(q)
            load_in("q0", 1)
            for q in range(14, 16):
                load_late(q)
            for part in range(2):
                load_in("q1", part)
            for part in range(3):
                load_out(part)

            def load_ffn(j, what):
                if isinstance(j, int) and j == 0:
                    free(FFN0 // 2 + "GUD".index(what))
                else:
                    last = {"G": (j - 1, "G1"), "U": (j - 1, "U1"), "D": (j, "D1")}[what]
                    if isinstance(j, int) and j == 1 and what != "D":
                        sp.wait_ge(lo_done, half_at(0, last[1]) + 1)
                    else:
                        jj, w = last
                        sp.wait_ge(lo_done, FFN0 + 5 + 6 * (jj - 1) + BLOCK.index(w) + 1)
                slot = (FFN0 // 2 + "GUD".index(what)) % NRAW
                if what == "D":
                    src = w_down[0].rearrange("(j f p) n -> j p f n", f=2, p=P)[j]
                    dst = raw[:, slot, :].rearrange("p (f n) -> p f n", f=2)
                else:
                    w = w_gate if what == "G" else w_up
                    src = w[0].rearrange("(k p) (j n) -> j p k n", p=P, n=256)[j]
                    dst = raw[:, slot, :].rearrange("p (k n) -> p k n", n=256)
                sp.dma_start(dst, src).then_inc(raw_in[slot], 16)

            for q in range(16, 32):
                load_late(q)
                if q == 20:
                    load_out(3)
                if q == 24:
                    load_ffn(0, "G")
                if q == 28:
                    load_ffn(0, "U")
            load_ffn(0, "D")
            for j in range(1, NJ):
                for what in "GUD":
                    load_ffn(j, what)

            for tt in range(TT):
                for nb in range(NB):
                    sp.wait_ge(out_ready, tt * NB + nb + 1)
                    sp.dma_start(out[0, tt * P:(tt + 1) * P, nb * 512:nb * 512 + 512],
                                 out_sb[:, tt, nb * 512:nb * 512 + 512]).then_inc(out_done, 16)
            sp.wait_ge(out_done, 16 * TT * NB)

        @block.gpsimd
        def _(gp):
            g = nc.gpsimd
            n_pool = [0]

            def link(ins):
                n_pool[0] += 1
                ins.then_inc(pool, 1)
                gp.wait_ge(pool, n_pool[0])

            g.memset(minus_half[:], -0.5)
            g.memset(ones[:], 1.0)
            g.memset(kcT[:], 0.0)
            link(g.memset(ident[:], 0.0))
            g.affine_select(out=ident[:], in_=ident[:], compare_op=ALU.not_equal, fill=1.0, base=0,
                            pattern=[[-1, P]], channel_multiplier=1).then_inc(consts, 1)

            def root(use, n, parts=P):
                k = ROOT[use]
                gp.wait_ge(var_ready, k + 1)
                g.tensor_tensor(roots[0:parts, k, 0:n], sums[0:parts, k, 0:n], minus_half[0:parts, 0:n], ALU.pow).then_inc(root_ready, 1)

            root("x", TT)
            slope = [2.0 ** (-8.0 * (h + 1) / H) for h in range(H)]
            link(g.iota(cdist[:], pattern=[[P, TT], [-STRIDE, NC]], base=1 - L, channel_multiplier=1,
                        allow_small_or_imprecise_dtypes=True))
            for h in range(H):
                pr, a, i = h // (2 * HG), h // HG % 2, h % HG
                for tt in range(TT):
                    last = g.tensor_scalar(cbias[:, pr, a, tt * HG + i, :], cdist[:, tt, :], slope[h], 0.0, ALU.mult, ALU.add)
            link(last)
            link(g.memset(cmask[:], 1.0))
            g.affine_select(out=cmask[:].rearrange("p (t i) n -> p t i n", t=TT), in_=cmask[:].rearrange("p (t i) n -> p t i n", t=TT),
                            compare_op=ALU.is_ge, fill=0.0, base=1 - L, pattern=[[P, TT], [0, HG], [-STRIDE, NC]], channel_multiplier=1)
            for pr in range(NP):
                v = cbias[:, pr].rearrange("p a (t i) n -> p a t i n", t=TT)
                for a in range(2):
                    last = g.affine_select(out=v[:, a], in_=v[:, a], compare_op=ALU.is_ge, fill=MASKED, base=1 - L,
                                           pattern=[[P, TT], [0, HG], [-STRIDE, NC]], channel_multiplier=1)
            link(last)
            gp.wait_ge(ada_used, KD)
            link(g.iota(bias[:, H - 1, :], pattern=[[-1, 2 * P]], base=P, channel_multiplier=1,
                        allow_small_or_imprecise_dtypes=True))
            for h in range(H):
                last = g.tensor_scalar(bias[:, h, :], bias[:, H - 1, :], slope[h], 0.0, ALU.mult, ALU.add)
            link(last)
            for h in range(0, H, HG):
                last = g.affine_select(out=bias[:, h:h + HG, :], in_=bias[:, h:h + HG, :], compare_op=ALU.is_ge, fill=MASKED, base=P,
                                       pattern=[[0, HG], [-1, 2 * P]], channel_multiplier=1)
            last.then_inc(bias_ready, 1)

            root(("s", 0), G)
            root(("s", 1), G)
            root(("w", 0), G)
            root(("w", 1), G)
            root("kc", 1, G * NC)
            root(("q0", 0), 2 * HG)
            root(("q0", 1), 2 * HG)

            def normalise(m):
                n = P * (STEPS[m][1] + 1)
                gp.wait_ge(weight_ready, m + 1)
                for ab in range(4):
                    last = g.tensor_scalar(prob[:, m % 4, ab, 0:n], prob[:, m % 4, ab, 0:n], weight[:, m % 4, ab:ab + 1], 1.0,
                                           ALU.mult, ALU.mult)
                last.then_inc(p_ready, 1)

            for m in range(NS):
                if m in (3, 4):
                    root(("q1", m - 3), 2 * HG)
                normalise(m)
            root(("x2", 0), 1)
            root(("x2", 1), 1)

        @block.scalar
        def _(act):
            s = nc.scalar
            def load_bias(gr):
                for j in range(4):
                    b = 4 * gr + j
                    act.dma_start(ada_bias[32 * j:32 * j + 32, :],
                                  ada_b[0:1, 512 * b:512 * b + 512].to_broadcast([32, 512])).then_inc(bias_in[gr], 16)

            act.wait_ge(c_in, 16)
            s.activation(cols[:, C_ACT, :], cols[:, C_IN, :], ACT.Tanh, scale=0.5).then_inc(c_tanh, 1)

            n_own = [0]

            def hi(n):
                w = width_of(n)
                act.wait_ge(raw_in[unit_of(n) % NRAW], raw_target(n))
                if n >= NRING:
                    act.wait_ge(used, n - NRING + 1)
                s.activation(w_hi[:, n % NRING, 0:w], raw_half(n, w), ACT.Copy).then_inc(hi_done, 1)

            def raw_target(n):
                u = unit_of(n)
                return 16 * sum(2 if START["out"] // 2 <= v < FFN0 // 2 else 1 for v in range(u % NRAW, u + 1, NRAW))

            def hi_ffn(j, what):
                o = owner(j, what)
                slot = (FFN0 // 2 + "GUD".index(what[0])) % NRAW
                act.wait_ge(raw_in[slot], ffn_target(slot, o))
                n = half_at(j, what)
                act.wait_ge(used, n - NRING + 1)
                r = slot_of(j, what)
                s.activation(split_parts(w_hi, r, what), raw_ffn(what), ACT.Copy).then_inc(hi_done, 1)

            def ffn_target(slot, o):
                before = 16 * sum(2 if START["out"] // 2 <= v < FFN0 // 2 else 1 for v in range(slot, FFN0 // 2, NRAW))
                return before + 16 * (o + 1)

            DONE = {name: START[name] + (2 if name == "gates" else 4) for name in START}
            PREV = dict(zip(list(NAT)[2:], list(NAT)))

            def square(name, tt, bk, width):
                act.wait_ge(used, DONE[name])
                if (name, tt) in PREV:
                    act.wait_ge(var_ready, ROOT[PREV[name, tt]] + 1)
                s.activation(sq[:, NAT[name, tt] % 2, 0:width], bank[bk][:, 0:width], ACT.Square).then_inc(squared, 1)

            def keys(name, tt, bk, br):
                square(name, tt, bk, KV)
                s.activation(v_nat[:, tt, br, :], bank[bk][:, KV:2 * KV], ACT.Copy).then_inc(copied, 1)

            hi(0)
            for i in range(4):
                if i % 2:
                    act.wait_ge(cols_ready, 1)
                    act.wait_ge(xnT, i + 1)
                    for k in (2 * i, 2 * i + 1):
                        last = s.activation(h_f[:, k, :], bank[i][:, (k % 2) * 256:(k % 2) * 256 + 256], ACT.Identity,
                                            scale=cols[:, SC_MIX, k:k + 1], bias=cols[:, SH_MIX, k:k + 1])
                    n_own[0] += 1
                    last.then_inc(own, 1)
                    act.wait_ge(own, n_own[0])
                else:
                    act.wait_ge(hf_ready, i // 2 + 1)
                s.activation(h_hi[:, 2 * i:2 * i + 2, :], h_f[:, 2 * i:2 * i + 2, :], ACT.Copy).then_inc(hhi_ready, 1)
                if i == 1:
                    hi(1)
            for n in range(2, 7):
                hi(n)
            act.wait_ge(rows_ready, 1)
            load_bias(1)
            act.wait_ge(used, DONE["c"])
            for tt in range(TT):
                s.activation(kcv[:, tt], spread(bank[4 + 2 * tt][:, :].rearrange("p (g d) -> p g d", d=DK), 2, 2), ACT.Copy).then_inc(copied, 1)
            for n in range(7, 12):
                hi(n)
            for tt in range(TT):
                keys("s", tt, tt, 0)
            for n in range(12, 15):
                hi(n)
            act.wait_ge(t_filled, T_AT["hid",] + 1)
            hid = bank[4 + T_AT["hid",] % 2][:, 0:128].rearrange("p (v n) -> p v n", v=2)[:, :, 0:G * NC]
            s.activation(gel_t[:], hid, ACT.Square).then_inc(gel_sq, 1)
            for n in range(15, 16):
                hi(n)
            act.wait_ge(gel_in, 1)
            s.activation(gel_t[:], gel_t[:], ACT.Tanh, scale=GELU_C).then_inc(gel_tanh, 1)
            for tt in range(TT):
                keys("w", tt, 2 + tt, 1)
            hi(16)
            act.wait_ge(used, DONE["gates"])
            s.activation(gates_t[:], bank[6][0:3 * H, 0:SEQ], ACT.Tanh, scale=0.5).then_inc(gates_done, 1)
            for n in range(17, 20):
                hi(n)
            act.wait_ge(t_filled, T_AT["cw2",] + 1)
            kcb = bank[4 + T_AT["cw2",] % 2]
            s.activation(kc_nat[:, 0, :], kcb[0:G * NC, 0:DK], ACT.Square, accum_out=sums[0:G * NC, ROOT["kc"], 1:2]).then_inc(kc_sum, 1)
            for n in range(20, 22):
                hi(n)
            for tt in range(TT):
                square("q0", tt, tt, 512)
            act.wait_ge(rows_ready, 2)
            load_bias(2)

            def c_exp(pr):
                act.wait_ge(cs_ready, pr + 1)
                s.activation(cprob[:, pr], cprob[:, pr], ACT.Exp, scale=-1.0).then_inc(ce_ready, 1)

            def exps(m):
                n = P * (STEPS[m][1] + 1)
                for ab in range(4):
                    act.wait_ge(max_ready, 4 * m + ab + 1)
                    v = prob[:, m % 4, ab, 0:n]
                    s.activation(v, v, ACT.Exp, bias=negmax[:, m % 4, ab:ab + 1], scale=-1.0,
                                 accum_out=den[:, m % 4, ab:ab + 1]).then_inc(exp_ready, 1)

            def o_part(v):
                pr, tt = v // TT, v % TT
                act.wait_ge(pv_done, v + 1)
                s.activation(o_hi[:, tt, HG * pr:HG * pr + HG, :], bank[6][:, :].rearrange("p (i n) -> p i n", i=HG),
                             ACT.Copy).then_inc(ohi_ready, 1)

            ahead = {0: 22, 1: 23, 2: 24, 4: 25, 5: 26, 6: 27}
            for m in range(NS + LAG):
                if m < NS:
                    exps(m)
                if m in C_STEP:
                    c_exp(C_STEP.index(m))
                if m in ahead:
                    hi(ahead[m])
                if m == 2:
                    for tt in range(TT):
                        square("q1", tt, 6 + tt, 512)
                if m > LAG and (m - LAG) % HG == 0:
                    o_part((m - LAG) // HG - 1)
            o_part(NP * TT - 1)
            for n in (28, 29):
                hi(n)
            for what in FIRST_BLOCK[0:2]:
                hi_ffn(0, what)

            def norm_x(tt):
                for nb in range(NB):
                    act.wait_ge(x2_ready, tt * NB + nb + 1)
                    s.activation(xn[:, tt, nb * 512:nb * 512 + 512], x_sb[:, tt, nb * 512:nb * 512 + 512], ACT.Square,
                                 accum_out=sums[:, ROOT["x2", tt], 4 + nb:5 + nb]).then_inc(x2_squared, 1)
                act.wait_ge(root_ready, ROOT["x2", tt] + 1)
                s.activation(xn[:, tt, 512:1024], x_sb[:, tt, 512:1024], ACT.Copy, scale=roots[:, ROOT["x2", tt], 0:1]).then_inc(xn2_act, 1)

            def modulate_x(tt):
                ts = slice(tt * P, (tt + 1) * P)
                act.wait_ge(xn2T, 2 * tt + 2)
                for k in range(4, 8):
                    last = s.activation(h_f[:, k, ts], bank[4 + 2 * tt + 1][:, (k % 4) * P:(k % 4 + 1) * P], ACT.Identity,
                                        scale=cols[:, SC_FFN, k:k + 1], bias=cols[:, SH_FFN, k:k + 1])
                n_own[0] += 1
                last.then_inc(own, 1)
                act.wait_ge(own, n_own[0])
                s.activation(h_hi[:, 4:8, ts], h_f[:, 4:8, ts], ACT.Copy).then_inc(h2hi_ready, 1)
                act.wait_ge(h2f_ready, tt + 1)
                s.activation(h_hi[:, 0:4, ts], h_f[:, 0:4, ts], ACT.Copy).then_inc(h2hi_ready, 1)

            for tt in range(TT):
                norm_x(tt)
                modulate_x(tt)
            for what in FIRST_BLOCK[2:]:
                hi_ffn(0, what)

            def act_gate(j, f):
                act.wait_ge(used, half_at(j, f"U{f}") + 1)
                s.activation(th[:, f, :], bank[4 + f][:, 0:256], ACT.Tanh, scale=0.5).then_inc(th_ready, 1)
                act.wait_ge(act_ready, 2 * j + f + 1)
                s.activation(act_hi[:, f, :], act_f[:, f, :], ACT.Copy).then_inc(ahi_ready, 1)

            act_gate(0, 0)
            for what in ("G0", "U0"):
                hi_ffn(1, what)
            act_gate(0, 1)
            hi_ffn(1, "D1")

            def act_block(j):
                for what in ("G1", "U1", "D0"):
                    hi_ffn(j, what)
                act_gate(j, 0)
                for what in ("G0", "U0"):
                    hi_ffn(j + 1, what)
                act_gate(j, 1)
                hi_ffn(j + 1, "D1")

            for j in range(1, NJ - 1):
                act_block(j)
            j = NJ - 1
            for what in ("G1", "U1", "D0"):
                hi_ffn(j, what)
            act_gate(j, 0)
            act_gate(j, 1)
            hi_ffn(NJ, "D1")

        @block.vector
        def _(ve):
            v = nc.vector
            n_dve = [0]

            def link(ins):
                n_dve[0] += 1
                ins.then_inc(dve, 1)
                ve.wait_ge(dve, n_dve[0])

            def mean_eps(use, n, size, parts=P):
                v.tensor_scalar(sums[0:parts, ROOT[use], 0:n], sums[0:parts, ROOT[use], 0:n], 1.0 / size, EPS,
                                ALU.mult, ALU.add).then_inc(var_ready, 1)

            for t in range(TT):
                ve.wait_ge(x_in[t], 16)
                link(v.tensor_tensor_reduce(xn[:, t, :], x_sb[:, t, :], x_sb[:, t, :], 1.0, 0.0, ALU.mult, ALU.add,
                                            sums[:, ROOT["x"], t:t + 1]))
            mean_eps("x", TT, D)
            ve.wait_ge(c_tanh, 1)
            link(v.tensor_scalar(cols[:, C_ACT, :], cols[:, C_ACT, :], 0.5, 0.5, ALU.mult, ALU.add))
            link(v.tensor_tensor(cols[:, C_ACT, :], cols[:, C_ACT, :], cols[:, C_IN, :], ALU.mult))
            v.tensor_copy(c_rep[:], spread(cols[:, C_ACT, :], 2, 32)).then_inc(c_ready, 1)
            ve.wait_ge(root_ready, ROOT["x"] + 1)
            for t in range(TT):
                v.tensor_scalar(xn[:, t, :], x_sb[:, t, :], roots[:, ROOT["x"], t:t + 1], None, ALU.mult).then_inc(xn_ready, 1)
            ve.wait_ge(params_t, 1)
            pb = bank[5]
            v.tensor_copy(cols[:, W_MIX:W_FFN + 1, :], pb[:, 0:16].rearrange("p (a k) -> p a k", a=2))
            v.tensor_scalar(qk_col[:, 0:1], pb[:, 16:17], -SCALE, None, ALU.mult)
            v.tensor_copy(qk_col[:, 1:4], pb[:, 17:20])
            link(v.tensor_copy(pos_col[:], pb[:, 32:64].rearrange("p (a k) -> p a k", a=2)))

            def lo(n):
                w = width_of(n)
                ve.wait_ge(hi_done, n + 1)
                v.tensor_tensor(w_lo[:, n % NRING, 0:w], raw_half(n, w), w_hi[:, n % NRING, 0:w].bitcast(F32), ALU.subtract).then_inc(lo_done, 1)

            def lo_ffn(j, what):
                ve.wait_ge(hi_done, half_at(j, what) + 1)
                r = slot_of(j, what)
                v.tensor_tensor(split_parts(w_lo, r, what), raw_ffn(what), split_parts(w_hi, r, what).bitcast(F32),
                                ALU.subtract).then_inc(lo_done, 1)

            def rows_of(gr, bk):
                ve.wait_ge(ada_used, KD) if gr == 0 else ve.wait_ge(late_used, 16 * gr)
                ve.wait_ge(bias_in[gr], 64)
                v.tensor_tensor(rows[:, gr % 2, :], bank[bk][:, :], ada_bias[:], ALU.add).then_inc(rows_ready, 1)

            def columns_in(b, j0):
                return b[:, :].rearrange("p (q j r) -> p j q r", q=4, j=4)[:, j0:j0 + 2, :, 0]

            def as_rows(c):
                return cols[:, c, :].rearrange("p (j q) -> p j q", q=4)

            rows_of(0, 4)
            ve.wait_ge(mix_cols, 1)
            v.tensor_copy(as_rows(SH_MIX), columns_in(pb, 0))
            v.scalar_tensor_tensor(out=as_rows(SC_MIX), in0=columns_in(pb, 2), scalar=1.0, in1=as_rows(W_MIX), op0=ALU.add, op1=ALU.mult).then_inc(cols_ready, 1)
            ve.wait_ge(cols_ready, 1)

            def modulate(i):
                for k in (2 * i, 2 * i + 1):
                    last = v.tensor_scalar(h_f[:, k, :], bank[i][:, (k % 2) * 256:(k % 2) * 256 + 256],
                                           cols[:, SC_MIX, k:k + 1], cols[:, SH_MIX, k:k + 1], ALU.mult, ALU.add)
                last.then_inc(hf_ready, 1)

            def h_rest(i):
                ve.wait_ge(hhi_ready, i + 1)
                v.tensor_tensor(h_lo[:, 2 * i:2 * i + 2, :], h_f[:, 2 * i:2 * i + 2, :], h_hi[:, 2 * i:2 * i + 2, :].bitcast(F32),
                                ALU.subtract).then_inc(h_ready, 1)

            modulate(0)
            lo(0)
            h_rest(0)
            modulate(2)
            h_rest(1)
            h_rest(2)
            lo(1)
            h_rest(3)
            for n in range(2, 7):
                lo(n)

            def t_bank(*use):
                ve.wait_ge(t_filled, T_AT[use] + 1)
                return bank[4 + T_AT[use] % 2]

            def drained(*use, ins):
                ins.then_inc(t_drained, 1)

            def spread_blocks(tt, kv):
                b = t_bank("c", tt, kv)
                for a in range(2):
                    first = (0, 1)[a] if tt == 0 else 0
                    n = (8, 7)[a] if tt == 0 else (7, 8)[a]
                    at_n = 8 * tt + first - a
                    src = b[64 * a:64 * a + 64, :].rearrange("p (g n l) -> p g l n", g=G, l=STRIDE)
                    dst = blocks[64 * a:64 * a + 64, kv].rearrange("p l (g n) -> p g l n", g=G)
                    for g in range(G):
                        last = v.tensor_tensor(dst[:, g, :, at_n:at_n + n], src[:, g, :, first:first + n],
                                               spread(pos_col[64 * a:64 * a + 64, kv, :], 2, n), ALU.add)
                drained("c", tt, kv, ins=last)

            def head_sums(name, tt, heads):
                k = NAT[name, tt]
                ve.wait_ge(squared, k + 1)
                link(v.tensor_reduce(sums[:, ROOT[name, tt], 0:heads], sq[:, k % 2, 0:heads * DK].rearrange("p (h d) -> p h d", d=DK), AX_X, ALU.add))
                v.tensor_scalar(sums[:, ROOT[name, tt], 0:heads], sums[:, ROOT[name, tt], 0:heads], 1.0 / DK, EPS,
                                ALU.mult, ALU.add).then_inc(var_ready, 1)

            def head_scale(name, tt, dst, bk, heads):
                ve.wait_ge(root_ready, ROOT[name, tt] + 1)
                if name[0] != "q":
                    ve.wait_ge(copied, NAT[name, tt] + 3)
                r = roots[:, ROOT[name, tt], 0:heads]
                if name[0] == "q":
                    v.tensor_tensor(dst.rearrange("p (i a d) -> p a i d", a=2, d=DK), bank[bk][:, :].rearrange("p (a i d) -> p a i d", a=2, d=DK),
                                    spread(r.rearrange("p (a i) -> p a i", a=2), 3, DK), ALU.mult).then_inc(scaled, 1)
                else:
                    v.tensor_tensor(dst.rearrange("p (h d) -> p h d", d=DK), bank[bk][:, 0:heads * DK].rearrange("p (h d) -> p h d", d=DK),
                                    spread(r, 2, DK), ALU.mult).then_inc(scaled, 1)

            for n, (tt, kv) in zip((7, 8, 9, 10), ((0, 0), (0, 1), (1, 0), (1, 1))):
                lo(n)
                spread_blocks(tt, kv)
            lo(11)
            for tt in range(TT):
                head_sums("s", tt, G)
            lo(12)
            for tt in range(TT):
                head_scale("s", tt, k_nat[:, tt, 0, :], tt, G)
            for n in range(13, 15):
                lo(n)
            b = t_bank("hid")
            hid = b[:, 0:128].rearrange("p (v n) -> p v n", v=2)[:, :, 0:G * NC]
            ve.wait_ge(gel_sq, 1)
            link(v.tensor_scalar(gel_t[:], gel_t[:], GELU_A, 1.0, ALU.mult, ALU.add))
            v.tensor_tensor(gel_t[:], gel_t[:], hid, ALU.mult).then_inc(gel_in, 1)
            lo(15)
            ve.wait_ge(gel_tanh, 1)
            link(v.tensor_scalar(gel_t[:], gel_t[:], 0.5, 0.5, ALU.mult, ALU.add))
            v.tensor_tensor(gel[:], gel_t[:], hid, ALU.mult).then_inc(t_drained, 1)
            for tt in range(TT):
                head_sums("w", tt, G)
            lo(16)
            for tt in range(TT):
                head_scale("w", tt, k_nat[:, tt, 1, :], 2 + tt, G)
            b = t_bank("gates")
            v.tensor_scalar(gates[:], b[:, 0:TT * 3 * H].rearrange("p (t n) -> p t n", t=TT), 0.5, 0.5, ALU.mult, ALU.add).then_inc(t_drained, 1)
            for tt in range(TT):
                b = t_bank("k", tt)
                for br in range(2):
                    last = v.tensor_scalar(kT[:, :, br, tt * P:(tt + 1) * P], b[:, br * 256:br * 256 + 256].rearrange("p (r n) -> p r n", r=NP),
                                           qk_col[:, 2 + br:3 + br], None, ALU.mult)
                last.then_inc(t_drained, 1)
                lo(17 + tt)
            lo(19)
            b = t_bank("cw2")
            ve.wait_ge(kc_sum, 1)
            v.tensor_copy(vc[:], b[0:NC, DK:DK + G * DK].rearrange("p (g d) -> p g d", g=G))
            v.tensor_scalar(sums[0:G * NC, ROOT["kc"], 0:1], sums[0:G * NC, ROOT["kc"], 1:2], 1.0 / DK, EPS,
                            ALU.mult, ALU.add).then_inc(var_ready, 1)
            ve.wait_ge(root_ready, ROOT["kc"] + 1)
            for a in range(2):
                last = v.tensor_scalar(kc_nat[:, a, :], b[0:G * NC, 0:DK], roots[0:G * NC, ROOT["kc"], 0:1], None, ALU.mult)
            last.then_inc(t_drained, 1)
            lo(20)
            rows_of(1, 7)

            def queries(pr):
                for tt in range(TT):
                    b = t_bank("q", pr, tt)
                    v.tensor_scalar(qT[:, pr, tt], b[:, :].rearrange("p (i n) -> p i n", i=HG), qk_col[:, 0:1], None, ALU.mult).then_inc(t_drained, 1)

            for tt in range(TT):
                head_sums("q0", tt, 2 * HG)
            lo(21)
            b = t_bank("kc")
            for a in range(2):
                hp = slice(64 * a, 64 * a + 64)
                last = v.tensor_scalar(kcT[hp, :, a, :], b[hp, 0:G * NC].rearrange("p (r a n) -> p r a n", r=NP, a=2)[:, :, a, :],
                                       qk_col[hp, 1:2], None, ALU.mult)
            last.then_inc(t_drained, 1)
            for tt in range(TT):
                head_scale("q0", tt, q_nat[:, tt, :], tt, 2 * HG)
            queries(0)
            ve.wait_ge(bias_ready, 1)

            def c_scores(pr):
                cp = cprob[:, pr]
                b = t_bank("cs", pr)
                for a in range(2):
                    last = v.tensor_tensor(cp[:, a * TT * HG:(a + 1) * TT * HG, :],
                                           b[:, 0:2 * TT * HG * NC].rearrange("p (t a n) -> p a t n", a=2, n=NC)[:, a], cbias[:, pr, a], ALU.add)
                last.then_inc(t_drained, 1)
                ve.wait_ge(t_drained, T_AT["cs", pr] + 1)
                link(v.tensor_reduce(cstat[:, 0, :], cp, AX_X, ALU.min))
                v.tensor_tensor(cp, cp, spread(cstat[:, 0, :], 2, NC), ALU.subtract).then_inc(cs_ready, 1)

            def c_weights(pr):
                cp = cprob[:, pr]
                ve.wait_ge(ce_ready, pr + 1)
                for a in range(2):
                    last = v.tensor_tensor(cp[:, a * TT * HG:(a + 1) * TT * HG, :], cp[:, a * TT * HG:(a + 1) * TT * HG, :], cmask[:], ALU.mult)
                link(last)
                link(v.tensor_reduce(cstat[:, 1, :], cp, AX_X, ALU.add))
                link(v.tensor_scalar(cstat[:, 1, :], cstat[:, 1, :], 1e-30, None, ALU.max))
                link(v.reciprocal(cstat[:, 2, :], cstat[:, 1, :]))
                for a in range(2):
                    h0 = (2 * pr + a) * HG
                    last = v.tensor_tensor(cstat[:, 3, a * TT * HG:(a + 1) * TT * HG].rearrange("p (t i) -> p t i", t=TT),
                                           cstat[:, 2, a * TT * HG:(a + 1) * TT * HG].rearrange("p (t i) -> p t i", t=TT),
                                           gates[:, :, h0:h0 + HG], ALU.mult)
                link(last)
                v.tensor_tensor(cp, cp, spread(cstat[:, 3, :], 2, NC), ALU.mult).then_inc(cp_ready, 1)

            def maxima(m):
                pr, tt, i = STEPS[m]
                n = P * (tt + 1)
                ve.wait_ge(s_ready, m + 1)
                if m >= 4:
                    ve.wait_ge(t_filled, T_AT["p", m - 4, STEPS[m - 4][1]] + 1)
                for a in range(2):
                    h = (2 * pr + a) * HG + i
                    for br in range(2):
                        v.tensor_tensor_reduce(prob[:, m % 4, 2 * a + br, 0:n], bank[2 * (m % 2) + a][:, br * n:(br + 1) * n],
                                               bias[:, h, 2 * P - n:2 * P], 1.0, HUGE, ALU.add, ALU.min,
                                               negmax[:, m % 4, 2 * a + br:2 * a + br + 1]).then_inc(max_ready, 1)

            def weights(m):
                pr, tt, i = STEPS[m]
                ve.wait_ge(exp_ready, 4 * m + 4)
                link(v.reciprocal(recip[:, m % 4, :], den[:, m % 4, :]))
                gt = gates[:, tt, H:3 * H].rearrange("p (b r a i) -> p r i a b", b=2, r=NP, a=2)[:, pr, i]
                v.tensor_tensor(weight[:, m % 4, :].rearrange("p (a b) -> p a b", a=2), recip[:, m % 4, :].rearrange("p (a b) -> p a b", a=2),
                                gt, ALU.mult).then_inc(weight_ready, 1)

            def take_p(m):
                pr, tt, i = STEPS[m]
                if pr > 0 and i == 0:
                    ve.wait_ge(pv_done, tt + 1)
                if tt == 0:
                    b = t_bank("p", m, 0)
                    v.tensor_copy(pt[0][:, :, :, 0, i * P:(i + 1) * P], b[:, :].rearrange("p (a b n) -> p a b n", a=2, b=2)).then_inc(t_drained, 1)
                else:
                    for a in range(2):
                        b = t_bank("p", m, a)
                        v.tensor_copy(pt[1][:, a, :, :, i * P:(i + 1) * P], b[:, :].rearrange("p (b k n) -> p b k n", b=2, k=2)).then_inc(t_drained, 1)

            def take_pc(pr, tt):
                if pr * TT + tt > 0:
                    ve.wait_ge(pv_done, pr * TT + tt)
                for a in range(2):
                    b = t_bank("pc", pr, tt, a)
                    v.tensor_copy(pcT[:, a, :], b[0:NC, :]).then_inc(t_drained, 1)

            def o_rest(n):
                pr, tt = n // TT, n % TT
                ve.wait_ge(ohi_ready, n + 1)
                v.tensor_tensor(o_lo[:, tt, HG * pr:HG * pr + HG, :], bank[6][:, :].rearrange("p (i n) -> p i n", i=HG),
                                o_hi[:, tt, HG * pr:HG * pr + HG, :].bitcast(F32), ALU.subtract).then_inc(o_ready, 1)

            ahead = {0: 22, 1: 23, 2: 24, 4: 25, 5: 26, 6: 27}
            for m in range(NS + LAG):
                if m == Q1_STEP:
                    queries(1)
                if m < NS:
                    maxima(m)
                if m in C_STEP:
                    c_scores(C_STEP.index(m))
                if m == Q1_STEP - 1:
                    for tt in range(TT):
                        head_scale("q1", tt, q_nat[:, tt, :], 6 + tt, 2 * HG)
                if m - 1 in C_STEP:
                    c_weights(C_STEP.index(m - 1))
                if 1 <= m <= NS:
                    weights(m - 1)
                if m in (2, 3):
                    head_sums("q1", m - 2, 2 * HG)
                if m - 1 in ahead:
                    lo(ahead[m - 1])
                if m >= LAG:
                    pr, tt, i = STEPS[m - LAG]
                    take_p(m - LAG)
                    if i == HG - 1:
                        take_pc(pr, tt)
                if m > LAG and (m - LAG) % HG == 0:
                    o_rest((m - LAG) // HG - 1)
                if m == 14:
                    rows_of(2, 7)
            o_rest(NP * TT - 1)
            for n in (28, 29):
                lo(n)
            for nb in range(NB):
                b = t_bank("gm", nb)
                v.tensor_copy(gm_b[:, nb * 512:nb * 512 + 512], b[:, :]).then_inc(t_drained, 1)
            v.tensor_copy(as_rows(SH_FFN), columns_in(t_bank("shf"), 2)).then_inc(t_drained, 1)
            v.scalar_tensor_tensor(out=as_rows(SC_FFN), in0=columns_in(t_bank("scf"), 0), scalar=1.0, in1=as_rows(W_FFN),
                                   op0=ALU.add, op1=ALU.mult).then_inc(t_drained, 1)
            for what in FIRST_BLOCK[0:2]:
                lo_ffn(0, what)

            def add_y(tt):
                ve.wait_ge(y_done, 1) if tt == 0 else ve.wait_ge(used, FFN0)
                for nb in range(NB):
                    link(v.tensor_tensor(mixed[:, nb, :], bank[tt * NB + nb][:, :], gm_b[:, nb * 512:nb * 512 + 512], ALU.mult))
                    v.tensor_tensor(x_sb[:, tt, nb * 512:nb * 512 + 512], x_sb[:, tt, nb * 512:nb * 512 + 512], mixed[:, nb, :],
                                    ALU.add).then_inc(x2_ready, 1)

            def norm_x(tt):
                k = ROOT["x2", tt]
                ve.wait_ge(x2_squared, NB * (tt + 1))
                link(v.tensor_tensor(sums[:, k, 0:1], sums[:, k, 4:5], sums[:, k, 5:6], ALU.add))
                mean_eps(("x2", tt), 1, D)
                ve.wait_ge(root_ready, k + 1)
                v.tensor_scalar(xn[:, tt, 0:512], x_sb[:, tt, 0:512], roots[:, k, 0:1], None, ALU.mult).then_inc(xn2_ready, 1)

            def modulate_x(tt):
                ts = slice(tt * P, (tt + 1) * P)
                ve.wait_ge(xn2T, 2 * tt + 1)
                for k in range(4):
                    last = v.tensor_scalar(h_f[:, k, ts], bank[4 + 2 * tt][:, k * P:(k + 1) * P],
                                           cols[:, SC_FFN, k:k + 1], cols[:, SH_FFN, k:k + 1], ALU.mult, ALU.add)
                last.then_inc(h2f_ready, 1)

            def rest_x(tt):
                ts = slice(tt * P, (tt + 1) * P)
                for half in (1, 0):
                    ks = slice(4 * half, 4 * half + 4)
                    ve.wait_ge(h2hi_ready, 2 * tt + 2 - half)
                    v.tensor_tensor(h_lo[:, ks, ts], h_f[:, ks, ts], h_hi[:, ks, ts].bitcast(F32), ALU.subtract).then_inc(h2_ready, 1)

            add_y(0)
            norm_x(0)
            modulate_x(0)
            add_y(1)
            rest_x(0)
            norm_x(1)
            modulate_x(1)
            rest_x(1)
            for what in FIRST_BLOCK[2:]:
                lo_ffn(0, what)

            def dve_gate(j, f):
                ve.wait_ge(th_ready, 2 * j + f + 1)
                v.scalar_tensor_tensor(out=sg[:, f, :], in0=th[:, f, :], scalar=1.0, in1=bank[4 + f][:, 0:256],
                                       op0=ALU.add, op1=ALU.mult).then_inc(dve, 1)
                ve.wait_ge(dve, n_dve[0] + 2 * j + f + 1)
                v.scalar_tensor_tensor(out=act_f[:, f, :], in0=sg[:, f, :], scalar=0.5, in1=bank[4 + f][:, 256:512],
                                       op0=ALU.mult, op1=ALU.mult).then_inc(act_ready, 1)
                ve.wait_ge(ahi_ready, 2 * j + f + 1)
                v.tensor_tensor(act_lo[:, f, :], act_f[:, f, :], act_hi[:, f, :].bitcast(F32), ALU.subtract).then_inc(a_ready, 1)

            dve_gate(0, 0)
            for what in ("G0", "U0"):
                lo_ffn(1, what)
            dve_gate(0, 1)
            lo_ffn(1, "D1")

            def dve_block(j):
                for what in ("G1", "U1", "D0"):
                    lo_ffn(j, what)
                dve_gate(j, 0)
                for what in ("G0", "U0"):
                    lo_ffn(j + 1, what)
                dve_gate(j, 1)
                lo_ffn(j + 1, "D1")

            for j in range(1, NJ - 1):
                dve_block(j)
            j = NJ - 1
            for what in ("G1", "U1", "D0"):
                lo_ffn(j, what)
            dve_gate(j, 0)
            dve_gate(j, 1)
            lo_ffn(NJ, "D1")
            n_dve[0] += 2 * NJ
            for nb in range(NB):
                b = t_bank("gf", nb)
                v.tensor_copy(gf_b[:, nb * 512:nb * 512 + 512], b[:, :]).then_inc(t_drained, 1)
            ve.wait_ge(t_drained, T_AT["gf", NB - 1] + 1)
            for tt in range(TT):
                ve.wait_ge(y2_done, 1) if tt == 0 else ve.wait_ge(used, half_at(NJ, "D1") + 1)
                for nb in range(NB):
                    link(v.tensor_tensor(mixed[:, nb, :], bank[tt * NB + nb][:, :], gf_b[:, nb * 512:nb * 512 + 512], ALU.mult))
                    v.tensor_tensor(out_sb[:, tt, nb * 512:nb * 512 + 512], x_sb[:, tt, nb * 512:nb * 512 + 512], mixed[:, nb, :],
                                    ALU.add).then_inc(out_ready, 1)

        @block.tensor
        def _(pe):
            t = nc.tensor

            def mm3(dst, l_hi, l_lo, r_hi, r_lo, start, stop):
                t.matmul(dst, l_hi, r_hi, start=start, stop=False, skip_group_check=True)
                t.matmul(dst, l_hi, r_lo, start=False, stop=False, skip_group_check=True)
                return t.matmul(dst, l_lo, r_hi, start=False, stop=stop, skip_group_check=True)

            pe.wait_ge(consts, 1)
            pe.wait_ge(norm_in, 32)
            pe.wait_ge(qk_in, 32)
            pe.wait_ge(pos_in, 32)
            for a in range(2):
                t.transpose(bank[5][:, 8 * a:8 * a + 8], norm_nat[:, a, :], ident[0:8, 0:8])
            t.transpose(bank[5][:, 16:20], qk_nat[:].rearrange("p a d -> p (a d)"), ident[0:4, 0:4])
            t.transpose(bank[5][:, 32:64], pos_nat[:].rearrange("p a d -> p (a d)"), ident[0:2 * STRIDE, 0:2 * STRIDE]).then_inc(params_t, 1)
            pe.wait_ge(c_ready, 1)
            for k in range(KD):
                if k == 4:
                    pe.wait_ge(xn_ready, TT)
                    for kk in range(KD):
                        for tt in range(TT):
                            last = t.transpose(bank[kk // 2][:, (kk % 2) * 256 + tt * P:(kk % 2) * 256 + (tt + 1) * P],
                                               xn[:, tt, kk * P:(kk + 1) * P], ident[:, :])
                        if kk % 2:
                            last.then_inc(xnT, 1)
                pe.wait_ge(ada_in[k], 16)
                for j in range(4):
                    last = t.matmul(bank[4][32 * j:32 * j + 32, :], c_rep[:, k, :], ada_e[k][:, j, :], start=(k == 0), stop=(k == KD - 1))
                last.then_inc(ada_used, 1)

            def turn_rows(b, gr):
                for q in range(4):
                    last = t.transpose(b[:, q * P:(q + 1) * P], rows[:, gr % 2, q * P:(q + 1) * P], ident[:, :])
                return last

            pe.wait_ge(rows_ready, 1)
            turn_rows(bank[5], 0).then_inc(mix_cols, 1)

            def late(q):
                g, h, k = q // 16, q // 8 % 2, q % 8
                slot = q % 16 % NLATE[g]
                pe.wait_ge(late_in[g][slot], 16 * (q % 16 // NLATE[g] + 1))
                for j in range(4):
                    last = t.matmul(bank[7][32 * j:32 * j + 32, 256 * h:256 * h + 256], c_rep[:, k, :], ada_l[g][slot][:, j, :],
                                    start=(k == 0), stop=(k == KD - 1))
                last.then_inc(late_used, 1)

            def project(name, bks, hh):
                n = START[name] + hh
                pe.wait_ge(lo_done, n + 1)
                if name == "c":
                    pe.wait_ge(h_ready, hh + 1)
                for kk in range(2):
                    k = 2 * hh + kk
                    w = slice(kk * 512, kk * 512 + 512)
                    for tt in range(TT):
                        last = mm3(bank[bks[tt]][:, :], h_hi[:, k, tt * P:(tt + 1) * P], h_lo[:, k, tt * P:(tt + 1) * P],
                                   w_hi[:, n % NRING, w], w_lo[:, n % NRING, w], k == 0, k == KD - 1)
                last.then_inc(used, 1)
                for q in LATE_BEHIND.get(n, ()):
                    late(q)

            def t_bank(*use):
                n = T_AT[use]
                if n >= 2:
                    pe.wait_ge(t_drained, n - 1)
                return bank[4 + n % 2]

            def turn_kv(tt, kv):
                pe.wait_ge(copied, tt + 1)
                b = t_bank("c", tt, kv)
                for g in range(G):
                    last = t.transpose(b[:, g * P:(g + 1) * P], kcv[:, tt, kv * G + g].rearrange("p a d -> p (a d)"), ident[:, :])
                last.then_inc(t_filled, 1)

            def hidden(kv):
                if kv == 0:
                    t_bank("hid")
                    pe.wait_ge(cw1_in, 64)
                    pe.wait_ge(t_drained, T_AT["c", 1, 1] + 1)
                b = bank[4 + T_AT["hid",] % 2]
                for l in range(STRIDE):
                    last = t.matmul(b[:, kv * 64:kv * 64 + G * NC], cw1[:, kv, l, :], blocks[:, kv, l, :], start=(l == 0), stop=(l == STRIDE - 1))
                if kv:
                    last.then_inc(t_filled, 1)

            def turn_k(tt):
                pe.wait_ge(scaled, 3 + tt)
                b = t_bank("k", tt)
                for br in range(2):
                    for pr in range(NP):
                        last = t.transpose(b[:, (br * NP + pr) * P:(br * NP + pr + 1) * P], k_nat[:, tt, br, pr * P:(pr + 1) * P], ident[:, :])
                last.then_inc(t_filled, 1)

            for hh in range(4):
                project("c", (4, 6), hh)
            for hh in range(4):
                project("s", (0, 1), hh)
                turn_kv(hh // 2, hh % 2)
            for hh in range(4):
                project("w", (2, 3), hh)
                if hh in (1, 2):
                    hidden(hh - 1)
            pe.wait_ge(copied, 2)
            for hh in range(2):
                n = START["gates"] + hh
                pe.wait_ge(lo_done, n + 1)
                for kk in range(4):
                    k = 4 * hh + kk
                    w = slice(kk * 3 * H, (kk + 1) * 3 * H)
                    last = mm3(bank[6][0:3 * H, 0:SEQ], w_hi[:, n % NRING, w], w_lo[:, n % NRING, w], h_hi[:, k, :], h_lo[:, k, :],
                               k == 0, k == KD - 1)
                last.then_inc(used, 1)
            pe.wait_ge(copied, 4)
            pe.wait_ge(scaled, 2)
            for hh in range(4):
                project("q0", (0, 1), hh)
                if hh == 0:
                    pe.wait_ge(gates_done, 1)
                    b = t_bank("gates")
                    for tt in range(TT):
                        last = t.transpose(b[:, tt * 3 * H:(tt + 1) * 3 * H], gates_t[:, tt * P:(tt + 1) * P], ident[0:3 * H, 0:3 * H])
                    last.then_inc(t_filled, 1)
                if hh in (1, 2):
                    turn_k(hh - 1)
                if hh == 2:
                    pe.wait_ge(t_drained, T_AT["hid",] + 1)
                    pe.wait_ge(cw2_in, 16)
                    b = t_bank("cw2")
                    t.matmul(b[0:G * NC, 0:DK], gel[:, 0, :], cw2[:, 0, :], start=True, stop=True)
                    for g in range(G):
                        last = t.matmul(b[0:NC, DK + g * DK:DK + (g + 1) * DK], gel[:, 1, g * NC:(g + 1) * NC], cw2[:, 1, :], start=True, stop=True)
                    last.then_inc(t_filled, 1)
            pe.wait_ge(rows_ready, 2)
            for hh in range(2):
                project("q1", (6, 7), hh)
                if hh == 0:
                    pe.wait_ge(t_drained, T_AT["cw2",] + 1)
                    b = t_bank("kc")
                    t.transpose(b[:, 0:G * NC], kc_nat[:].rearrange("p a d -> p (a d)"), ident[0:G * NC, 0:G * NC]).then_inc(t_filled, 1)

            def queries(pr):
                for tt in range(TT):
                    b = t_bank("q", pr, tt)
                    pe.wait_ge(scaled, 5 + 2 * pr + tt)
                    for i in range(HG):
                        last = t.transpose(b[:, i * P:(i + 1) * P], q_nat[:, tt, i * P:(i + 1) * P], ident[:, :])
                    last.then_inc(t_filled, 1)

            def c_scores(pr):
                b = t_bank("cs", pr)
                for tt in range(TT):
                    for i in range(HG):
                        o = (tt * HG + i) * 2 * NC
                        last = t.matmul(b[:, o:o + 2 * NC], qT[:, pr, tt, i, :], kcT[:, pr, :, :].rearrange("p a n -> p (a n)"), start=True, stop=True)
                last.then_inc(t_filled, 1)

            def scores(m):
                pr, tt, i = STEPS[m]
                n = P * (tt + 1)
                if m >= 2:
                    pe.wait_ge(max_ready, 4 * (m - 1))
                for a in range(2):
                    last = t.matmul(bank[2 * (m % 2) + a][:, 0:2 * n].rearrange("p (b n) -> p b n", b=2), qT[64 * a:64 * a + 64, pr, tt, i, :],
                                    kT[64 * a:64 * a + 64, pr, :, 0:n], start=True, stop=True)
                last.then_inc(s_ready, 1)

            def turn(m):
                pr, tt, i = STEPS[m]
                pe.wait_ge(p_ready, m + 1)
                for bk in range(tt + 1):
                    b = t_bank("p", m, bk)
                    for q in range(4):
                        ab, kt = (q, 0) if tt == 0 else (2 * bk + q // 2, q % 2)
                        last = t.transpose(b[:, q * P:(q + 1) * P], prob[:, m % 4, ab, kt * P:(kt + 1) * P], ident[:, :])
                    last.then_inc(t_filled, 1)

            def turn_c(pr, tt):
                pe.wait_ge(cp_ready, pr + 1)
                for a in range(2):
                    b = t_bank("pc", pr, tt, a)
                    for i in range(HG):
                        last = t.transpose(b[0:NC, i * P:(i + 1) * P], cprob[:, pr, (a * TT + tt) * HG + i, :], ident[:, :])
                    last.then_inc(t_filled, 1)

            def values(pr, tt):
                n = pr * TT + tt
                if n == 0:
                    pe.wait_ge(scaled, 7)
                else:
                    pe.wait_ge(o_ready, n)
                pe.wait_ge(t_drained, T_AT["pc", pr, tt, 1] + 1)
                for br in range(2):
                    for kt in range(tt + 1):
                        for a in range(2):
                            gc = (2 * pr + a) * DK
                            t.matmul(bank[6][64 * a:64 * a + 64, :], v_nat[:, kt, br, gc:gc + DK], pt[tt][:, a, br, kt, :],
                                     start=(br == 0 and kt == 0), stop=False)
                for a in range(2):
                    last = t.matmul(bank[6][64 * a:64 * a + 64, :], vc[:, 2 * pr + a, :], pcT[:, a, :], start=False, stop=True)
                last.then_inc(pv_done, 1)

            def attention_out(ck, tiles):
                n = START["out"] + ck
                pe.wait_ge(lo_done, n + 1)
                pe.wait_ge(o_ready, TT * (ck // HG + 1))
                for tt in tiles:
                    for nb in range(NB):
                        w = slice(nb * 512, nb * 512 + 512)
                        last = mm3(bank[tt * NB + nb][:, :], o_hi[:, tt, ck, :], o_lo[:, tt, ck, :], w_hi[:, n % NRING, w], w_lo[:, n % NRING, w],
                                   ck == 0, ck == KD - 1)
                if 1 in tiles:
                    last.then_inc(used, 1)
                elif ck == KD - 1:
                    last.then_inc(y_done, 1)

            queries(0)
            for m in range(NS + LAG):
                if m == Q1_STEP:
                    queries(1)
                if m in (0, NS // 2):
                    pe.wait_ge(t_drained, T_AT["q", 2 * m // NS, 1] + 1)
                if m in C_STEP:
                    c_scores(C_STEP.index(m))
                if m == 0:
                    pe.wait_ge(scaled, 6)
                    pe.wait_ge(copied, 6)
                if m < NS:
                    scores(m)
                if m == NS:
                    pe.wait_ge(max_ready, 4 * NS)
                if m >= NS:
                    attention_out(m - NS, range(TT))
                if m in Q1_AT:
                    project("q1", (6, 7), Q1_AT[m])
                if m == Q1_STEP:
                    pe.wait_ge(scaled, 8)
                if m in LATE_STEP:
                    late(LATE_STEP[m][0])
                if m >= LAG:
                    pr, tt, i = STEPS[m - LAG]
                    turn(m - LAG)
                if m in LATE_STEP:
                    late(LATE_STEP[m][1])
                if m >= LAG:
                    if i == HG - 1:
                        turn_c(pr, tt)
                        values(pr, tt)
            for ck in range(LAG, HG):
                attention_out(ck, range(TT))
            for nb in range(NB):
                b = t_bank("gm", nb)
                t.matmul(b[:, :], ones[32 * nb:32 * nb + 1, :], rows[32 * nb:32 * nb + 1, 1, :], start=True, stop=True).then_inc(t_filled, 1)
            turn_rows(t_bank("shf"), 1).then_inc(t_filled, 1)
            pe.wait_ge(rows_ready, 3)
            turn_rows(t_bank("scf"), 0).then_inc(t_filled, 1)
            def turn_x(tt):
                for half in range(2):
                    pe.wait_ge(xn2_act if half else xn2_ready, tt + 1)
                    b = bank[4 + 2 * tt + half]
                    for k in range(4):
                        last = t.transpose(b[:, k * P:(k + 1) * P], xn[:, tt, (4 * half + k) * P:(4 * half + k + 1) * P], ident[:, :])
                    last.then_inc(xn2T, 1)

            pe.wait_ge(t_drained, T_AT["scf",] + 1)
            for tt in range(TT):
                for ck in range(HG, KD):
                    attention_out(ck, [tt])
                    if tt == 1 and ck == KD - 2:
                        turn_x(0)
            turn_x(1)

            def gate_up(j, what):
                f = int(what[1])
                r = slot_of(j, what)
                pe.wait_ge(lo_done, half_at(j, what) + 1)
                col = 0 if what[0] == "G" else 256
                w = [tensor[:, r, :].rearrange("p (k n) -> p k n", n=P) for tensor in (w_hi, w_lo)]
                for k in range(KD):
                    last = mm3(bank[4 + f][:, col:col + SEQ], w[0][:, k, :], w[1][:, k, :], h_hi[:, k, :], h_lo[:, k, :], k == 0, k == KD - 1)
                last.then_inc(used, 1)

            def down(j, what, first=False, final=False):
                f = int(what[1])
                r = slot_of(j, what)
                pe.wait_ge(lo_done, half_at(j, what) + 1)
                pe.wait_ge(a_ready, 2 * owner(j, what) + f + 1)
                for tt in range(TT):
                    for nb in range(NB):
                        w = slice(nb * 512, nb * 512 + 512)
                        last = mm3(bank[tt * NB + nb][:, :], act_hi[:, f, tt * P:(tt + 1) * P], act_lo[:, f, tt * P:(tt + 1) * P],
                                   w_hi[:, r, w], w_lo[:, r, w], first, final)
                    if final and tt == 0:
                        last.then_inc(y2_done, 1)
                last.then_inc(used, 1)

            def up_block(j, first=False):
                for what in (FIRST_BLOCK if first else BLOCK):
                    if what[0] == "D":
                        down(j, what, first=first)
                    else:
                        if what[0] == "G":
                            if not first:
                                pe.wait_ge(act_ready, 2 * j + int(what[1]) - 1)
                        gate_up(j, what)

            pe.wait_ge(h2_ready, 4)
            up_block(0, first=True)
            for j in range(1, NJ):
                up_block(j)
            for nb in range(NB):
                b = t_bank("gf", nb)
                pe.wait_ge(act_ready, 2 * NJ)
                j = 2 + nb
                t.matmul(b[:, :], ones[32 * j:32 * j + 1, :], rows[32 * j:32 * j + 1, 0, :], start=True, stop=True).then_inc(t_filled, 1)
            down(NJ, "D1", final=True)


_INS = ["x", "c", "ada_w", "ada_b", "norm_mix_w", "norm_ffn_w", "ffn_w_gate", "ffn_w_up", "ffn_w_down",
        "nsa_w_in", "nsa_cmp_pos", "nsa_cmp_w1", "nsa_cmp_w2", "nsa_qk_norm", "nsa_w_out"]


def kernel(**inputs):
    import numpy as _np
    import concourse.bacc as _bacc
    from concourse import mybir as _mybir
    from concourse.bass_utils import run_bass_kernel_spmd as _run

    nc = _bacc.Bacc("TRN2", target_bir_lowering=False, num_devices=1)
    arrays, args = {}, []
    for name in _INS:
        a = _np.ascontiguousarray(inputs[name])
        arrays[f"in_{name}"] = a
        args.append(nc.dram_tensor(f"in_{name}", a.shape, _mybir.dt.from_np(a.dtype), kind="ExternalInput").ap())
    args.append(nc.dram_tensor("out_0", inputs["x"].shape, _mybir.dt.float32, kind="ExternalOutput").ap())
    trunk_kernel(nc, *args)
    r = _run(nc, [arrays], core_ids=[0])
    return r.results[0]["out_0"]
```

```python
from contextlib import ExitStack

import concourse.bass as bass
from concourse import mybir

F32 = mybir.dt.float32
F32R = mybir.dt.float32r
ALU = mybir.AluOpType
ACT = mybir.ActivationFunctionType
AX_X = mybir.AxisListType.X

P = 128
MASKED = 1e30
HUGE = 3e38
EPS = 1e-6
GELU_C = 0.7978845608028654
GELU_A = 0.044715


def spread(ap, axis, n):
    ap = ap.unsqueeze(axis)
    shape = list(ap.shape)
    shape[axis] = n
    return ap.to_broadcast(shape)


def trunk_kernel(nc, x, c, ada_w, ada_b, norm_mix_w, norm_ffn_w, w_gate, w_up, w_down,
                 w_in, cmp_pos, cmp_w1, cmp_w2, qk_norm, w_out, out):
    _, SEQ, D = x.shape
    F = w_gate.shape[2]
    DK = qk_norm.shape[2]
    H = w_out.shape[1] // DK
    G = (w_in.shape[2] - H * DK - 3 * H) // (6 * DK)
    HG = H // G
    L = cmp_pos.shape[2]
    STRIDE = L // 2
    NC = (SEQ - L) // STRIDE + 1
    TT = SEQ // P
    KD = D // P
    NP = G // 2
    QD, KV = H * DK, G * DK
    NB = D // 512
    NJ = F // 256
    SCALE = float(DK) ** -0.5
    assert TT == 2 and KD == 8 and NP == 2 and DK == 64 and HG == 4 and L == 32 and F == NJ * 256

    HALF = 1024
    NRAW, NRING = 3, 6
    START = {"c": 0, "s": 4, "w": 8, "gates": 12, "q0": 14, "q1": 18, "out": 22}
    FFN0 = START["out"] + KD
    COLUMN = {"q0": 0, "q1": NP * HG * DK, "c": QD, "s": QD + 2 * KV, "w": QD + 4 * KV, "gates": QD + 6 * KV}
    NAT = {("s", 0): 0, ("s", 1): 1, ("w", 0): 2, ("w", 1): 3, ("q0", 0): 4, ("q0", 1): 5, ("q1", 0): 6, ("q1", 1): 7}
    ROOT = {use: n for n, use in enumerate(
        ["x", ("s", 0), ("s", 1), ("w", 0), ("w", 1), "kc", ("q0", 0), ("q0", 1), ("q1", 0), ("q1", 1),
         ("x2", 0), ("x2", 1)])}
    FIRST_BLOCK = ["G0", "U0", "G1", "U1", "D0"]
    BLOCK = ["G0", "U0", "D1", "G1", "U1", "D0"]

    def half_at(j, what):
        if isinstance(j, int) and j == 0:
            return FFN0 + FIRST_BLOCK.index(what)
        return FFN0 + 5 + 6 * (j - 1) + (0 if isinstance(j, int) and j == NJ else BLOCK.index(what))

    def slot_of(j, what):
        if isinstance(j, int):
            return half_at(j, what) % NRING
        return (FFN0 + 5 + BLOCK.index(what)) % NRING

    STEPS = [(pr, tt, i) for pr in range(NP) for tt in range(TT) for i in range(HG)]
    NS = len(STEPS)
    LAG = 3
    Q1_BEFORE = 2
    Q1_SQUARES, Q1_SUMS, Q1_ROOTS, Q1_SCALE = 1, 2, 2, 4
    Q1_STEP = 5
    LATE_AT = 7
    C_STEP = (2, NS // 2 + 1)
    X_BANK = (4, 0)
    AHEAD = {0: 22, 4: 23, 5: 24, 8: 25, 10: 26, 11: 27}
    LATE_BEHIND = {}
    for n, q in zip(range(START["s"], START["gates"]), ((0,), (1, 2), (3,), (4, 5), (6,), (7, 8), (9,), (10,))):
        LATE_BEHIND[n] = q
    for n, q in zip(range(START["q0"], START["q1"]), ((11, 12), (13,), (14,), (15,))):
        LATE_BEHIND[n] = q
    LATE_STEP = {LATE_AT + n: (16 + 2 * n, 17 + 2 * n) for n in range(8)}
    order = [("c", tt, kv) for tt in range(TT) for kv in range(2)]
    order += [("hid",), ("gates",), ("k", 0), ("k", 1), ("cw2",), ("q", 0, 0), ("q", 0, 1)]
    for m in range(NS + LAG):
        if m == 0:
            order += [("kc",)]
        if m >= LAG:
            pr, tt, i = STEPS[m - LAG]
            order += [("p", m - LAG, b) for b in range(tt + 1)]
        if m in C_STEP:
            order += [("cs", C_STEP.index(m))]
    order += [("gm", 0), ("gm", 1), ("shf",), ("scf",), ("gf", 0), ("gf", 1)]
    T_AT = {use: n for n, use in enumerate(order)}

    with ExitStack() as ctx:
        def sem(name):
            return ctx.enter_context(nc.semaphore(name))

        base = (nc.sbuf_base + 31) // 32 * 32
        here = [base]

        def sized(shape):
            n = 4
            for s in shape[1:]:
                n *= s
            return (n + 31) // 32 * 32

        def at(name, shape, offset, dt=F32):
            return nc.alloc_sbuf_tensor_at(name, shape, dt, offset=offset)

        def sb(name, shape, dt=F32):
            offset = here[0]
            here[0] += sized(shape)
            return at(name, shape, offset, dt)

        def region(nbytes):
            offset = here[0]
            here[0] += nbytes
            return offset

        x_sb = sb("x_sb", [P, TT, D])
        raw = sb("raw", [P, NRAW, 2 * HALF])
        w_hi = sb("w_hi", [P, NRING, HALF], F32R)
        w_lo = sb("w_lo", [P, NRING, HALF], F32R)
        r_h = region(16384)
        h_hi = at("h_hi", [P, KD, SEQ], r_h, F32R)
        h_lo = at("h_lo", [P, KD, SEQ], r_h + 8192, F32R)
        pcT = at("pcT", [2 * NC, HG * P], r_h + 12288)
        ident = sb("ident", [P, P])
        ones = sb("ones", [P, P])
        W_MIX, W_FFN, SC_MIX, SH_MIX, SC_FFN, SH_FFN, C_IN, C_ACT = range(8)
        cols = sb("cols", [P, 8, KD])
        c_rep = sb("c_rep", [P, KD, 32])
        rows = sb("rows", [P, 2, 512])
        ada_bias = sb("ada_bias", [P, 512])
        sums = sb("sums", [P, 12, 8])
        roots = sb("roots", [P, 12, 8])
        minus_half = sb("minus_half", [P, 8])
        cw2 = sb("cw2", [P, 2, DK])
        qk_col = sb("qk_col", [P, 4])
        pos_col = sb("pos_col", [P, 2, STRIDE])
        norm_nat = sb("norm_nat", [8, 2, P])
        gates = sb("gates", [P, TT, 3 * H])
        den = sb("den", [P, 4, 4])
        recip = sb("recip", [P, 4, 4])
        weight = sb("weight", [P, 4, 4])
        negmax = sb("negmax", [P, 4, 4])
        qk_nat = sb("qk_nat", [4, 2, DK])
        pos_nat = sb("pos_nat", [2 * STRIDE, 2, DK])
        gel = sb("gel", [P, 2, 60])
        gel_t = sb("gel_t", [P, 2, 60])
        kcT = sb("kcT", [P, NP, 2, NC])
        kc_nat = sb("kc_nat", [G * NC, 2, DK])
        vc = sb("vc", [2 * NC, NP, 2, DK])
        own_rows = sb("own_rows", [2 * NC, 2])
        cmask = sb("cmask", [P, TT * HG, NC])
        cbias = sb("cbias", [P, NP, 2, TT * HG, NC])
        cprob = sb("cprob", [P, NP, TT * HG, 2, NC])
        cstat = sb("cstat", [P, 4, 2 * TT * HG])
        cdist = sb("cdist", [P, TT, NC])
        kT = sb("kT", [P, NP, 2, SEQ])
        v_nat = sb("v_nat", [P, TT, 2, KV])

        r_q = region(4096)
        q_nat = at("q_nat", [P, TT, 512], r_q)
        gates_t = at("gates_t", [3 * H, SEQ], r_q)
        gm_b = at("gm_b", [P, D], r_q)
        r_qT = region(8192)
        qT = at("qT", [P, NP, TT, HG, P], r_qT)
        r_bias = region(16384)
        bias = at("bias", [P, H, 2 * P], r_bias)
        gf_b = at("gf_b", [P, D], r_bias)
        r_o = region(16384)
        o_hi = at("o_hi", [P, TT, KD, P], r_o, F32R)
        o_lo = at("o_lo", [P, TT, KD, P], r_o + 8192, F32R)
        sq = at("sq", [P, 2, 512], r_o)
        kcv = at("kcv", [P, TT, 2 * G, 2, DK], r_o + 8192)
        k_nat = at("k_nat", [P, TT, 2, KV], r_o + 4096)
        out_sb = at("out_sb", [P, TT, D], r_o + 8192)
        r_p = region(16384)
        prob = at("prob", [P, 4, 4, 2 * P], r_p)
        xn = at("xn", [P, TT, D], r_p)
        h_f = at("h_f", [P, KD, SEQ], r_p + 8192)
        NLATE = (4, 3)
        ada_l = [[at(f"ada_late{g}_{i}", [P, 4, 256], (r_p, r_h)[g] + 4096 * i) for i in range(NLATE[g])] for g in range(2)]
        r_pt = region(24576)
        cw1 = at("cw1", [P, 2, STRIDE, P], r_pt)
        blocks = at("blocks", [P, 2, STRIDE, G * NC], r_pt + 16384)
        pt = [at("pt0", [P, 2, 2, 1, HG * P], r_pt + 16384), at("pt1", [P, 2, 2, 2, HG * P], r_pt)]
        ada_e = [at(f"ada_e{k}", [P, 4, 512], offset) for k, offset in enumerate(
            [r_bias, r_bias + 8192, r_o, r_o + 8192, r_qT, r_pt, r_pt + 8192, r_pt + 16384])]
        th = at("th", [P, 2, 256], r_pt)
        sg = at("sg", [P, 2, 256], r_pt + 2048)
        act_f = at("act_f", [P, 2, 256], r_pt + 4096)
        act_hi = at("act_hi", [P, 2, 256], r_pt + 6144, F32R)
        act_lo = at("act_lo", [P, 2, 256], r_pt + 8192, F32R)
        mixed = at("mixed", [P, 2, 512], r_pt + 10240)
        assert here[0] <= nc.sbuf_usable_end, here[0]

        bank = [ctx.enter_context(nc.psum_tensor(f"bank{i}", [P, 512], F32)) for i in range(8)]

        x_in = [sem(f"x_in{t}") for t in range(TT)]
        c_in, norm_in, qk_in, pos_in, cw2_in, cw1_in = (sem(n) for n in ("c_in", "norm_in", "qk_in", "pos_in", "cw2_in", "cw1_in"))
        bias_in = [sem(f"bias_in{g}") for g in range(3)]
        ada_in = [sem(f"ada_in{k}") for k in range(KD)]
        late_in = [[sem(f"late_in{g}_{i}") for i in range(NLATE[g])] for g in range(2)]
        raw_in = [sem(f"raw_in{i}") for i in range(NRAW)]
        d1_in = sem("d1_in")
        hi_done, lo_done, used = sem("hi_done"), sem("lo_done"), sem("used")
        consts = sem("consts")
        bias_ready = sem("bias_ready")
        dve = sem("dve")
        own = sem("own")
        pool = sem("pool")
        c_tanh, c_ready, sq_x = sem("c_tanh"), sem("c_ready"), sem("sq_x")
        params_t, cols_ready = sem("params_t"), sem("cols_ready")
        x2_ready, x2_squared, xn2_act = sem("x2_ready"), sem("x2_squared"), sem("xn2_act")
        var_ready, root_ready = sem("var_ready"), sem("root_ready")
        xn_ready, xnT, gates_done = sem("xn_ready"), sem("xnT"), sem("gates_done")
        ada_used, rows_ready, mix_cols = sem("ada_used"), sem("rows_ready"), sem("mix_cols")
        hf_ready, hhi_ready, h_ready = sem("hf_ready"), sem("hhi_ready"), sem("h_ready")
        copied, squared, scaled = sem("copied"), sem("squared"), sem("scaled")
        gates_ready = sem("gates_ready")
        t_filled, t_drained = sem("t_filled"), sem("t_drained")
        gel_sq, gel_in, gel_tanh, gel_ready, kc_sum, kc_ready = (sem(n) for n in ("gel_sq", "gel_in", "gel_tanh", "gel_ready", "kc_sum", "kc_ready"))
        s_ready, max_ready, exp_ready, weight_ready, p_ready = (sem(n) for n in ("s_ready", "max_ready", "exp_ready", "weight_ready", "p_ready"))
        cs_ready, ce_ready, cp_ready = sem("cs_ready"), sem("ce_ready"), sem("cp_ready")
        pv_done, ohi_ready, o_ready = sem("pv_done"), sem("ohi_ready"), sem("o_ready")
        q_turned, q_taken = sem("q_turned"), sem("q_taken")
        pc_turned, pc_taken = sem("pc_turned"), sem("pc_taken")
        late_used = sem("late_used")
        y_done = sem("y_done")
        xn2_ready, xn2T, h2f_ready, h2hi_ready, h2_ready = (sem(n) for n in ("xn2_ready", "xn2T", "h2f_ready", "h2hi_ready", "h2_ready"))
        th_ready, act_ready, ahi_ready, a_ready = (sem(n) for n in ("th_ready", "act_ready", "ahi_ready", "a_ready"))
        y2_done, out_ready, out_done = sem("y2_done"), sem("out_ready"), sem("out_done")

        def unit_of(n):
            return n // 2

        def raw_half(n, width=HALF):
            return raw[:, unit_of(n) % NRAW, (n % 2) * width:(n % 2 + 1) * width]

        def raw_ffn(what):
            slot = (START["out"] + KD) // 2 % NRAW + "GUD".index(what[0])
            f = int(what[1])
            if what[0] == "D":
                return raw[:, slot % NRAW, f * HALF:(f + 1) * HALF]
            return raw[:, slot % NRAW, :].rearrange("p (k n) -> p k n", n=256)[:, :, f * P:(f + 1) * P]

        def split_parts(tensor, slot, what):
            v = tensor[:, slot, :]
            return v if what[0] == "D" else v.rearrange("p (k n) -> p k n", n=P)

        def owner(j, what):
            return j - 1 if what == "D1" else j

        def width_of(n):
            return KD // 2 * 3 * H if START["gates"] <= n < START["q0"] else HALF

        block = ctx.enter_context(nc.Block())

        @block.sync
        def _(sp):
            sp.dma_start(cols[:, C_IN, :], c[0].rearrange("(p k) -> p k", k=KD)).then_inc(c_in, 16)
            for t in range(TT):
                sp.dma_start(x_sb[:, t, :], x[0, t * P:(t + 1) * P, :]).then_inc(x_in[t], 16)
            ada_v = ada_w[0].rearrange("(p k) n -> p k n", k=KD)

            def load(u, src, cols_of=2 * HALF, shape=None):
                dst = raw[:, u % NRAW, 0:cols_of]
                if shape:
                    dst = dst.rearrange("p (k n) -> p k n", n=shape)
                sp.dma_start(dst, src).then_inc(raw_in[u % NRAW], 16)

            def free(u):
                if u >= NRAW:
                    sp.wait_ge(lo_done, 2 * (u - NRAW) + 2)

            def small_loads(k):
                if k == 0:
                    for a, w in enumerate((norm_mix_w, norm_ffn_w)):
                        sp.dma_start(norm_nat[:, a, :], w[0].rearrange("(k p) -> k p", p=P)).then_inc(norm_in, 16)
                    for a in range(2):
                        sp.dma_start(qk_nat[:, a, :], qk_norm[0]).then_inc(qk_in, 16)
                    for kv in range(2):
                        sp.dma_start(pos_nat[STRIDE * kv:STRIDE * (kv + 1), :, :],
                                     cmp_pos[0, kv].rearrange("(a l) d -> l a d", a=2)).then_inc(pos_in, 16)
                if k == 1:
                    for j in range(4):
                        sp.dma_start(ada_bias[32 * j:32 * j + 32, :],
                                     ada_b[0:1, 512 * j:512 * j + 512].to_broadcast([32, 512])).then_inc(bias_in[0], 16)
                    sp.dma_start(cw2[:], cmp_w2[0].rearrange("v f d -> f v d")).then_inc(cw2_in, 16)

            for k in range(KD):
                small_loads(k)
                sp.dma_start(ada_e[k][:], ada_v[:, k, 0:2048].rearrange("p (j n) -> p j n", j=4)).then_inc(ada_in[k], 16)

            w_in_v = w_in[0].rearrange("(k p) n -> p k n", p=P)

            def load_in(name, part):
                u = START[name] // 2 + part
                free(u)
                if name == "gates":
                    load(u, w_in_v[:, :, COLUMN[name]:COLUMN[name] + 3 * H], KD * 3 * H, 3 * H)
                else:
                    load(u, w_in_v[:, 4 * part:4 * part + 4, COLUMN[name]:COLUMN[name] + 512], shape=512)

            def load_out(part):
                u = START["out"] // 2 + part
                free(u)
                pr, i = part // 2, 2 * (part % 2)
                v = w_out[0].rearrange("(r a i d) n -> r a d i n", r=NP, a=2, i=HG)
                for a in range(2):
                    sp.dma_start(raw[64 * a:64 * a + 64, u % NRAW, :].rearrange("p (i n) -> p i n", i=2),
                                 v[pr, a, :, i:i + 2, :]).then_inc(raw_in[u % NRAW], 8 * 2)

            def load_late(q):
                g, h, k = q // 16, q // 8 % 2, q % 8
                n, slot = q % 16, q % 16 % NLATE[g]
                if n >= NLATE[g]:
                    sp.wait_ge(late_used, q - NLATE[g] + 1)
                elif g == 0:
                    sp.wait_ge(h_ready, 4)
                else:
                    sp.wait_ge(used, START["out"])
                src = ada_v[:, k, 2048 * (g + 1):2048 * (g + 2)].rearrange("p (j n) -> p j n", j=4)[:, :, 256 * h:256 * h + 256]
                sp.dma_start(ada_l[g][slot][:], src).then_inc(late_in[g][slot], 16)

            for part in range(2):
                load_in("c", part)
            load_in("s", 0)
            w1_v = cmp_w1[0].rearrange("v (a l d) f -> v a d l f", a=2, l=STRIDE)
            sp.wait_ge(ada_used, KD)
            for kv in range(2):
                for a in range(2):
                    sp.dma_start(cw1[64 * a:64 * a + 64, kv, :, :], w1_v[kv, a]).then_inc(cw1_in, 16)
            for q in range(2):
                load_late(q)
            load_in("s", 1)
            for q in range(2, 5):
                load_late(q)
            load_in("w", 0)
            for q in range(5, 8):
                load_late(q)
            load_in("w", 1)
            for q in range(8, 10):
                load_late(q)
            load_in("gates", 0)
            load_late(10)
            load_in("q0", 0)
            for q in range(11, 14):
                load_late(q)
            load_in("q0", 1)
            for q in range(14, 16):
                load_late(q)
            for part in range(2):
                load_in("q1", part)
            for part in range(3):
                load_out(part)

            def load_ffn(j, what):
                if isinstance(j, int) and j == 0:
                    free(FFN0 // 2 + "GUD".index(what[0]))
                elif what == "D1":
                    sp.wait_ge(lo_done, half_at(j, "D1") + 1)
                else:
                    sp.wait_ge(lo_done, half_at(j - 1, {"G": "G1", "U": "U1", "D0": "D0"}[what]) + 1)
                slot = (FFN0 // 2 + "GUD".index(what[0])) % NRAW
                if what[0] == "D":
                    f = int(what[1])
                    sp.dma_start(raw[:, slot, f * HALF:(f + 1) * HALF],
                                 w_down[0].rearrange("(j f p) n -> j f p n", f=2, p=P)[j, f]).then_inc(d1_in if f else raw_in[slot], 16)
                else:
                    w = w_gate if what == "G" else w_up
                    src = w[0].rearrange("(k p) (j n) -> j p k n", p=P, n=256)[j]
                    sp.dma_start(raw[:, slot, :].rearrange("p (k n) -> p k n", n=256), src).then_inc(raw_in[slot], 16)

            for q in range(16, 32):
                load_late(q)
            load_out(3)
            load_ffn(0, "G")
            load_ffn(0, "U")
            load_ffn(0, "D0")
            load_ffn(0, "D1")
            for what in ("G", "U", "D0"):
                load_ffn(1, what)
            with sp.Fori(2, NJ) as j:
                load_ffn(j - 1, "D1")
                for what in ("G", "U", "D0"):
                    load_ffn(j, what)
            load_ffn(NJ - 1, "D1")

            for tt in range(TT):
                for nb in range(NB):
                    sp.wait_ge(out_ready, tt * NB + nb + 1)
                    sp.dma_start(out[0, tt * P:(tt + 1) * P, nb * 512:nb * 512 + 512],
                                 out_sb[:, tt, nb * 512:nb * 512 + 512]).then_inc(out_done, 16)
            sp.wait_ge(out_done, 16 * TT * NB)

        @block.gpsimd
        def _(gp):
            g = nc.gpsimd
            n_pool = [0]

            def link(ins):
                n_pool[0] += 1
                ins.then_inc(pool, 1)
                gp.wait_ge(pool, n_pool[0])

            g.memset(minus_half[:], -0.5)
            g.memset(ones[:], 1.0)
            g.memset(kcT[:], 0.0)
            link(g.memset(own_rows[:], 1.0))
            g.affine_select(out=own_rows[:, 0:1], in_=own_rows[:, 0:1], compare_op=ALU.is_ge, fill=0.0, base=NC - 1,
                            pattern=[[0, 1]], channel_multiplier=-1)
            g.affine_select(out=own_rows[:, 1:2], in_=own_rows[:, 1:2], compare_op=ALU.is_ge, fill=0.0, base=-NC,
                            pattern=[[0, 1]], channel_multiplier=1)
            link(g.memset(ident[:], 0.0))
            g.affine_select(out=ident[:], in_=ident[:], compare_op=ALU.not_equal, fill=1.0, base=0,
                            pattern=[[-1, P]], channel_multiplier=1).then_inc(consts, 1)

            def root(use, n, parts=P):
                k = ROOT[use]
                gp.wait_ge(var_ready, k + 1)
                g.tensor_tensor(roots[0:parts, k, 0:n], sums[0:parts, k, 0:n], minus_half[0:parts, 0:n], ALU.pow).then_inc(root_ready, 1)

            root("x", TT)
            slope = [2.0 ** (-8.0 * (h + 1) / H) for h in range(H)]
            link(g.iota(cdist[:], pattern=[[P, TT], [-STRIDE, NC]], base=1 - L, channel_multiplier=1,
                        allow_small_or_imprecise_dtypes=True))
            for h in range(H):
                pr, a, i = h // (2 * HG), h // HG % 2, h % HG
                for tt in range(TT):
                    last = g.tensor_scalar(cbias[:, pr, a, tt * HG + i, :], cdist[:, tt, :], slope[h], 0.0, ALU.mult, ALU.add)
            link(last)
            link(g.memset(cmask[:], 1.0))
            g.affine_select(out=cmask[:].rearrange("p (t i) n -> p t i n", t=TT), in_=cmask[:].rearrange("p (t i) n -> p t i n", t=TT),
                            compare_op=ALU.is_ge, fill=0.0, base=1 - L, pattern=[[P, TT], [0, HG], [-STRIDE, NC]], channel_multiplier=1)
            for pr in range(NP):
                v = cbias[:, pr].rearrange("p a (t i) n -> p a t i n", t=TT)
                for a in range(2):
                    last = g.affine_select(out=v[:, a], in_=v[:, a], compare_op=ALU.is_ge, fill=MASKED, base=1 - L,
                                           pattern=[[P, TT], [0, HG], [-STRIDE, NC]], channel_multiplier=1)
            link(last)
            gp.wait_ge(ada_used, KD)
            link(g.iota(bias[:, H - 1, :], pattern=[[-1, 2 * P]], base=P, channel_multiplier=1,
                        allow_small_or_imprecise_dtypes=True))
            for h in range(H):
                last = g.tensor_scalar(bias[:, h, :], bias[:, H - 1, :], slope[h], 0.0, ALU.mult, ALU.add)
            link(last)
            for h in range(0, H, HG):
                last = g.affine_select(out=bias[:, h:h + HG, :], in_=bias[:, h:h + HG, :], compare_op=ALU.is_ge, fill=MASKED, base=P,
                                       pattern=[[0, HG], [-1, 2 * P]], channel_multiplier=1)
            last.then_inc(bias_ready, 1)

            root(("s", 0), G)
            root(("s", 1), G)
            root(("w", 0), G)
            root(("w", 1), G)
            root("kc", 1, G * NC)
            root(("q0", 0), 2 * HG)
            root(("q0", 1), 2 * HG)

            def normalise(m):
                n = P * (STEPS[m][1] + 1)
                gp.wait_ge(weight_ready, m + 1)
                for ab in range(4):
                    last = g.tensor_scalar(prob[:, m % 4, ab, 0:n], prob[:, m % 4, ab, 0:n], weight[:, m % 4, ab:ab + 1], 1.0,
                                           ALU.mult, ALU.mult)
                last.then_inc(p_ready, 1)

            for m in range(NS):
                if m == Q1_ROOTS:
                    root(("q1", 0), 2 * HG)
                    root(("q1", 1), 2 * HG)
                normalise(m)
            root(("x2", 0), 1)
            root(("x2", 1), 1)

        @block.scalar
        def _(act):
            s = nc.scalar
            def load_bias(gr):
                for j in range(4):
                    b = 4 * gr + j
                    act.dma_start(ada_bias[32 * j:32 * j + 32, :],
                                  ada_b[0:1, 512 * b:512 * b + 512].to_broadcast([32, 512])).then_inc(bias_in[gr], 16)

            act.wait_ge(c_in, 16)
            s.activation(cols[:, C_ACT, :], cols[:, C_IN, :], ACT.Tanh, scale=0.5).then_inc(c_tanh, 1)

            n_own = [0]

            def hi(n):
                w = width_of(n)
                act.wait_ge(raw_in[unit_of(n) % NRAW], raw_target(n))
                if n >= NRING:
                    act.wait_ge(used, n - NRING + 1)
                s.activation(w_hi[:, n % NRING, 0:w], raw_half(n, w), ACT.Copy).then_inc(hi_done, 1)

            def raw_target(n):
                u = unit_of(n)
                return 16 * sum(2 if START["out"] // 2 <= v < FFN0 // 2 else 1 for v in range(u % NRAW, u + 1, NRAW))

            def hi_ffn(j, what):
                o = owner(j, what)
                slot = (FFN0 // 2 + "GUD".index(what[0])) % NRAW
                if what == "D1":
                    act.wait_ge(d1_in, 16 * (o + 1))
                else:
                    act.wait_ge(raw_in[slot], ffn_target(slot, o))
                n = half_at(j, what)
                act.wait_ge(used, n - NRING + 1)
                r = slot_of(j, what)
                s.activation(split_parts(w_hi, r, what), raw_ffn(what), ACT.Copy).then_inc(hi_done, 1)

            def ffn_target(slot, o):
                before = 16 * sum(2 if START["out"] // 2 <= v < FFN0 // 2 else 1 for v in range(slot, FFN0 // 2, NRAW))
                return before + 16 * (o + 1)

            DONE = {name: START[name] + (2 if name == "gates" else 4) for name in START}
            PREV = dict(zip(list(NAT)[2:], list(NAT)))

            def square(name, tt, bk, width):
                act.wait_ge(used, DONE[name])
                if (name, tt) in PREV:
                    act.wait_ge(var_ready, ROOT[PREV[name, tt]] + 1)
                s.activation(sq[:, NAT[name, tt] % 2, 0:width], bank[bk][:, 0:width], ACT.Square).then_inc(squared, 1)

            def keys(name, tt, bk, br):
                square(name, tt, bk, KV)
                s.activation(v_nat[:, tt, br, :], bank[bk][:, KV:2 * KV], ACT.Copy).then_inc(copied, 1)

            hi(0)
            for i in range(4):
                if i % 2 == 0:
                    act.wait_ge(cols_ready, 1)
                    act.wait_ge(xnT, i + 1)
                    for k in (2 * i, 2 * i + 1):
                        last = s.activation(h_f[:, k, :], bank[i][:, (k % 2) * 256:(k % 2) * 256 + 256], ACT.Identity,
                                            scale=cols[:, SC_MIX, k:k + 1], bias=cols[:, SH_MIX, k:k + 1])
                    n_own[0] += 1
                    last.then_inc(own, 1)
                    act.wait_ge(own, n_own[0])
                else:
                    act.wait_ge(hf_ready, i // 2 + 1)
                s.activation(h_hi[:, 2 * i:2 * i + 2, :], h_f[:, 2 * i:2 * i + 2, :], ACT.Copy).then_inc(hhi_ready, 1)
                if i == 0:
                    hi(1)
            for n in range(2, 7):
                hi(n)
            act.wait_ge(rows_ready, 1)
            load_bias(1)
            act.wait_ge(used, DONE["c"])
            for tt in range(TT):
                s.activation(kcv[:, tt], spread(bank[4 + 2 * tt][:, :].rearrange("p (g d) -> p g d", d=DK), 2, 2), ACT.Copy).then_inc(copied, 1)
            for n in range(7, 12):
                hi(n)
            for tt in range(TT):
                keys("s", tt, tt, 0)
            for n in range(12, 15):
                hi(n)
            act.wait_ge(t_filled, T_AT["hid",] + 1)
            hid = bank[4 + T_AT["hid",] % 2][:, 0:128].rearrange("p (v n) -> p v n", v=2)[:, :, 0:G * NC]
            s.activation(gel_t[:], hid, ACT.Square).then_inc(gel_sq, 1)
            for n in range(15, 16):
                hi(n)
            act.wait_ge(gel_in, 1)
            s.activation(gel_t[:], gel_t[:], ACT.Tanh, scale=GELU_C).then_inc(gel_tanh, 1)
            for tt in range(TT):
                keys("w", tt, 2 + tt, 1)
            hi(16)
            act.wait_ge(used, DONE["gates"])
            s.activation(gates_t[:], bank[6][0:3 * H, 0:SEQ], ACT.Tanh, scale=0.5).then_inc(gates_done, 1)
            for n in range(17, 20):
                hi(n)
            act.wait_ge(t_filled, T_AT["cw2",] + 1)
            kcb = bank[4 + T_AT["cw2",] % 2]
            s.activation(kc_nat[:, 0, :], kcb[0:G * NC, 0:DK], ACT.Square, accum_out=sums[0:G * NC, ROOT["kc"], 1:2]).then_inc(kc_sum, 1)
            for n in range(20, 22):
                hi(n)
            for tt in range(TT):
                square("q0", tt, tt, 512)
            act.wait_ge(rows_ready, 2)
            load_bias(2)

            def c_exp(pr):
                act.wait_ge(cs_ready, pr + 1)
                s.activation(cprob[:, pr], cprob[:, pr], ACT.Exp, scale=-1.0).then_inc(ce_ready, 1)

            def exps(m):
                n = P * (STEPS[m][1] + 1)
                for ab in range(4):
                    act.wait_ge(max_ready, 4 * m + ab + 1)
                    v = prob[:, m % 4, ab, 0:n]
                    s.activation(v, v, ACT.Exp, bias=negmax[:, m % 4, ab:ab + 1], scale=-1.0,
                                 accum_out=den[:, m % 4, ab:ab + 1]).then_inc(exp_ready, 1)

            def queries():
                for tt in range(TT):
                    act.wait_ge(q_turned, tt + 1)
                    s.activation(qT[:, 1, tt], bank[6 + tt][:, :].rearrange("p (i n) -> p i n", i=HG), ACT.Copy, scale=qk_col[:, 0:1]).then_inc(q_taken, 1)

            def take_pc(n):
                act.wait_ge(pc_turned, n + 1)
                if n:
                    act.wait_ge(pv_done, n)
                s.activation(pcT[:], bank[6][0:2 * NC, :], ACT.Copy).then_inc(pc_taken, 1)

            def o_part(v):
                pr, tt = v // TT, v % TT
                act.wait_ge(pv_done, v + 1)
                s.activation(o_hi[:, tt, HG * pr:HG * pr + HG, :], bank[6][:, :].rearrange("p (i n) -> p i n", i=HG),
                             ACT.Copy).then_inc(ohi_ready, 1)

            for m in range(NS + LAG):
                if m - 1 in C_STEP:
                    c_exp(C_STEP.index(m - 1))
                if m < NS:
                    exps(m)
                if m == Q1_STEP:
                    queries()
                if m >= LAG and (m - LAG) % HG == HG - 1:
                    take_pc((m - LAG) // HG)
                if m in AHEAD:
                    hi(AHEAD[m])
                if m == Q1_SQUARES:
                    for tt in range(TT):
                        square("q1", tt, 6 + tt, 512)
                if m - LAG > HG and (m - LAG) % HG == 1:
                    o_part((m - LAG) // HG - 1)
            o_part(NP * TT - 1)
            for n in (28, 29):
                hi(n)
            for what in FIRST_BLOCK[0:2]:
                hi_ffn(0, what)

            def square_x(tt):
                for nb in range(NB):
                    act.wait_ge(x2_ready, tt * NB + nb + 1)
                    s.activation(xn[:, tt, nb * 512:nb * 512 + 512], x_sb[:, tt, nb * 512:nb * 512 + 512], ACT.Square,
                                 accum_out=sums[:, ROOT["x2", tt], 4 + nb:5 + nb]).then_inc(x2_squared, 1)

            def scale_x(tt, half):
                act.wait_ge(root_ready, ROOT["x2", tt] + 1)
                hs = slice(512 * half, 512 * half + 512)
                s.activation(xn[:, tt, hs], x_sb[:, tt, hs], ACT.Copy, scale=roots[:, ROOT["x2", tt], 0:1]).then_inc(xn2_act if half else xn2_ready, 1)

            def modulate_x(tt):
                ts = slice(tt * P, (tt + 1) * P)
                act.wait_ge(xn2T, 2 * tt + 2)
                for k in range(4, 8):
                    last = s.activation(h_f[:, k, ts], bank[X_BANK[tt] + 1][:, (k % 4) * P:(k % 4 + 1) * P], ACT.Identity,
                                        scale=cols[:, SC_FFN, k:k + 1], bias=cols[:, SH_FFN, k:k + 1])
                last.then_inc(own, 1)

            def hi_x(tt, half):
                ts = slice(tt * P, (tt + 1) * P)
                ks = slice(4 * half, 4 * half + 4)
                if half:
                    act.wait_ge(own, n_own[0] + tt + 1)
                else:
                    act.wait_ge(h2f_ready, tt + 1)
                s.activation(h_hi[:, ks, ts], h_f[:, ks, ts], ACT.Copy).then_inc(h2hi_ready, 1)

            square_x(0)
            scale_x(0, 1)
            modulate_x(0)
            square_x(1)
            for half in range(2):
                scale_x(1, half)
            hi_x(0, 1)
            hi_x(0, 0)
            modulate_x(1)
            hi_x(1, 1)
            hi_x(1, 0)
            for what in FIRST_BLOCK[2:]:
                hi_ffn(0, what)

            def act_gate(j, f):
                act.wait_ge(used, half_at(j, f"U{f}") + 1)
                s.activation(th[:, f, :], bank[4 + f][:, 0:256], ACT.Tanh, scale=0.5).then_inc(th_ready, 1)
                act.wait_ge(act_ready, 2 * j + f + 1)
                s.activation(act_hi[:, f, :], act_f[:, f, :], ACT.Copy).then_inc(ahi_ready, 1)

            act_gate(0, 0)
            for what in ("G0", "U0"):
                hi_ffn(1, what)
            act_gate(0, 1)
            hi_ffn(1, "D1")

            def act_block(j):
                for what in ("G1", "U1", "D0"):
                    hi_ffn(j, what)
                act_gate(j, 0)
                for what in ("G0", "U0"):
                    hi_ffn(j + 1, what)
                act_gate(j, 1)
                hi_ffn(j + 1, "D1")

            with act.Fori(1, NJ - 1) as j:
                act_block(j)
            j = NJ - 1
            for what in ("G1", "U1", "D0"):
                hi_ffn(j, what)
            act_gate(j, 0)
            hi_ffn(NJ, "D1")
            act_gate(j, 1)

        @block.vector
        def _(ve):
            v = nc.vector
            n_dve = [0]

            def link(ins):
                n_dve[0] += 1
                ins.then_inc(dve, 1)
                ve.wait_ge(dve, n_dve[0])

            def mean_eps(use, n, size, parts=P):
                v.tensor_scalar(sums[0:parts, ROOT[use], 0:n], sums[0:parts, ROOT[use], 0:n], 1.0 / size, EPS,
                                ALU.mult, ALU.add).then_inc(var_ready, 1)

            for t in range(TT):
                ve.wait_ge(x_in[t], 16)
                link(v.tensor_tensor_reduce(xn[:, t, :], x_sb[:, t, :], x_sb[:, t, :], 1.0, 0.0, ALU.mult, ALU.add,
                                            sums[:, ROOT["x"], t:t + 1]))
            mean_eps("x", TT, D)
            ve.wait_ge(c_tanh, 1)
            link(v.tensor_scalar(cols[:, C_ACT, :], cols[:, C_ACT, :], 0.5, 0.5, ALU.mult, ALU.add))
            link(v.tensor_tensor(cols[:, C_ACT, :], cols[:, C_ACT, :], cols[:, C_IN, :], ALU.mult))
            v.tensor_copy(c_rep[:], spread(cols[:, C_ACT, :], 2, 32)).then_inc(c_ready, 1)
            ve.wait_ge(root_ready, ROOT["x"] + 1)
            for t in range(TT):
                v.tensor_scalar(xn[:, t, :], x_sb[:, t, :], roots[:, ROOT["x"], t:t + 1], None, ALU.mult).then_inc(xn_ready, 1)
            ve.wait_ge(params_t, 1)
            pb = bank[5]
            v.tensor_copy(cols[:, W_MIX:W_FFN + 1, :], pb[:, 0:16].rearrange("p (a k) -> p a k", a=2))
            v.tensor_scalar(qk_col[:, 0:1], pb[:, 16:17], -SCALE, None, ALU.mult)
            v.tensor_copy(qk_col[:, 1:4], pb[:, 17:20])
            link(v.tensor_copy(pos_col[:], pb[:, 32:64].rearrange("p (a k) -> p a k", a=2)))

            def lo(n):
                w = width_of(n)
                ve.wait_ge(hi_done, n + 1)
                v.tensor_tensor(w_lo[:, n % NRING, 0:w], raw_half(n, w), w_hi[:, n % NRING, 0:w].bitcast(F32), ALU.subtract).then_inc(lo_done, 1)

            def lo_ffn(j, what):
                ve.wait_ge(hi_done, half_at(j, what) + 1)
                r = slot_of(j, what)
                v.tensor_tensor(split_parts(w_lo, r, what), raw_ffn(what), split_parts(w_hi, r, what).bitcast(F32),
                                ALU.subtract).then_inc(lo_done, 1)

            def rows_of(gr, bk):
                ve.wait_ge(ada_used, KD) if gr == 0 else ve.wait_ge(late_used, 16 * gr)
                ve.wait_ge(bias_in[gr], 64)
                v.tensor_tensor(rows[:, gr % 2, :], bank[bk][:, :], ada_bias[:], ALU.add).then_inc(rows_ready, 1)

            def columns_in(b, j0):
                return b[:, :].rearrange("p (q j r) -> p j q r", q=4, j=4)[:, j0:j0 + 2, :, 0]

            def as_rows(c):
                return cols[:, c, :].rearrange("p (j q) -> p j q", q=4)

            rows_of(0, 4)
            ve.wait_ge(mix_cols, 1)
            v.tensor_copy(as_rows(SH_MIX), columns_in(pb, 0))
            v.scalar_tensor_tensor(out=as_rows(SC_MIX), in0=columns_in(pb, 2), scalar=1.0, in1=as_rows(W_MIX), op0=ALU.add, op1=ALU.mult).then_inc(cols_ready, 1)
            ve.wait_ge(cols_ready, 1)

            def modulate(i):
                for k in (2 * i, 2 * i + 1):
                    last = v.tensor_scalar(h_f[:, k, :], bank[i][:, (k % 2) * 256:(k % 2) * 256 + 256],
                                           cols[:, SC_MIX, k:k + 1], cols[:, SH_MIX, k:k + 1], ALU.mult, ALU.add)
                last.then_inc(hf_ready, 1)

            def h_rest(i):
                ve.wait_ge(hhi_ready, i + 1)
                v.tensor_tensor(h_lo[:, 2 * i:2 * i + 2, :], h_f[:, 2 * i:2 * i + 2, :], h_hi[:, 2 * i:2 * i + 2, :].bitcast(F32),
                                ALU.subtract).then_inc(h_ready, 1)

            lo(0)
            h_rest(0)
            modulate(1)
            lo(1)
            h_rest(1)
            modulate(3)
            h_rest(2)
            h_rest(3)
            for n in range(2, 7):
                lo(n)

            def t_bank(*use):
                ve.wait_ge(t_filled, T_AT[use] + 1)
                return bank[4 + T_AT[use] % 2]

            def spread_blocks(tt, kv):
                b = t_bank("c", tt, kv)
                for a in range(2):
                    first = (0, 1)[a] if tt == 0 else 0
                    n = (8, 7)[a] if tt == 0 else (7, 8)[a]
                    at_n = 8 * tt + first - a
                    src = b[64 * a:64 * a + 64, :].rearrange("p (g n l) -> p g l n", g=G, l=STRIDE)
                    dst = blocks[64 * a:64 * a + 64, kv].rearrange("p l (g n) -> p g l n", g=G)
                    for g in range(G):
                        last = v.tensor_tensor(dst[:, g, :, at_n:at_n + n], src[:, g, :, first:first + n],
                                               spread(pos_col[64 * a:64 * a + 64, kv, :], 2, n), ALU.add)
                last.then_inc(t_drained, 1)

            def head_sums(name, tt, heads):
                k = NAT[name, tt]
                ve.wait_ge(squared, k + 1)
                link(v.tensor_reduce(sums[:, ROOT[name, tt], 0:heads], sq[:, k % 2, 0:heads * DK].rearrange("p (h d) -> p h d", d=DK), AX_X, ALU.add))
                v.tensor_scalar(sums[:, ROOT[name, tt], 0:heads], sums[:, ROOT[name, tt], 0:heads], 1.0 / DK, EPS,
                                ALU.mult, ALU.add).then_inc(var_ready, 1)

            def head_scale(name, tt, dst, bk, heads):
                ve.wait_ge(root_ready, ROOT[name, tt] + 1)
                if name[0] != "q":
                    ve.wait_ge(copied, NAT[name, tt] + 3)
                r = roots[:, ROOT[name, tt], 0:heads]
                if name[0] == "q":
                    v.tensor_tensor(dst.rearrange("p (i a d) -> p a i d", a=2, d=DK), bank[bk][:, :].rearrange("p (a i d) -> p a i d", a=2, d=DK),
                                    spread(r.rearrange("p (a i) -> p a i", a=2), 3, DK), ALU.mult).then_inc(scaled, 1)
                else:
                    v.tensor_tensor(dst.rearrange("p (h d) -> p h d", d=DK), bank[bk][:, 0:heads * DK].rearrange("p (h d) -> p h d", d=DK),
                                    spread(r, 2, DK), ALU.mult).then_inc(scaled, 1)

            for n, (tt, kv) in zip((7, 8, 9, 10), ((0, 0), (0, 1), (1, 0), (1, 1))):
                lo(n)
                spread_blocks(tt, kv)
            lo(11)
            for tt in range(TT):
                head_sums("s", tt, G)
            lo(12)
            for tt in range(TT):
                head_scale("s", tt, k_nat[:, tt, 0, :], tt, G)
            for n in range(13, 15):
                lo(n)
            b = t_bank("hid")
            hid = b[:, 0:128].rearrange("p (v n) -> p v n", v=2)[:, :, 0:G * NC]
            ve.wait_ge(gel_sq, 1)
            link(v.tensor_scalar(gel_t[:], gel_t[:], GELU_A, 1.0, ALU.mult, ALU.add))
            v.tensor_tensor(gel_t[:], gel_t[:], hid, ALU.mult).then_inc(gel_in, 1)
            lo(15)
            ve.wait_ge(gel_tanh, 1)
            link(v.tensor_scalar(gel_t[:], gel_t[:], 0.5, 0.5, ALU.mult, ALU.add))
            v.tensor_tensor(gel[:], gel_t[:], hid, ALU.mult).then_inc(t_drained, 1)
            for tt in range(TT):
                head_sums("w", tt, G)
            lo(16)
            for tt in range(TT):
                head_scale("w", tt, k_nat[:, tt, 1, :], 2 + tt, G)
            b = t_bank("gates")
            v.tensor_scalar(gates[:], b[:, 0:TT * 3 * H].rearrange("p (t n) -> p t n", t=TT), 0.5, 0.5, ALU.mult, ALU.add).then_inc(t_drained, 1)
            for tt in range(TT):
                b = t_bank("k", tt)
                for br in range(2):
                    last = v.tensor_scalar(kT[:, :, br, tt * P:(tt + 1) * P], b[:, br * 256:br * 256 + 256].rearrange("p (r n) -> p r n", r=NP),
                                           qk_col[:, 2 + br:3 + br], None, ALU.mult)
                last.then_inc(t_drained, 1)
                lo(17 + tt)
            lo(19)
            rows_of(1, 7)
            b = t_bank("cw2")
            ve.wait_ge(kc_sum, 1)
            for a in range(2):
                v.tensor_scalar(vc[:, :, a, :], b[0:2 * NC, DK:DK + NP * DK].rearrange("p (r d) -> p r d", r=NP),
                                own_rows[:, a:a + 1], None, ALU.mult)
            v.tensor_scalar(sums[0:G * NC, ROOT["kc"], 0:1], sums[0:G * NC, ROOT["kc"], 1:2], 1.0 / DK, EPS,
                            ALU.mult, ALU.add).then_inc(var_ready, 1)
            for tt in range(TT):
                head_sums("q0", tt, 2 * HG)
            lo(20)
            ve.wait_ge(root_ready, ROOT["kc"] + 1)
            for a in range(2):
                last = v.tensor_scalar(kc_nat[:, a, :], b[0:G * NC, 0:DK], roots[0:G * NC, ROOT["kc"], 0:1], None, ALU.mult)
            last.then_inc(t_drained, 1)

            def queries():
                for tt in range(TT):
                    b = t_bank("q", 0, tt)
                    v.tensor_scalar(qT[:, 0, tt], b[:, :].rearrange("p (i n) -> p i n", i=HG), qk_col[:, 0:1], None, ALU.mult).then_inc(t_drained, 1)

            for tt in range(TT):
                head_scale("q0", tt, q_nat[:, tt, :], tt, 2 * HG)
            queries()
            lo(21)
            ve.wait_ge(bias_ready, 1)

            def c_scores(pr):
                cp = cprob[:, pr].rearrange("p t a n -> p (t a) n")
                b = t_bank("cs", pr)
                v.tensor_tensor(cprob[:, pr], b[:, 0:2 * TT * HG * NC].rearrange("p (t a n) -> p t a n", a=2, n=NC),
                                cbias[:, pr].rearrange("p a t n -> p t a n"), ALU.add).then_inc(t_drained, 1)
                ve.wait_ge(t_drained, T_AT["cs", pr] + 1)
                link(v.tensor_reduce(cstat[:, 0, :], cp, AX_X, ALU.min))
                v.tensor_tensor(cp, cp, spread(cstat[:, 0, :], 2, NC), ALU.subtract).then_inc(cs_ready, 1)

            def c_weights(pr):
                cp = cprob[:, pr].rearrange("p t a n -> p (t a) n")
                ve.wait_ge(ce_ready, pr + 1)
                link(v.tensor_tensor(cprob[:, pr], cprob[:, pr], spread(cmask[:], 2, 2), ALU.mult))
                link(v.tensor_reduce(cstat[:, 1, :], cp, AX_X, ALU.add))
                link(v.tensor_scalar(cstat[:, 1, :], cstat[:, 1, :], 1e-30, None, ALU.max))
                link(v.reciprocal(cstat[:, 2, :], cstat[:, 1, :]))
                for a in range(2):
                    h0 = (2 * pr + a) * HG
                    inv, wt = (cstat[:, k, :].rearrange("p (t i a) -> p a t i", t=TT, a=2)[:, a] for k in (2, 3))
                    last = v.tensor_tensor(wt, inv, gates[:, :, h0:h0 + HG], ALU.mult)
                link(last)
                v.tensor_tensor(cp, cp, spread(cstat[:, 3, :], 2, NC), ALU.mult).then_inc(cp_ready, 1)

            def maxima(m):
                pr, tt, i = STEPS[m]
                n = P * (tt + 1)
                ve.wait_ge(s_ready, m + 1)
                if m >= 4:
                    ve.wait_ge(t_filled, T_AT["p", m - 4, STEPS[m - 4][1]] + 1)
                for a in range(2):
                    h = (2 * pr + a) * HG + i
                    for br in range(2):
                        v.tensor_tensor_reduce(prob[:, m % 4, 2 * a + br, 0:n], bank[2 * (m % 2) + a][:, br * n:(br + 1) * n],
                                               bias[:, h, 2 * P - n:2 * P], 1.0, HUGE, ALU.add, ALU.min,
                                               negmax[:, m % 4, 2 * a + br:2 * a + br + 1]).then_inc(max_ready, 1)

            def weights(m):
                pr, tt, i = STEPS[m]
                ve.wait_ge(exp_ready, 4 * m + 4)
                link(v.reciprocal(recip[:, m % 4, :], den[:, m % 4, :]))
                gt = gates[:, tt, H:3 * H].rearrange("p (b r a i) -> p r i a b", b=2, r=NP, a=2)[:, pr, i]
                v.tensor_tensor(weight[:, m % 4, :].rearrange("p (a b) -> p a b", a=2), recip[:, m % 4, :].rearrange("p (a b) -> p a b", a=2),
                                gt, ALU.mult).then_inc(weight_ready, 1)

            def take_p(m):
                pr, tt, i = STEPS[m]
                if pr > 0 and i == 0:
                    ve.wait_ge(pv_done, tt + 1)
                if tt == 0:
                    b = t_bank("p", m, 0)
                    v.tensor_copy(pt[0][:, :, :, 0, i * P:(i + 1) * P], b[:, :].rearrange("p (a b n) -> p a b n", a=2, b=2)).then_inc(t_drained, 1)
                else:
                    for a in range(2):
                        b = t_bank("p", m, a)
                        v.tensor_copy(pt[1][:, a, :, :, i * P:(i + 1) * P], b[:, :].rearrange("p (b k n) -> p b k n", b=2, k=2)).then_inc(t_drained, 1)

            def o_rest(n):
                pr, tt = n // TT, n % TT
                ve.wait_ge(ohi_ready, n + 1)
                v.tensor_tensor(o_lo[:, tt, HG * pr:HG * pr + HG, :], bank[6][:, :].rearrange("p (i n) -> p i n", i=HG),
                                o_hi[:, tt, HG * pr:HG * pr + HG, :].bitcast(F32), ALU.subtract).then_inc(o_ready, 1)

            for m in range(NS + LAG):
                if m < NS:
                    maxima(m)
                if m == 0:
                    b = t_bank("kc")
                    for a in range(2):
                        hp = slice(64 * a, 64 * a + 64)
                        last = v.tensor_scalar(kcT[hp, :, a, :], b[hp, 0:G * NC].rearrange("p (r a n) -> p r a n", r=NP, a=2)[:, :, a, :],
                                               qk_col[hp, 1:2], None, ALU.mult)
                    last.then_inc(t_drained, 1)
                if m >= LAG:
                    pr, tt, i = STEPS[m - LAG]
                    take_p(m - LAG)
                if m < NS:
                    weights(m)
                if m == Q1_SCALE:
                    for tt in range(TT):
                        head_scale("q1", tt, q_nat[:, tt, :], 6 + tt, 2 * HG)
                if m - LAG > HG and (m - LAG) % HG == 1:
                    o_rest((m - LAG) // HG - 1)
                if m in C_STEP:
                    c_scores(C_STEP.index(m))
                if m - 1 in C_STEP:
                    c_weights(C_STEP.index(m - 1))
                if m == Q1_SUMS:
                    for tt in range(TT):
                        head_sums("q1", tt, 2 * HG)
                if m - 1 in AHEAD:
                    lo(AHEAD[m - 1])
                if m == LATE_AT + 8:
                    rows_of(2, 7)
            for nb in range(NB):
                b = t_bank("gm", nb)
                v.tensor_copy(gm_b[:, nb * 512:nb * 512 + 512], b[:, :]).then_inc(t_drained, 1)
            v.tensor_copy(as_rows(SH_FFN), columns_in(t_bank("shf"), 2)).then_inc(t_drained, 1)
            v.scalar_tensor_tensor(out=as_rows(SC_FFN), in0=columns_in(t_bank("scf"), 0), scalar=1.0, in1=as_rows(W_FFN),
                                   op0=ALU.add, op1=ALU.mult).then_inc(t_drained, 1)
            o_rest(NP * TT - 1)
            for n in (28, 29):
                lo(n)
            for what in FIRST_BLOCK[0:2]:
                lo_ffn(0, what)

            def add_y(tt):
                ve.wait_ge(y_done, 1) if tt == 0 else ve.wait_ge(used, FFN0)
                for nb in range(NB):
                    link(v.tensor_tensor(mixed[:, nb, :], bank[tt * NB + nb][:, :], gm_b[:, nb * 512:nb * 512 + 512], ALU.mult))
                    v.tensor_tensor(x_sb[:, tt, nb * 512:nb * 512 + 512], x_sb[:, tt, nb * 512:nb * 512 + 512], mixed[:, nb, :],
                                    ALU.add).then_inc(x2_ready, 1)

            def norm_x(tt):
                k = ROOT["x2", tt]
                ve.wait_ge(x2_squared, NB * (tt + 1))
                link(v.tensor_tensor(sums[:, k, 0:1], sums[:, k, 4:5], sums[:, k, 5:6], ALU.add))
                mean_eps(("x2", tt), 1, D)
                if tt == 0:
                    ve.wait_ge(root_ready, k + 1)
                    v.tensor_scalar(xn[:, tt, 0:512], x_sb[:, tt, 0:512], roots[:, k, 0:1], None, ALU.mult).then_inc(xn2_ready, 1)

            def modulate_x(tt):
                ts = slice(tt * P, (tt + 1) * P)
                ve.wait_ge(xn2T, 2 * tt + 1)
                for k in range(4):
                    last = v.tensor_scalar(h_f[:, k, ts], bank[X_BANK[tt]][:, k * P:(k + 1) * P],
                                           cols[:, SC_FFN, k:k + 1], cols[:, SH_FFN, k:k + 1], ALU.mult, ALU.add)
                last.then_inc(h2f_ready, 1)

            def rest_x(tt):
                ts = slice(tt * P, (tt + 1) * P)
                for half in (1, 0):
                    ks = slice(4 * half, 4 * half + 4)
                    ve.wait_ge(h2hi_ready, 2 * tt + 2 - half)
                    v.tensor_tensor(h_lo[:, ks, ts], h_f[:, ks, ts], h_hi[:, ks, ts].bitcast(F32), ALU.subtract).then_inc(h2_ready, 1)

            add_y(0)
            norm_x(0)
            add_y(1)
            norm_x(1)
            modulate_x(0)
            modulate_x(1)
            rest_x(0)
            rest_x(1)
            for what in FIRST_BLOCK[2:]:
                lo_ffn(0, what)

            def dve_gate(j, f):
                ve.wait_ge(th_ready, 2 * j + f + 1)
                v.scalar_tensor_tensor(out=sg[:, f, :], in0=th[:, f, :], scalar=1.0, in1=bank[4 + f][:, 0:256],
                                       op0=ALU.add, op1=ALU.mult).then_inc(dve, 1)
                ve.wait_ge(dve, n_dve[0] + 2 * j + f + 1)
                v.scalar_tensor_tensor(out=act_f[:, f, :], in0=sg[:, f, :], scalar=0.5, in1=bank[4 + f][:, 256:512],
                                       op0=ALU.mult, op1=ALU.mult).then_inc(act_ready, 1)
                ve.wait_ge(ahi_ready, 2 * j + f + 1)
                v.tensor_tensor(act_lo[:, f, :], act_f[:, f, :], act_hi[:, f, :].bitcast(F32), ALU.subtract).then_inc(a_ready, 1)

            dve_gate(0, 0)
            for what in ("G0", "U0"):
                lo_ffn(1, what)
            dve_gate(0, 1)
            for nb in range(NB):
                ve.wait_ge(t_filled, T_AT["gf", nb] + 1)
                v.tensor_copy(gf_b[:, nb * 512:nb * 512 + 512], bank[6 + nb][:, :]).then_inc(t_drained, 1)
            ve.wait_ge(t_drained, T_AT["gf", NB - 1] + 1)
            lo_ffn(1, "D1")

            def dve_block(j):
                for what in ("G1", "U1", "D0"):
                    lo_ffn(j, what)
                dve_gate(j, 0)
                for what in ("G0", "U0"):
                    lo_ffn(j + 1, what)
                dve_gate(j, 1)
                lo_ffn(j + 1, "D1")

            with ve.Fori(1, NJ - 1) as j:
                dve_block(j)
            j = NJ - 1
            for what in ("G1", "U1", "D0"):
                lo_ffn(j, what)
            dve_gate(j, 0)
            lo_ffn(NJ, "D1")
            dve_gate(j, 1)
            n_dve[0] += 2 * NJ
            for tt in range(TT):
                for nb in range(NB):
                    ve.wait_ge(y2_done, tt * NB + nb + 1)
                    link(v.tensor_tensor(mixed[:, nb, :], bank[tt * NB + nb][:, :], gf_b[:, nb * 512:nb * 512 + 512], ALU.mult))
                    v.tensor_tensor(out_sb[:, tt, nb * 512:nb * 512 + 512], x_sb[:, tt, nb * 512:nb * 512 + 512], mixed[:, nb, :],
                                    ALU.add).then_inc(out_ready, 1)

        @block.tensor
        def _(pe):
            t = nc.tensor

            def mm3(dst, l_hi, l_lo, r_hi, r_lo, start, stop):
                t.matmul(dst, l_hi, r_hi, start=start, stop=False, skip_group_check=True)
                t.matmul(dst, l_hi, r_lo, start=False, stop=False, skip_group_check=True)
                return t.matmul(dst, l_lo, r_hi, start=False, stop=stop, skip_group_check=True)

            pe.wait_ge(consts, 1)
            pe.wait_ge(norm_in, 32)
            pe.wait_ge(qk_in, 32)
            pe.wait_ge(pos_in, 32)
            for a in range(2):
                t.transpose(bank[5][:, 8 * a:8 * a + 8], norm_nat[:, a, :], ident[0:8, 0:8])
            t.transpose(bank[5][:, 16:20], qk_nat[:].rearrange("p a d -> p (a d)"), ident[0:4, 0:4])
            t.transpose(bank[5][:, 32:64], pos_nat[:].rearrange("p a d -> p (a d)"), ident[0:2 * STRIDE, 0:2 * STRIDE]).then_inc(params_t, 1)
            pe.wait_ge(c_ready, 1)
            for k in range(KD):
                if k == 4:
                    pe.wait_ge(xn_ready, TT)
                    for kk in range(KD):
                        for tt in range(TT):
                            last = t.transpose(bank[kk // 2][:, (kk % 2) * 256 + tt * P:(kk % 2) * 256 + (tt + 1) * P],
                                               xn[:, tt, kk * P:(kk + 1) * P], ident[:, :])
                        if kk % 2:
                            last.then_inc(xnT, 1)
                pe.wait_ge(ada_in[k], 16)
                for j in range(4):
                    last = t.matmul(bank[4][32 * j:32 * j + 32, :], c_rep[:, k, :], ada_e[k][:, j, :], start=(k == 0), stop=(k == KD - 1))
                last.then_inc(ada_used, 1)

            def turn_rows(b, gr):
                for q in range(4):
                    last = t.transpose(b[:, q * P:(q + 1) * P], rows[:, gr % 2, q * P:(q + 1) * P], ident[:, :])
                return last

            pe.wait_ge(rows_ready, 1)
            turn_rows(bank[5], 0).then_inc(mix_cols, 1)

            def late(q):
                g, h, k = q // 16, q // 8 % 2, q % 8
                slot = q % 16 % NLATE[g]
                pe.wait_ge(late_in[g][slot], 16 * (q % 16 // NLATE[g] + 1))
                for j in range(4):
                    last = t.matmul(bank[7][32 * j:32 * j + 32, 256 * h:256 * h + 256], c_rep[:, k, :], ada_l[g][slot][:, j, :],
                                    start=(k == 0), stop=(k == KD - 1))
                last.then_inc(late_used, 1)

            def project(name, bks, hh):
                n = START[name] + hh
                pe.wait_ge(lo_done, n + 1)
                if name == "c":
                    pe.wait_ge(h_ready, hh + 1)
                for kk in range(2):
                    k = 2 * hh + kk
                    w = slice(kk * 512, kk * 512 + 512)
                    for tt in range(TT):
                        last = mm3(bank[bks[tt]][:, :], h_hi[:, k, tt * P:(tt + 1) * P], h_lo[:, k, tt * P:(tt + 1) * P],
                                   w_hi[:, n % NRING, w], w_lo[:, n % NRING, w], k == 0, k == KD - 1)
                last.then_inc(used, 1)
                for q in LATE_BEHIND.get(n, ()):
                    late(q)

            def t_bank(*use):
                n = T_AT[use]
                if n >= 2:
                    pe.wait_ge(t_drained, n - 1)
                return bank[4 + n % 2]

            def turn_kv(tt, kv):
                pe.wait_ge(copied, tt + 1)
                b = t_bank("c", tt, kv)
                for g in range(G):
                    last = t.transpose(b[:, g * P:(g + 1) * P], kcv[:, tt, kv * G + g].rearrange("p a d -> p (a d)"), ident[:, :])
                last.then_inc(t_filled, 1)

            def hidden(kv):
                if kv == 0:
                    t_bank("hid")
                    pe.wait_ge(cw1_in, 64)
                    pe.wait_ge(t_drained, T_AT["c", 1, 1] + 1)
                b = bank[4 + T_AT["hid",] % 2]
                for l in range(STRIDE):
                    last = t.matmul(b[:, kv * 64:kv * 64 + G * NC], cw1[:, kv, l, :], blocks[:, kv, l, :], start=(l == 0), stop=(l == STRIDE - 1))
                if kv:
                    last.then_inc(t_filled, 1)

            def turn_k(tt):
                pe.wait_ge(scaled, 3 + tt)
                b = t_bank("k", tt)
                for br in range(2):
                    for pr in range(NP):
                        last = t.transpose(b[:, (br * NP + pr) * P:(br * NP + pr + 1) * P], k_nat[:, tt, br, pr * P:(pr + 1) * P], ident[:, :])
                last.then_inc(t_filled, 1)

            for hh in range(4):
                project("c", (4, 6), hh)
            for hh in range(4):
                project("s", (0, 1), hh)
                turn_kv(hh // 2, hh % 2)
            for hh in range(4):
                project("w", (2, 3), hh)
                if hh in (1, 2):
                    hidden(hh - 1)
            pe.wait_ge(copied, 2)
            for hh in range(2):
                n = START["gates"] + hh
                pe.wait_ge(lo_done, n + 1)
                for kk in range(4):
                    k = 4 * hh + kk
                    w = slice(kk * 3 * H, (kk + 1) * 3 * H)
                    last = mm3(bank[6][0:3 * H, 0:SEQ], w_hi[:, n % NRING, w], w_lo[:, n % NRING, w], h_hi[:, k, :], h_lo[:, k, :],
                               k == 0, k == KD - 1)
                last.then_inc(used, 1)
            pe.wait_ge(copied, 4)
            pe.wait_ge(scaled, 2)
            for hh in range(4):
                project("q0", (0, 1), hh)
                if hh == 0:
                    pe.wait_ge(gates_done, 1)
                    b = t_bank("gates")
                    for tt in range(TT):
                        last = t.transpose(b[:, tt * 3 * H:(tt + 1) * 3 * H], gates_t[:, tt * P:(tt + 1) * P], ident[0:3 * H, 0:3 * H])
                    last.then_inc(t_filled, 1)
                if hh in (1, 2):
                    turn_k(hh - 1)
                if hh == 2:
                    pe.wait_ge(t_drained, T_AT["hid",] + 1)
                    pe.wait_ge(cw2_in, 16)
                    b = t_bank("cw2")
                    t.matmul(b[0:G * NC, 0:DK], gel[:, 0, :], cw2[:, 0, :], start=True, stop=True)
                    for pr in range(NP):
                        last = t.matmul(b[0:2 * NC, DK + pr * DK:DK + (pr + 1) * DK], gel[:, 1, 2 * pr * NC:2 * (pr + 1) * NC], cw2[:, 1, :],
                                        start=True, stop=True)
                    last.then_inc(t_filled, 1)
            def queries(pr):
                for tt in range(TT):
                    b = t_bank("q", pr, tt) if pr == 0 else bank[6 + tt]
                    pe.wait_ge(scaled, 5 + 2 * pr + tt)
                    for i in range(HG):
                        last = t.transpose(b[:, i * P:(i + 1) * P], q_nat[:, tt, i * P:(i + 1) * P], ident[:, :])
                    last.then_inc(q_turned if pr else t_filled, 1)

            def c_scores(pr):
                b = t_bank("cs", pr)
                if pr == 0:
                    pe.wait_ge(t_drained, T_AT["kc",] + 1)
                for tt in range(TT):
                    for i in range(HG):
                        o = (tt * HG + i) * 2 * NC
                        last = t.matmul(b[:, o:o + 2 * NC], qT[:, pr, tt, i, :], kcT[:, pr, :, :].rearrange("p a n -> p (a n)"), start=True, stop=True)
                last.then_inc(t_filled, 1)

            def scores(m):
                pr, tt, i = STEPS[m]
                n = P * (tt + 1)
                if m >= 2:
                    pe.wait_ge(max_ready, 4 * (m - 1))
                for a in range(2):
                    last = t.matmul(bank[2 * (m % 2) + a][:, 0:2 * n].rearrange("p (b n) -> p b n", b=2), qT[64 * a:64 * a + 64, pr, tt, i, :],
                                    kT[64 * a:64 * a + 64, pr, :, 0:n], start=True, stop=True)
                last.then_inc(s_ready, 1)

            def turn(m):
                pr, tt, i = STEPS[m]
                pe.wait_ge(p_ready, m + 1)
                for bk in range(tt + 1):
                    b = t_bank("p", m, bk)
                    for q in range(4):
                        ab, kt = (q, 0) if tt == 0 else (2 * bk + q // 2, q % 2)
                        last = t.transpose(b[:, q * P:(q + 1) * P], prob[:, m % 4, ab, kt * P:(kt + 1) * P], ident[:, :])
                    last.then_inc(t_filled, 1)

            def turn_c(pr, tt):
                pe.wait_ge(cp_ready, pr + 1)
                n = pr * TT + tt
                if n == 0:
                    pe.wait_ge(q_taken, 1)
                else:
                    pe.wait_ge(o_ready, n)
                for i in range(HG):
                    last = t.transpose(bank[6][0:2 * NC, i * P:(i + 1) * P], cprob[:, pr, tt * HG + i, :, :].rearrange("p a n -> p (a n)"), ident[:, :])
                last.then_inc(pc_turned, 1)

            def values(pr, tt):
                n = pr * TT + tt
                pe.wait_ge(pc_taken, n + 1)
                pe.wait_ge(t_drained, T_AT["p", (n + 1) * HG - 1, tt] + 1)
                for br in range(2):
                    for kt in range(tt + 1):
                        for a in range(2):
                            gc = (2 * pr + a) * DK
                            t.matmul(bank[6][64 * a:64 * a + 64, :], v_nat[:, kt, br, gc:gc + DK], pt[tt][:, a, br, kt, :],
                                     start=(br == 0 and kt == 0), stop=False, skip_group_check=True)
                t.matmul(bank[6][:, :], vc[:, pr].rearrange("k a d -> k (a d)"), pcT[:, :], start=False, stop=True,
                         skip_group_check=True).then_inc(pv_done, 1)

            def attention_out(ck, tiles):
                n = START["out"] + ck
                pe.wait_ge(lo_done, n + 1)
                pe.wait_ge(o_ready, TT * (ck // HG + 1))
                for tt in tiles:
                    for nb in range(NB):
                        w = slice(nb * 512, nb * 512 + 512)
                        last = mm3(bank[tt * NB + nb][:, :], o_hi[:, tt, ck, :], o_lo[:, tt, ck, :], w_hi[:, n % NRING, w], w_lo[:, n % NRING, w],
                                   ck == 0, ck == KD - 1)
                if 1 in tiles:
                    last.then_inc(used, 1)
                elif ck == KD - 1:
                    last.then_inc(y_done, 1)

            pe.wait_ge(rows_ready, 2)
            for hh in range(Q1_BEFORE):
                project("q1", (6, 7), hh)

            def gates_wide(name):
                for nb in range(NB):
                    gr, j = {"gm": (1, nb), "gf": (2, 2 + nb)}[name]
                    b = t_bank(name, nb) if name == "gm" else bank[6 + nb]
                    t.matmul(b[:, :], ones[32 * j:32 * j + 1, :], rows[32 * j:32 * j + 1, gr % 2, :], start=True, stop=True).then_inc(t_filled, 1)

            queries(0)
            for m in range(NS + LAG):
                if m == 0:
                    pe.wait_ge(t_drained, T_AT["q", 0, 1] + 1)
                if m == NS // 2:
                    pe.wait_ge(q_taken, TT)
                if m == 0:
                    pe.wait_ge(scaled, 6)
                    pe.wait_ge(copied, 6)
                if m < NS:
                    scores(m)
                if m == NS:
                    pe.wait_ge(max_ready, 4 * NS)
                if m >= NS:
                    attention_out(m - NS, range(TT))
                if m < 4 - Q1_BEFORE:
                    project("q1", (6, 7), Q1_BEFORE + m)
                if m == 0:
                    pe.wait_ge(t_drained, T_AT["cw2",] + 1)
                    b = t_bank("kc")
                    t.transpose(b[:, 0:G * NC], kc_nat[:].rearrange("p a d -> p (a d)"), ident[0:G * NC, 0:G * NC]).then_inc(t_filled, 1)
                if m == Q1_STEP:
                    queries(1)
                if m > LAG and (m - LAG) % HG == 0:
                    values(*STEPS[m - LAG - 1][0:2])
                if m == LATE_AT:
                    pe.wait_ge(q_taken, TT)
                if m in LATE_STEP:
                    late(LATE_STEP[m][0])
                if m >= LAG:
                    pr, tt, i = STEPS[m - LAG]
                    turn(m - LAG)
                if m in LATE_STEP:
                    late(LATE_STEP[m][1])
                if m >= LAG and i == HG - 1:
                    turn_c(pr, tt)
                if m in C_STEP:
                    c_scores(C_STEP.index(m))
            gates_wide("gm")
            values(NP - 1, TT - 1)
            turn_rows(t_bank("shf"), 1).then_inc(t_filled, 1)
            pe.wait_ge(rows_ready, 3)
            turn_rows(t_bank("scf"), 0).then_inc(t_filled, 1)
            for ck in range(LAG, HG):
                attention_out(ck, range(TT))

            def turn_x(tt):
                for half in range(2):
                    pe.wait_ge(xn2_act if half else xn2_ready, tt + 1)
                    b = bank[X_BANK[tt] + half]
                    for k in range(4):
                        last = t.transpose(b[:, k * P:(k + 1) * P], xn[:, tt, (4 * half + k) * P:(4 * half + k + 1) * P], ident[:, :])
                    last.then_inc(xn2T, 1)

            pe.wait_ge(t_drained, T_AT["scf",] + 1)
            for tt in range(TT):
                for ck in range(HG, KD):
                    attention_out(ck, [tt])
            turn_x(0)
            gates_wide("gf")
            turn_x(1)

            def gate_up(j, what):
                f = int(what[1])
                r = slot_of(j, what)
                pe.wait_ge(lo_done, half_at(j, what) + 1)
                col = 0 if what[0] == "G" else 256
                w = [tensor[:, r, :].rearrange("p (k n) -> p k n", n=P) for tensor in (w_hi, w_lo)]
                for k in range(KD):
                    last = mm3(bank[4 + f][:, col:col + SEQ], w[0][:, k, :], w[1][:, k, :], h_hi[:, k, :], h_lo[:, k, :], k == 0, k == KD - 1)
                last.then_inc(used, 1)

            def down(j, what, first=False, final=False):
                f = int(what[1])
                r = slot_of(j, what)
                pe.wait_ge(lo_done, half_at(j, what) + 1)
                pe.wait_ge(a_ready, 2 * owner(j, what) + f + 1)
                for tt in range(TT):
                    for nb in range(NB):
                        w = slice(nb * 512, nb * 512 + 512)
                        last = mm3(bank[tt * NB + nb][:, :], act_hi[:, f, tt * P:(tt + 1) * P], act_lo[:, f, tt * P:(tt + 1) * P],
                                   w_hi[:, r, w], w_lo[:, r, w], first, final)
                        if final:
                            last.then_inc(y2_done, 1)
                if not final:
                    last.then_inc(used, 1)

            def up_block(j, first=False):
                for what in (FIRST_BLOCK if first else BLOCK):
                    if what[0] == "D":
                        down(j, what, first=first)
                    else:
                        if what[0] == "G":
                            if not first:
                                pe.wait_ge(act_ready, 2 * j + int(what[1]) - 1)
                        gate_up(j, what)

            pe.wait_ge(h2_ready, 4)
            up_block(0, first=True)
            with pe.Fori(1, NJ) as j:
                up_block(j)
            down(NJ, "D1", final=True)


_INS = ["x", "c", "ada_w", "ada_b", "norm_mix_w", "norm_ffn_w", "ffn_w_gate", "ffn_w_up", "ffn_w_down",
        "nsa_w_in", "nsa_cmp_pos", "nsa_cmp_w1", "nsa_cmp_w2", "nsa_qk_norm", "nsa_w_out"]


def kernel(**inputs):
    import numpy as _np
    import concourse.bacc as _bacc
    from concourse import mybir as _mybir
    from concourse.bass_utils import run_bass_kernel_spmd as _run

    nc = _bacc.Bacc("TRN2", target_bir_lowering=False, num_devices=1)
    arrays, args = {}, []
    for name in _INS:
        a = _np.ascontiguousarray(inputs[name])
        arrays[f"in_{name}"] = a
        args.append(nc.dram_tensor(f"in_{name}", a.shape, _mybir.dt.from_np(a.dtype), kind="ExternalInput").ap())
    args.append(nc.dram_tensor("out_0", inputs["x"].shape, _mybir.dt.float32, kind="ExternalOutput").ap())
    trunk_kernel(nc, *args)
    r = _run(nc, [arrays], core_ids=[0])
    return r.results[0]["out_0"]
```
